# Optimizing a Trainium2 kernel written in Bass

```python
import jax, jax.numpy as jnp
from jax import lax
import numpy as np

D_MODEL = 1024
BATCH = 1
SEQ = 256
DEPTH = 1

RWKV_HEADS = 8
RWKV_HEAD_DIM = 64
RWKV_DIM = RWKV_HEADS * RWKV_HEAD_DIM
DECAY_LORA = 64
AAA_LORA = 64
GATE_LORA = 128
RWKV_PROJ = 3 * RWKV_DIM + DECAY_LORA + AAA_LORA + GATE_LORA
LNX_EPS = 64e-5

SWA_Q_HEADS = 8
SWA_KV_HEADS = 2
SWA_GROUP = SWA_Q_HEADS // SWA_KV_HEADS
SWA_HEAD_DIM = 64
SWA_DIM = SWA_Q_HEADS * SWA_HEAD_DIM
SWA_KV_DIM = SWA_KV_HEADS * SWA_HEAD_DIM
SWA_PROJ = SWA_DIM + 2 * SWA_KV_DIM
WINDOW = 128
Q_BLOCK = 128
ALIBI_MAX = 8.0

MEM_LEN = 256
MEM_HEADS = 4
MEM_HEAD_DIM = 128
MEM_DIM = MEM_HEADS * MEM_HEAD_DIM

N_BRANCH = 3
BRANCH_DIM = 512
IN_PROJ = RWKV_PROJ + SWA_PROJ + MEM_DIM

N_EXPERTS = 32
TOP_K = 4
D_FF = 1024
SWIGLU_ALPHA = 1.702
SWIGLU_LIMIT = 7.0
EXPERT_BLOCK = 128

NORM_EPS = 1e-5

kernel_name = 'hybrid_rwkv7_swa_mem_moe_block'

def rms_norm(x, w):
    xf = x.astype(jnp.float32)
    y = xf * lax.rsqrt(jnp.mean(xf * xf, axis=-1, keepdims=True) + NORM_EPS)
    return (y * w).astype(x.dtype)

def token_shift_lerp(p, mu):
    prev = jnp.pad(p, ((0, 0), (1, 0), (0, 0)))[:, :-1]
    return p + (prev - p) * mu

def rwkv7_recurrence(r, decay, k, v, a, b):
    Bsz, T, H, N = r.shape

    def step(S, inp):
        r_t, w_t, k_t, v_t, a_t, b_t = inp
        Sa = jnp.einsum('bhvk,bhk->bhv', S, a_t)
        S = (S * w_t[:, :, None, :] + Sa[..., None] * b_t[:, :, None, :]
             + v_t[..., None] * k_t[:, :, None, :])
        return S, jnp.einsum('bhvk,bhk->bhv', S, r_t)

    xs = tuple(jnp.swapaxes(z, 0, 1) for z in (r, decay, k, v, a, b))
    S0 = jnp.zeros((Bsz, H, N, N), jnp.float32)
    _, y = lax.scan(step, S0, xs)
    return jnp.swapaxes(y, 0, 1)

def rwkv7_branch(p, mu, w0, w2, a0, a2, g2, k_k, k_a, r_k, lnx_w, lnx_b):
    Bsz, T, _ = p.shape
    f32 = jnp.float32
    p = token_shift_lerp(p, mu)
    r, k, v, pw, pa, pg = jnp.split(
        p, [RWKV_DIM, 2 * RWKV_DIM, 3 * RWKV_DIM, 3 * RWKV_DIM + DECAY_LORA,
            3 * RWKV_DIM + DECAY_LORA + AAA_LORA], axis=-1)
    w_log = -jax.nn.softplus(-(w0 + jnp.tanh(pw) @ w2).astype(f32)) - 0.5
    decay = jnp.exp(-jnp.exp(w_log))
    a = jax.nn.sigmoid((a0 + pa @ a2).astype(f32))
    g = jax.nn.sigmoid(pg) @ g2

    def heads(z):
        return z.astype(f32).reshape(Bsz, T, RWKV_HEADS, RWKV_HEAD_DIM)

    kk = heads(k * k_k)
    kk = kk / jnp.maximum(jnp.linalg.norm(kk, axis=-1, keepdims=True), 1e-12)
    k = k.astype(f32) * (1.0 + (a - 1.0) * k_a)
    rh, kh, vh, ah = heads(r), heads(k), heads(v), heads(a)
    y = rwkv7_recurrence(rh, heads(decay), kh, vh, -kk, kk * ah)
    m = jnp.mean(y, axis=-1, keepdims=True)
    var = jnp.mean(jnp.square(y - m), axis=-1, keepdims=True)
    y = ((y - m) * lax.rsqrt(var + LNX_EPS)).reshape(Bsz, T, RWKV_DIM) * lnx_w + lnx_b
    bonus = jnp.sum(rh * kh * r_k, axis=-1, keepdims=True) * vh
    y = y + bonus.reshape(Bsz, T, RWKV_DIM)
    return (y * g).astype(p.dtype)

def alibi_slopes(n_heads):
    return 2.0 ** (-ALIBI_MAX * jnp.arange(1, n_heads + 1, dtype=jnp.float32) / n_heads)

def swa_sink_alibi_branch(p, sinks):
    Bsz, T, _ = p.shape
    nb = T // Q_BLOCK
    f32 = jnp.float32
    q, k, v = jnp.split(p, [SWA_DIM, SWA_DIM + SWA_KV_DIM], axis=-1)
    q = q.reshape(Bsz, nb, Q_BLOCK, SWA_KV_HEADS, SWA_GROUP, SWA_HEAD_DIM)

    def band(z):
        z = z.reshape(Bsz, T, SWA_KV_HEADS, SWA_HEAD_DIM)
        prev = jnp.pad(z, ((0, 0), (Q_BLOCK, 0), (0, 0), (0, 0)))[:, :T]
        shp = (Bsz, nb, Q_BLOCK, SWA_KV_HEADS, SWA_HEAD_DIM)
        return jnp.concatenate([prev.reshape(shp), z.reshape(shp)], axis=2)

    kb, vb = band(k), band(v)
    scores = jnp.einsum('bnqhgd,bnkhd->bnhgqk', q, kb).astype(f32) * (SWA_HEAD_DIM ** -0.5)
    i = jnp.arange(Q_BLOCK)[:, None]
    j = jnp.arange(2 * Q_BLOCK)[None, :]
    dist = i + Q_BLOCK - j
    s_pos = jnp.arange(nb)[:, None, None] * Q_BLOCK - Q_BLOCK + j[None]
    valid = (dist >= 0) & (dist < WINDOW) & (s_pos >= 0)
    slopes = alibi_slopes(SWA_Q_HEADS).reshape(SWA_KV_HEADS, SWA_GROUP)
    scores = scores - slopes[:, :, None, None] * dist.astype(f32)
    scores = jnp.where(valid[None, :, None, None], scores, -jnp.inf)
    sink = jnp.broadcast_to(sinks.astype(f32).reshape(SWA_KV_HEADS, SWA_GROUP, 1, 1),
                            scores.shape[:-1] + (1,))
    probs = jax.nn.softmax(jnp.concatenate([scores, sink], axis=-1), axis=-1)[..., :-1]
    out = jnp.einsum('bnhgqk,bnkhd->bnqhgd', probs.astype(p.dtype), vb)
    return out.reshape(Bsz, T, SWA_DIM)

def memory_cross_branch(q, mem_n, w_mem_kv):
    Bsz, T, _ = q.shape
    M = mem_n.shape[1]
    km, vm = jnp.split(mem_n @ w_mem_kv, 2, axis=-1)
    qh = q.reshape(Bsz, T, MEM_HEADS, MEM_HEAD_DIM)
    km = km.reshape(Bsz, M, MEM_HEADS, MEM_HEAD_DIM)
    vm = vm.reshape(Bsz, M, MEM_HEADS, MEM_HEAD_DIM)
    scores = jnp.einsum('bthd,bmhd->bhtm', qh, km).astype(jnp.float32) * (MEM_HEAD_DIM ** -0.5)
    probs = jax.nn.softmax(scores, axis=-1).astype(q.dtype)
    return jnp.einsum('bhtm,bmhd->bthd', probs, vm).reshape(Bsz, T, MEM_DIM)

def hybrid_mixer(xn, mem_n, w_in, b_swa, rwkv_mu, rwkv_w0, rwkv_w2, rwkv_a0, rwkv_a2,
                 rwkv_g2, rwkv_kk, rwkv_ka, rwkv_rk, rwkv_lnx_w, rwkv_lnx_b, swa_sinks,
                 w_mem_kv, w_gate, w_branch, w_out):
    p = xn @ w_in
    p_rwkv, p_swa, p_mem = jnp.split(p, [RWKV_PROJ, RWKV_PROJ + SWA_PROJ], axis=-1)
    y_rwkv = rwkv7_branch(p_rwkv, rwkv_mu, rwkv_w0, rwkv_w2, rwkv_a0, rwkv_a2, rwkv_g2,
                          rwkv_kk, rwkv_ka, rwkv_rk, rwkv_lnx_w, rwkv_lnx_b)
    y_swa = swa_sink_alibi_branch(p_swa + b_swa, swa_sinks)
    y_mem = memory_cross_branch(p_mem, mem_n, w_mem_kv)
    branches = (y_rwkv, y_swa, y_mem)
    merged = jax.nn.sigmoid(xn @ w_gate[0]) * (branches[0] @ w_branch[0])
    for bi in range(1, N_BRANCH):
        merged = merged + jax.nn.sigmoid(xn @ w_gate[bi]) * (branches[bi] @ w_branch[bi])
    return merged @ w_out

def clamped_swiglu(h):
    h_glu, h_lin = h[..., ::2], h[..., 1::2]
    h_glu = jnp.minimum(h_glu, SWIGLU_LIMIT)
    h_lin = jnp.clip(h_lin, -SWIGLU_LIMIT, SWIGLU_LIMIT)
    return h_glu * jax.nn.sigmoid(SWIGLU_ALPHA * h_glu) * (h_lin + 1.0)

def sparse_moe(xn, w_router, b_router, w1, b1, w2, b2):
    Bsz, T, D = xn.shape
    xt = xn.reshape(-1, D)
    N = xt.shape[0]
    logits = (xt @ w_router + b_router).astype(jnp.float32)
    top_vals, top_idx = lax.top_k(logits, TOP_K)
    gates = jax.nn.softmax(top_vals, axis=-1)
    A = N * TOP_K
    flat_e = top_idx.reshape(-1).astype(jnp.int32)
    flat_tok = jnp.arange(A, dtype=jnp.int32) // TOP_K
    flat_g = gates.reshape(-1).astype(xt.dtype)
    order = jnp.argsort(flat_e)
    e_sorted = flat_e[order]
    counts = jnp.bincount(flat_e, length=N_EXPERTS)
    starts = jnp.cumsum(counts) - counts
    padded = ((counts + EXPERT_BLOCK - 1) // EXPERT_BLOCK) * EXPERT_BLOCK
    pad_ends = jnp.cumsum(padded)
    pad_starts = pad_ends - padded
    dest = pad_starts[e_sorted] + (jnp.arange(A, dtype=jnp.int32) - starts[e_sorted])
    n_blocks = -(-A // EXPERT_BLOCK) + N_EXPERTS
    P = n_blocks * EXPERT_BLOCK
    slot_tok = jnp.full((P,), N, jnp.int32).at[dest].set(flat_tok[order])
    slot_g = jnp.zeros((P,), xt.dtype).at[dest].set(flat_g[order])
    block_e = jnp.minimum(
        jnp.searchsorted(pad_ends, jnp.arange(n_blocks) * EXPERT_BLOCK, side='right'),
        N_EXPERTS - 1)
    x_pad = jnp.concatenate([xt, jnp.zeros((1, D), xt.dtype)], axis=0)

    def run_block(args):
        tok, e = args
        h = x_pad[tok] @ w1[e] + b1[e]
        return clamped_swiglu(h) @ w2[e] + b2[e]

    y = lax.map(run_block, (slot_tok.reshape(n_blocks, EXPERT_BLOCK), block_e))
    y = y.reshape(P, D) * slot_g[:, None]
    out = jnp.zeros((N + 1, D), y.dtype).at[slot_tok].add(y)[:N]
    return out.reshape(Bsz, T, D)

def setup_inputs(seed: int = 0) -> dict:
    key = jax.random.key(seed)
    ks = jax.random.split(key, 30)
    f32 = jnp.float32
    L, D = DEPTH, D_MODEL

    def nrm(i, shape, scale):
        return jax.random.normal(ks[i], shape, f32) * scale

    def unif(i, shape, lo, hi):
        return jax.random.uniform(ks[i], shape, f32, lo, hi)

    return {
        'x': nrm(0, (BATCH, SEQ, D), 1.0),
        'mem': nrm(1, (BATCH, MEM_LEN, D), 1.0),
        'attn_norm_w': 1.0 + nrm(2, (L, D), 0.02),
        'mem_norm_w': 1.0 + nrm(3, (L, D), 0.02),
        'w_in': nrm(4, (L, D, IN_PROJ), D ** -0.5),
        'b_swa': nrm(5, (L, SWA_PROJ), 0.01),
        'rwkv_mu': unif(6, (L, RWKV_PROJ), 0.0, 1.0),
        'rwkv_w0': unif(7, (L, RWKV_DIM), -6.0, 1.0),
        'rwkv_w2': nrm(8, (L, DECAY_LORA, RWKV_DIM), 0.1 * DECAY_LORA ** -0.5),
        'rwkv_a0': nrm(9, (L, RWKV_DIM), 0.1),
        'rwkv_a2': nrm(10, (L, AAA_LORA, RWKV_DIM), 0.1 * AAA_LORA ** -0.5),
        'rwkv_g2': nrm(11, (L, GATE_LORA, RWKV_DIM), GATE_LORA ** -0.5),
        'rwkv_kk': 0.85 + nrm(12, (L, RWKV_DIM), 0.02),
        'rwkv_ka': 1.0 + nrm(13, (L, RWKV_DIM), 0.02),
        'rwkv_rk': nrm(14, (L, RWKV_HEADS, RWKV_HEAD_DIM), 0.1),
        'rwkv_lnx_w': 1.0 + nrm(15, (L, RWKV_DIM), 0.02),
        'rwkv_lnx_b': nrm(16, (L, RWKV_DIM), 0.01),
        'swa_sinks': nrm(17, (L, SWA_Q_HEADS), 1.0),
        'w_mem_kv': nrm(18, (L, D, 2 * MEM_DIM), D ** -0.5),
        'w_gate': nrm(19, (L, N_BRANCH, D, D), D ** -0.5),
        'w_branch': nrm(20, (L, N_BRANCH, BRANCH_DIM, D), BRANCH_DIM ** -0.5),
        'w_out': nrm(21, (L, D, D), D ** -0.5),
        'ffn_norm_w': 1.0 + nrm(22, (L, D), 0.02),
        'w_router': nrm(23, (L, D, N_EXPERTS), D ** -0.5),
        'b_router': nrm(24, (L, N_EXPERTS), 0.01),
        'w_exp1': nrm(25, (L, N_EXPERTS, D, 2 * D_FF), D ** -0.5),
        'b_exp1': nrm(26, (L, N_EXPERTS, 2 * D_FF), 0.01),
        'w_exp2': nrm(27, (L, N_EXPERTS, D_FF, D), D_FF ** -0.5),
        'b_exp2': nrm(28, (L, N_EXPERTS, D), 0.01),
        'final_norm_w': 1.0 + nrm(29, (D,), 0.02),
    }

def reference(x, mem, attn_norm_w, mem_norm_w, w_in, b_swa, rwkv_mu, rwkv_w0, rwkv_w2,
              rwkv_a0, rwkv_a2, rwkv_g2, rwkv_kk, rwkv_ka, rwkv_rk, rwkv_lnx_w, rwkv_lnx_b,
              swa_sinks, w_mem_kv, w_gate, w_branch, w_out, ffn_norm_w, w_router, b_router,
              w_exp1, b_exp1, w_exp2, b_exp2, final_norm_w):
    h = x
    for l in range(DEPTH):
        xn = rms_norm(h, attn_norm_w[l])
        mem_n = rms_norm(mem, mem_norm_w[l])
        h = h + hybrid_mixer(xn, mem_n, w_in[l], b_swa[l], rwkv_mu[l], rwkv_w0[l], rwkv_w2[l],
                             rwkv_a0[l], rwkv_a2[l], rwkv_g2[l], rwkv_kk[l], rwkv_ka[l],
                             rwkv_rk[l], rwkv_lnx_w[l], rwkv_lnx_b[l], swa_sinks[l],
                             w_mem_kv[l], w_gate[l], w_branch[l], w_out[l])
        h = h + sparse_moe(rms_norm(h, ffn_norm_w[l]), w_router[l], b_router[l],
                           w_exp1[l], b_exp1[l], w_exp2[l], b_exp2[l])
    return rms_norm(h, final_norm_w)


_drawn_inputs = setup_inputs


def setup_inputs(seed=0):
    import zlib

    import numpy as np

    out = dict(_drawn_inputs(seed))
    spreads = {}
    factors = {'mem_norm_w': 8.0,
     'b_swa': 26.646,
     'rwkv_w2': 44.856,
     'rwkv_kk': 22.008,
     'rwkv_lnx_b': 31.736,
     'swa_sinks': 16.05,
     'b_exp1': 32.199,
     'b_exp2': 36.923,
     'final_norm_w': 8.603,
     'rwkv_a0': 8.0,
     'rwkv_a2': 8.0,
     'rwkv_ka': 8.0,
     'rwkv_rk': 2.711,
     'rwkv_lnx_w': 8.0,
     'ffn_norm_w': 4.325,
     'b_router': 5.357}
    for name, (base, spread) in spreads.items():
        noise = np.random.default_rng([zlib.crc32(name.encode()), seed]).standard_normal(out[name].shape)
        drawn = base * np.exp(spread * noise) if base else spread * noise
        out[name] = __import__('jax').numpy.asarray(drawn.astype(out[name].dtype))
    for name, factor in factors.items():
        out[name] = (out[name] * factor).astype(out[name].dtype)
    return out
```

```python
from contextlib import ExitStack

import numpy as np

import concourse.bass as bass
from concourse import mybir

P = 128
D = 1024
T = 256
KC = D // P
TT = T // P
F32 = mybir.dt.float32
I32 = mybir.dt.int32
ALU = mybir.AluOpType
ACT = mybir.ActivationFunctionType
AX = mybir.AxisListType

HR = 8
HP = HR // 2
CH = 64
NCH = T // CH
LEVELS = 6
EXP_HALF = float(np.exp(-0.5))
LNX_EPS = 64e-5
EPS = 1e-5
N_RWKV = 14
C_RWKV = N_RWKV * P
C_REST = 10 * P
MEM_SCALE = float(P) ** -0.5
SWA_SCALE = 64.0 ** -0.5
SLOPES = [2.0 ** (-8.0 * (h + 1) / 8) for h in range(8)]
MASKED = 1e30

NE = 32
NPAIR = NE // 2
SLOTS = 64
PASSES = T // SLOTS
ALPHA = 1.702
LIMIT = 7.0

RING = 12
HALF = RING // 2
SLOT = 2048
CPE = 12

PCOLS = {}
_at = 0
for _n, _w in (("attn", 8), ("memn", 8), ("mu", 14), ("w0", 4), ("a0", 4), ("kk", 4), ("ka", 4), ("rk", 4),
               ("lnw", 4), ("lnb", 4), ("bswa", 6)):
    PCOLS[_n] = _at
    _at += _w
NPCOL = _at

CONST = {}
_at = 0
for _n, _w in (("ident", P), ("heads", P), ("causal", 2 * P), ("level", LEVELS * P), ("level0t", P), ("before", P),
               ("ones", P), ("dist", 2 * P), ("iota", T), ("resets", T)):
    CONST[_n] = (_at, _w)
    _at += _w
NCONST = _at


def constants():
    c = np.zeros((P, NCONST), np.float32)

    def put(name, a):
        at, w = CONST[name]
        c[:, at:at + w] = a

    i = np.arange(P)
    p, f = i[:, None], i[None, :]
    same = (p // CH) == (f // CH)
    put("ident", p == f)
    put("heads", same)
    put("causal", np.concatenate([same & (p < f), same & (p <= f)], 1))
    level = [((p >> (j + 1)) == (f >> (j + 1))) & ((p >> j) % 2 == 1) & ((f >> j) % 2 == 0) for j in range(LEVELS)]
    put("level", np.concatenate(level, 1))
    put("level0t", level[0].T)
    put("before", p < f)
    put("ones", 1.0)
    j = np.arange(2 * P)[None, :]
    dist = p + P - j
    put("dist", np.where((dist >= 0) & (dist < P), dist, MASKED))
    put("iota", np.arange(1, T + 1)[None, :])
    put("resets", (np.arange(T)[None, :] % CH != 0))
    return c


def mixer_chunks():
    order = [("in_rwkv", c) for c in range(KC)] + [("in_rest", c) for c in range(KC)]
    order += [("mem_kv", c) for c in range(KC // 2)]
    n_narrow = len(order)
    for b in range(3):
        order += [("gate", (b, c)) for c in range(KC // 2)] + [("branch", (b, c)) for c in range(2)]
    order += [("out", c) for c in range(KC // 2)]
    wide = len(order) - n_narrow
    slots = [n % HALF for n in range(n_narrow)] + [(n - wide) % RING for n in range(wide)]
    return order, slots


def build(nc, x, mem, attn_norm_w, mem_norm_w, w_in, b_swa, rwkv_mu, rwkv_w0, rwkv_w2, rwkv_a0, rwkv_a2, rwkv_g2,
          rwkv_kk, rwkv_ka, rwkv_rk, rwkv_lnx_w, rwkv_lnx_b, swa_sinks, w_mem_kv, w_gate, w_branch, w_out,
          ffn_norm_w, w_router, b_router, w_exp1, b_exp1, w_exp2, b_exp2, final_norm_w, consts, out):
    order, slots = mixer_chunks()
    NMIX = len(order)
    index = {key: n for n, key in enumerate(order)}
    uses = [slots.count(s) for s in range(RING)]
    past = [slots[:n].count(s) for n, s in enumerate(slots)]
    previous = [max([m for m in range(n) if slots[m] == s], default=None) for n, s in enumerate(slots)]
    last_in = [max(m for m in range(NMIX) if slots[m] == s) for s in range(RING)]
    assert last_in == list(range(NMIX - RING, NMIX))

    with ExitStack() as ctx:
        def sb(name, shape, dt=F32):
            return ctx.enter_context(nc.sbuf_tensor(name, shape, dt))

        def sem(name):
            return ctx.enter_context(nc.semaphore(name))

        ring = sb("ring", [P, RING * SLOT])
        upper = sb("upper", [P, 70 * 256])
        cst = sb("cst", [P, NCONST])
        xrows = sb("xrows", [P, TT, D])
        xT = sb("xT", [P, KC, T])
        lora = sb("lora", [P, 512])
        gate2 = sb("gate2", [P, 512])
        prows = sb("prows", [NPCOL, P])
        prm = sb("prm", [P, NPCOL])
        omka = sb("omka", [P, HP])
        bq = sb("bq", [P, HP])
        epsc = sb("epsc", [P, 2])
        ss = sb("ss", [P, 8])
        sinks = sb("sinks", [P, 8])
        stat = sb("stat", [P, 6, 8])
        pend = sb("pend", [P, HP, NCH])
        brt = sb("brt", [P, NE])
        logit = sb("logit", [P, TT, NE])
        top8 = sb("top8", [P, TT, 8])
        rest = sb("rest", [P, TT, NE])
        chosen = sb("chosen", [P, TT, NE])
        gates = sb("gates", [P, TT, NE])
        rank1 = sb("rank1", [P, TT, NE])
        rtmp = sb("rtmp", [P, TT, 4])
        cnt = sb("cnt", [P, 1])
        cnti = sb("cnti", [P, 1], I32)
        ps = ctx.enter_context(nc.psum_tensor("ps", [P, 8, 512], F32))

        def kb(at, size, pattern=None, **dims):
            if at < 48:
                assert at + size <= 48
                a = ring[:, HALF * SLOT + at * 256:HALF * SLOT + (at + size) * 256]
            else:
                a = upper[:, (at - 48) * 256:(at - 48 + size) * 256]
            return a.rearrange(pattern, **dims) if pattern else a

        def const(name, at=0, width=None):
            a, w = CONST[name]
            return cst[:, a + at:a + at + (width or w)]

        def col(name, n=0):
            return prm[:, PCOLS[name] + n:PCOLS[name] + n + 1]

        ident = const("ident")
        heads = const("heads")
        ones = const("ones")
        four = "p (c t) -> p c t"

        proj = kb(0, 14, four, c=14)
        raw = ring[:, HALF * SLOT + 22 * 256:HALF * SLOT + 22 * 256 + N_RWKV * (T + 1)].rearrange(four, c=N_RWKV)
        csum = kb(14, 4, four, c=4)
        pex = kb(18, 4, four, c=4)
        pinv = kb(22, 4, four, c=4)
        pinc = kb(26, 4, four, c=4)
        rate_a = kb(30, 4, four, c=4)
        kkn = kb(34, 4, four, c=4)
        ar = kb(38, 8, "p (c k t) -> p c k t", c=4, k=2)
        bT = kb(48, 4, four, c=4)
        kT = kb(52, 4, four, c=4)
        gT = kb(56, 4, four, c=4)
        btok = kb(60, 4, "p (t f) -> p t f", t=TT)
        ktok = kb(64, 4, "p (t f) -> p t f", t=TT)
        vtok = kb(68, 4, "p (t f) -> p t f", t=TT)
        dump = kb(38, 8, "p (t f) -> p t f", t=TT)
        xscaled = kb(60, 8, "p (t f) -> p t f", t=TT)
        probs = kb(60, 8)
        gram = kb(72, 32, "p (u k t) -> p u k t", u=16, k=4)
        memT = kb(72, 8, "p (c t) -> p c t", c=KC)
        memrows = kb(80, 8, "p (t f) -> p t f", t=TT)
        probsT = kb(80, 8)
        sq_ = kb(88, 4, four, c=4)
        skd = kb(92, 2, four, c=2)
        svT = kb(94, 1)
        sv = kb(95, 1, "p (t f) -> p t f", t=TT)
        mq = kb(96, 4, four, c=4)
        kmT = kb(100, 4, four, c=4)
        vm = kb(104, 4, "p (t f) -> p t f", t=TT)
        y_swa = kb(110, 4, four, c=4)
        y_mem = kb(114, 4, four, c=4)
        inv = kb(14, 8, "p (u t) -> p u t", u=16)
        invT = kb(22, 8, "p (u t) -> p u t", u=16)
        bonus = kb(30, 4, four, c=4)
        sqr = kb(34, 4, four, c=4)
        t1s = kb(0, 8, "p (g u t) -> p g u t", g=4, u=4)
        av = kb(0, 4, "p (t f) -> p t f", t=TT)
        us = kb(4, 4, "p (t f) -> p t f", t=TT)
        rs_ = kb(12, 2)
        state = kb(48, 4, "p (b c v) -> p b c v", b=2, c=HP)
        decay_end = kb(52, 4, "p (b c v) -> p b c v", b=2, c=HP)
        yT = kb(14, 4, four, c=4)
        yc = kb(18, 4, four, c=4)
        gsig = kb(60, 8, "p (b n) -> p b n", b=4)
        merged = kb(72, 8, "p (b n) -> p b n", b=4)
        mergedT = kb(72, 8, four, c=KC)
        ffnw = kb(80, 4)
        finw = kb(84, 4)
        b1row = kb(88, 16, "p (e f) -> p e f", e=2)
        b2rows = kb(104, 4)
        wrt = kb(108, 1, "p (c e) -> p c e", c=KC)
        hn = kb(60, 8, "p (t f) -> p t f", t=TT)
        hnT = kb(110, 8, "p (c t) -> p c t", c=KC)
        xg = kb(48, 4, "p (c s) -> p c s", c=KC)
        glu = kb(52, 2)
        lin = kb(54, 2)
        sig = kb(68, 2)
        act_ = kb(70, 2)
        actT = kb(72, 2, "p (m h s) -> p m h s", m=4, h=2)
        yrow = kb(74, 4)
        sel = kb(78, 1, "p (t e s) -> p t e s", t=TT, e=2)
        selg = kb(79, 1, "p (t e s) -> p t e s", t=TT, e=2)
        selgT = kb(108, 1, "p (t n) -> p t n", t=TT)
        gatesT = kb(109, 1)
        outrow = kb(110, 8, "p (t f) -> p t f", t=TT)

        def slot(s):
            return ring[:, s * SLOT:(s + 1) * SLOT]

        slot_full = [sem(f"slot_full{s}") for s in range(RING)]
        slots_used = sem("slots_used")
        x_loaded, mem_loaded, prm_loaded, cst_loaded = sem("x_loaded"), sem("mem_loaded"), sem("prm_loaded"), sem("cst_loaded")
        lora_loaded, sink_loaded, late_loaded = sem("lora_loaded"), sem("sink_loaded"), sem("late_loaded")
        b1_full = [sem("b1_full0"), sem("b1_full1")]
        ssum, root, scaled, scaled_m = sem("ssum"), sem("root"), sem("scaled"), sem("scaled_m")
        prm_ps, prm_sb = sem("prm_ps"), sem("prm_sb")
        xT_ps, memT_ps, xT_sb, memT_sb = sem("xT_ps"), sem("memT_ps"), sem("xT_sb"), sem("memT_sb")
        rwkv_ps, raw_sb, lora_in, shifted, lora_act = sem("rwkv_ps"), sem("raw_sb"), sem("lora_in"), sem("shifted"), sem("lora_act")
        rest_ps, rest_sb, kv_ps, kv_sb = sem("rest_ps"), sem("rest_sb"), sem("kv_ps"), sem("kv_sb")
        zw_ps, za_ps, g_ps, rate_sb, a_sb, g_sb = sem("zw_ps"), sem("za_ps"), sem("g_ps"), sem("rate_sb"), sem("a_sb"), sem("g_sb")
        kk_sq, kk_ps, kk_clamped, kk_root = sem("kk_sq"), sem("kk_ps"), sem("kk_clamped"), sem("kk_root")
        csum_sb, powers_sb, tilde_sb, rk_sb, rk_ps, bonus_sb = (sem("csum_sb"), sem("powers_sb"), sem("tilde_sb"),
                                                               sem("rk_sb"), sem("rk_ps"), sem("bonus_sb"))
        score_ps, score_sb, negmax, expd, normed, pT_ps, pT_sb, pv_ps, pv_sb = (
            sem("score_ps"), sem("score_sb"), sem("negmax"), sem("expd"), sem("normed"), sem("pT_ps"), sem("pT_sb"),
            sem("pv_ps"), sem("pv_sb"))
        svT_ps, sv_sb = sem("svT_ps"), sem("sv_sb")
        tok_ps, tok_sb = sem("tok_ps"), sem("tok_sb")
        gram_ps, gram_sb, ab_ps, inv_sb, t1_ps, t1_sb, xx_ps = (sem("gram_ps"), sem("gram_sb"), sem("ab_ps"),
                                                              sem("inv_sb"), sem("t1_ps"), sem("t1_sb"), sem("xx_ps"))
        av_ps, av_sb, zeroed, r_ps, r_sb, u_ps, u_sb, s_ps, s_sb, yh_ps = (
            sem("av_ps"), sem("av_sb"), sem("zeroed"), sem("r_ps"), sem("r_sb"), sem("u_ps"), sem("u_sb"),
            sem("s_ps"), sem("s_sb"), sem("yh_ps"))
        yh_sb, mean_ps, yc_sb, var_ps, var_root, y_rwkv_sb = (sem("yh_sb"), sem("mean_ps"), sem("yc_sb"), sem("var_ps"),
                                                              sem("var_root"), sem("y_rwkv_sb"))
        gate_ps, gate_sb, branch_ps, merged_sb, out_ps, resid = (sem("gate_ps"), sem("gate_sb"), sem("branch_ps"),
                                                                 sem("merged_sb"), sem("out_ps"), sem("resid"))
        ffn_ss, ffn_root, hn_sb, hnT_ps, hnT_sb, logit_ps = (sem("ffn_ss"), sem("ffn_root"), sem("hn_sb"), sem("hnT_ps"),
                                                             sem("hnT_sb"), sem("logit_ps"))
        top_sb, top_exp, chosen_sb, rank_ps, gates_sb, gT_ps, gT_sb, b2_ps, route_done = (
            sem("top_sb"), sem("top_exp"), sem("chosen_sb"), sem("rank_ps"), sem("gates_sb"), sem("gT_ps"), sem("gT_sb"),
            sem("b2_ps"), sem("route_done"))
        sel_sb, xg_ps, xg_sb, up_ps, up_read, glu_sb, sig_sb, prod_sb, act_sb = (
            sem("sel_sb"), sem("xg_ps"), sem("xg_sb"), sem("up_ps"), sem("up_read"), sem("glu_sb"), sem("sig_sb"),
            sem("prod_sb"), sem("act_sb"))
        actT_ps, actT_sb, down_ps, yrow_sb, selg_raw, selg_sb, selgT_ps, selgT_sb, sc_ps, acc_sb = (
            sem("actT_ps"), sem("actT_sb"), sem("down_ps"), sem("yrow_sb"), sem("selg_raw"), sem("selg_sb"),
            sem("selgT_ps"), sem("selgT_sb"), sem("sc_ps"), sem("acc_sb"))
        moe_done, fin_ss, fin_root, final_sb, stored = (sem("moe_done"), sem("fin_ss"), sem("fin_root"), sem("final_sb"),
                                                        sem("stored"))
        dve_step, act_step = sem("dve_step"), sem("act_step")

        block = ctx.enter_context(nc.Block())

        def w1_place(c, E, zero):
            if zero:
                return c, E + 1, E * CPE + c
            return (c - 4) % RING, E + (0 if c < 4 else 1), E * CPE + (c - 4)

        def w2_place(i, E, final):
            if final:
                return i + 8, E + 1, E * CPE + (i + 8)
            return i + 4, E + 2, E * CPE + (i + 16)

        def rows(w):
            return w.rearrange("(c p) f -> p c f", p=P)

        @block.sync
        def _(sp):
            sp.dma_start(xrows[:], x[0].rearrange("(t p) d -> p t d", p=P)).then_inc(x_loaded, 16)
            sp.dma_start(memrows, mem[0].rearrange("(t p) d -> p t d", p=P)).then_inc(mem_loaded, 16)
            w_in_r = rows(w_in[0])
            kv_r = rows(w_mem_kv[0])
            out_r = rows(w_out[0])
            for n, (name, c) in enumerate(order):
                s = slots[n]
                if previous[n] is not None:
                    sp.wait_ge(slots_used, previous[n] + 1)
                elif s >= HALF:
                    sp.wait_ge(y_rwkv_sb, 1)
                wide = slot(s).rearrange("p (c f) -> p c f", c=2)
                if name == "in_rwkv":
                    dst, src = slot(s)[:, 0:C_RWKV], w_in_r[:, c, 0:C_RWKV]
                elif name == "in_rest":
                    dst, src = slot(s)[:, 0:C_REST], w_in_r[:, c, C_RWKV:C_RWKV + C_REST]
                elif name == "mem_kv":
                    dst, src = wide, kv_r[:, 2 * c:2 * c + 2, :]
                elif name == "gate":
                    dst, src = wide, rows(w_gate[0, c[0]])[:, 2 * c[1]:2 * c[1] + 2, :]
                elif name == "branch":
                    dst, src = wide, rows(w_branch[0, c[0]])[:, 2 * c[1]:2 * c[1] + 2, :]
                else:
                    dst, src = wide, out_r[:, 2 * c:2 * c + 2, :]
                sp.dma_start(dst, src).then_inc(slot_full[s], 16)
                if (name, c) == ("gate", (1, 0)):
                    sp.wait_ge(y_rwkv_sb, 1)
                    sp.dma_start(ffnw, ffn_norm_w.to_broadcast([P, D])).then_inc(late_loaded, 16)
                    sp.dma_start(finw, final_norm_w.unsqueeze(0).to_broadcast([P, D])).then_inc(late_loaded, 16)
                    sp.dma_start(b2rows[0:NE, :], b_exp2[0]).then_inc(late_loaded, 16)
                    sp.dma_start(wrt, w_router[0].rearrange("(c p) e -> p c e", p=P)).then_inc(late_loaded, 16)
                    sp.dma_start(brt[:], b_router.to_broadcast([P, NE])).then_inc(late_loaded, 16)

            def load_w1(e, E, parity, zero=False):
                for c in range(KC):
                    s, _, n = w1_place(c, E, zero)
                    sp.wait_ge(slots_used, n + (NMIX - RING + 1))
                    if c == 0:
                        sp.dma_start(b1row[0:1, parity, :], b_exp1[0, bass.ds(e, 1), :]).then_inc(b1_full[parity], 16)
                    sp.dma_start(slot(s), w_exp1[0, bass.ds(e, 1), c * P:(c + 1) * P, :].rearrange("a p f -> p (a f)"))\
                      .then_inc(slot_full[s], 16)

            def load_w2(e, E, final=False):
                for i in range(4):
                    s, _, n = w2_place(i, E, final)
                    sp.wait_ge(slots_used, n + (NMIX - RING + 1))
                    sp.dma_start(slot(s).rearrange("p (c f) -> p c f", c=2),
                                 w_exp2[0, bass.ds(e, 1), 2 * i * P:(2 * i + 2) * P, :].rearrange("a (c p) f -> p (a c) f", p=P))\
                      .then_inc(slot_full[s], 16)

            def load_pass(q):
                E = q * NE
                load_w1(0, E, 0, True)
                with sp.Fori(0, NPAIR - 1) as k:
                    load_w1(k * 2 + 1, E + k * 2 + 1, 1)
                    load_w2(k * 2, E + k * 2)
                    load_w1(k * 2 + 2, E + k * 2 + 2, 0)
                    load_w2(k * 2 + 1, E + k * 2 + 1)
                load_w1(NE - 1, E + NE - 1, 1)
                load_w2(NE - 2, E + NE - 2)
                load_w2(NE - 1, E + NE - 1, True)

            load_pass(0)
            sp.wait_ge(route_done, 1)
            most = sp.value_load(cnti[0:1, 0:1], min_val=0, max_val=T)
            with sp.If(most > SLOTS):
                with sp.Fori(1, PASSES) as q:
                    load_pass(q)
            sp.wait_ge(final_sb, 1)
            sp.dma_start(out[0].rearrange("(t p) d -> p t d", p=P)[:, 0, :], outrow[:, 0, :]).then_inc(stored, 16)
            sp.wait_ge(final_sb, 2)
            sp.dma_start(out[0].rearrange("(t p) d -> p t d", p=P)[:, 1, :], outrow[:, 1, :]).then_inc(stored, 16)
            sp.wait_ge(stored, 32)

        @block.tensor
        def _(pe):
            def mm(o, l, r, start=True, stop=True):
                return pe.matmul(o, l, r, start=start, stop=stop, skip_group_check=True)

            def half(bank, n):
                return ps[:, bank + n // 2, (n % 2) * T:(n % 2) * T + T]

            def take(name, c):
                n = index[(name, c)]
                pe.wait_ge(slot_full[slots[n]], 16 * (past[n] + 1))
                return slot(slots[n])

            pe.wait_ge(cst_loaded, 16)
            pe.wait_ge(prm_loaded, 16 * 11)
            pe.transpose(ps[:, 7, 0:NPCOL], prows[:], ident[0:NPCOL, 0:NPCOL]).then_inc(prm_ps, 1)
            for t in range(TT):
                pe.wait_ge(scaled, t + 1)
                for c in range(KC):
                    last = pe.transpose(half(0, c)[:, t * P:(t + 1) * P], xscaled[:, t, c * P:(c + 1) * P], ident)
            last.then_inc(xT_ps, 1)
            pe.wait_ge(prm_sb, 1)
            for t in range(TT):
                pe.wait_ge(scaled_m, t + 1)
                for c in range(KC):
                    last = pe.transpose(half(4, c)[:, t * P:(t + 1) * P], memrows[:, t, c * P:(c + 1) * P], ident)
            last.then_inc(memT_ps, 1)

            pe.wait_ge(xT_sb, 1)
            pe.wait_ge(memT_sb, 1)
            for c in range(KC):
                w = take("in_rwkv", c)
                for f in range(N_RWKV):
                    last = mm(half(0, f), w[:, f * P:(f + 1) * P], xT[:, c, :], c == 0 and f % 2 == 0, c == KC - 1)
                last.then_inc(slots_used, 1)
            pe.wait_ge(slots_used, KC)
            pe.sem_inc(rwkv_ps, 1)
            pe.wait_ge(raw_sb, 6)
            for c in range(KC):
                w = take("in_rest", c)
                for f in range(10):
                    last = mm(half(0, f), w[:, f * P:(f + 1) * P], xT[:, c, :], c == 0 and f % 2 == 0, c == KC - 1)
                last.then_inc(slots_used, 1)
            pe.wait_ge(slots_used, 2 * KC)
            pe.sem_inc(rest_ps, 1)
            pe.wait_ge(raw_sb, 7)
            pe.wait_ge(rest_sb, 2)
            for c in range(KC // 2):
                w = take("mem_kv", c)
                for cc in range(2):
                    k = 2 * c + cc
                    for f in range(4):
                        mm(half(5, f), w[:, cc * D + f * P:cc * D + (f + 1) * P], memT[:, k, :], k == 0 and f % 2 == 0, k == KC - 1)
                    for t in range(TT):
                        last = mm(ps[:, (7 + t) % 8, :], memT[:, k, t * P:(t + 1) * P], w[:, cc * D + 512:cc * D + D],
                                  k == 0, k == KC - 1)
                last.then_inc(slots_used, 1)
            pe.wait_ge(slots_used, 2 * KC + KC // 2)
            pe.sem_inc(kv_ps, 1)
            pe.wait_ge(lora_loaded, 48)
            pe.wait_ge(lora_act, 2)
            pe.wait_ge(rest_sb, 9)
            for f in range(HP):
                last = mm(half(1, f), lora[0:64, f * P:(f + 1) * P], proj[0:64, 12, :], f % 2 == 0)
            last.then_inc(zw_ps, 1)
            pe.wait_ge(rest_sb, 11)
            for f in range(HP):
                last = mm(half(3, f), lora[64:P, f * P:(f + 1) * P], proj[64:P, 12, :], f % 2 == 0)
            last.then_inc(za_ps, 1)
            pe.wait_ge(kv_sb, 2)
            for f in range(HP):
                last = mm(half(5, f), gate2[:, f * P:(f + 1) * P], proj[:, 13, :], f % 2 == 0)
            last.then_inc(g_ps, 1)
            pe.wait_ge(kv_sb, 4)
            pe.wait_ge(kk_sq, 1)
            for b in range(2):
                last = mm(ps[:, (7 + b) % 8, :], heads, csum[:, 2 * b:2 * b + 2, :])
            last.then_inc(kk_ps, 1)

            for n in range(TT):
                pe.wait_ge(rate_sb if n == 0 else a_sb, 1)
                for h in range(4):
                    last = mm(half(1 + 2 * n, h), mq[:, h, n * P:(n + 1) * P], kmT[:, h, :], h % 2 == 0)
                last.then_inc(score_ps, 1)
            pe.wait_ge(g_sb, 1)
            for t in range(TT):
                last = pe.transpose(ps[:, 5, t * P:(t + 1) * P], svT[:, t * P:(t + 1) * P], ident)
            last.then_inc(svT_ps, 1)
            pe.wait_ge(kk_clamped, 1)
            pe.wait_ge(rk_sb, 1)
            for b in range(2):
                last = mm(ps[:, (7 + b) % 8, :], heads, kkn[:, 2 * b:2 * b + 2, :])
            last.then_inc(rk_ps, 1)
            pT3 = probsT.rearrange("p (n h m q) -> p n h m q", n=2, h=4, m=2)
            pm = probs.rearrange("p (n h m) -> p n h m", n=2, h=4)
            pe.wait_ge(sv_sb, 1)
            for n in range(TT):
                pe.wait_ge(normed, n + 1)
                if n == 1:
                    pe.wait_ge(bonus_sb, 1)
                for h in range(4):
                    for m in range(2):
                        bank = (5 + 2 * n + h // 2) % 8
                        last = pe.transpose(ps[:, bank, (h % 2) * T + m * P:(h % 2) * T + (m + 1) * P],
                                            pm[:, n, h, m * P:(m + 1) * P], ident)
                last.then_inc(pT_ps, 1)
            for n in range(TT):
                pe.wait_ge(pT_sb, 2 * n + 2)
                pe.wait_ge(expd, 2)
                for h in range(4):
                    for m in range(2):
                        last = mm(ps[:, 1 + n, h * P:(h + 1) * P], vm[:, m, h * P:(h + 1) * P], pT3[:, n, h, m, :],
                                  h == 0 and m == 0, m == 1)
                last.then_inc(pv_ps, 1)
            for h in range(8):
                b = 64 * (h % 2)
                last = mm(ps[:, 3 + h % 2, (h // 2) * P:(h // 2 + 1) * P], sq_[b:b + 64, h // 2, 0:P],
                          skd[b:b + 64, h // 4, 0:P], h < 2)
            last.then_inc(score_ps, 1)
            pe.wait_ge(normed, 3)
            pe.wait_ge(pT_sb, 4)
            for h in range(8):
                last = pe.transpose(ps[:, 5 + h // 4, (h % 4) * P:(h % 4 + 1) * P],
                                    probs[:, ((h % 2) * 4 + h // 2) * P:((h % 2) * 4 + h // 2 + 1) * P], ident)
            last.then_inc(pT_ps, 1)
            pe.wait_ge(pT_sb, 6)
            pe.wait_ge(pv_sb, 2)
            for h in range(8):
                b = 64 * (h % 2)
                last = mm(ps[b:b + 64, 1, (h // 2) * P:(h // 2 + 1) * P], sv[:, 0, (h // 4) * 64:(h // 4) * 64 + 64],
                          probsT[:, h * P:(h + 1) * P], h < 2)
            last.then_inc(pv_ps, 1)
            for h in range(8):
                b = 64 * (h % 2)
                bank = 3 + h // 4 if h % 2 == 0 else (7 + h // 4) % 8
                last = mm(ps[:, bank, (h // 2 % 2) * T:(h // 2 % 2 + 1) * T], sq_[b:b + 64, h // 2, P:T],
                          skd[b:b + 64, h // 4, :], h // 2 % 2 == 0)
            last.then_inc(score_ps, 1)
            pe.wait_ge(normed, 4)
            for h in range(8):
                for m in range(2):
                    at = ((h % 2) * 4 + h // 2) * T + m * P
                    last = pe.transpose(ps[:, 3 + h // 2, (h % 2) * T + m * P:(h % 2) * T + (m + 1) * P],
                                        probs[:, at:at + P], ident)
            last.then_inc(pT_ps, 1)
            pe.wait_ge(pT_sb, 10)
            for h in range(8):
                b = 64 * (h % 2)
                for m in range(2):
                    last = mm(ps[b:b + 64, 2, (h // 2) * P:(h // 2 + 1) * P], sv[:, m, (h // 4) * 64:(h // 4) * 64 + 64],
                              probsT[:, (2 * h + m) * P:(2 * h + m + 1) * P], h < 2 and m == 0, m == 1)
            last.then_inc(pv_ps, 1)

            pe.wait_ge(tilde_sb, 1)
            for i, src in enumerate((bT, kT, proj[:, 8:12, :])):
                for t in range(TT):
                    for c in range(HP):
                        last = pe.transpose(ps[:, (3 + 2 * i + t) % 8, c * P:(c + 1) * P], src[:, c, t * P:(t + 1) * P], ident)
                    last.then_inc(tok_ps, 1)
            pe.wait_ge(tok_sb, 6)
            pe.wait_ge(pv_sb, 4)
            for g in range(4):
                t, par = g // 2, g % 2
                b = 64 * par
                for i in range(4):
                    n = 4 * g + i
                    if n >= 6:
                        pe.wait_ge(gram_sb, n - 5)
                    ts = slice(t * P, (t + 1) * P)
                    mm(ps[:, n % 6, 0:T], bT[b:b + 64, i, ts], ar[b:b + 64, i, :, ts])
                    mm(ps[:, n % 6, T:2 * T], kT[b:b + 64, i, ts], ar[b:b + 64, i, :, ts], False).then_inc(gram_ps, 1)
                if g >= 2:
                    pe.wait_ge(inv_sb, g - 1)
                for i in range(4):
                    last = mm(ps[:, 6 + par, i * P:(i + 1) * P], ar[b:b + 64, i, 0, ts], bT[b:b + 64, i, ts], i == 0)
                last.then_inc(ab_ps, 1)
            for j in range(1, LEVELS):
                for g in range(4):
                    pe.wait_ge(inv_sb, 4 * (j - 1) + g + 1)
                    if j == 1:
                        pe.wait_ge(gram_sb, 16)
                    for i in range(4):
                        u = 4 * g + i
                        last = mm(ps[:, g, i * P:(i + 1) * P], gram[:, u, 0, :], inv[:, u, :], i == 0)
                    last.then_inc(t1_ps, 1)
                for g in range(4):
                    n = 4 * (j - 1) + g
                    pe.wait_ge(t1_sb, n + 1)
                    pe.wait_ge(inv_sb, 4 + n - 1)
                    for i in range(4):
                        u = 4 * g + i
                        mm(ps[:, 4 + 2 * (g % 2), i * P:(i + 1) * P], invT[:, u, :], t1s[:, g, i, :], i == 0)
                    for i in range(4):
                        u = 4 * g + i
                        last = mm(ps[:, 5 + 2 * (g % 2), i * P:(i + 1) * P], t1s[:, g, i, :], invT[:, u, :], i == 0)
                    last.then_inc(xx_ps, 1)
            pe.wait_ge(inv_sb, 4 * LEVELS)
            for t in range(TT):
                for h in range(HR):
                    last = mm(ps[:, 4 + 2 * t + h // 4, (h % 4) * P:(h % 4 + 1) * P],
                              gram[:, t * 8 + (h % 2) * 4 + h // 2, 2, :], vtok[:, t, (h // 2) * P:(h // 2 + 1) * P], h % 4 == 0)
                last.then_inc(av_ps, 1)
            pe.wait_ge(zeroed, 3)
            pe.wait_ge(av_sb, 4)
            for ch in range(NCH):
                t, c = ch // 2, ch % 2
                rs = slice(64 * c, 64 * c + 64)
                toks = slice(ch * CH, (ch + 1) * CH)
                if ch:
                    pe.wait_ge(s_sb, ch)
                for hp in range(HP):
                    last = mm(ps[rs, 0, hp * P:(hp + 1) * P], ar[:, hp, 0, toks], state[:, ch % 2, hp, :], hp == 0)
                last.then_inc(r_ps, 1)
                for hp in range(HP):
                    mm(ps[:, 3, hp * P:(hp + 1) * P], ktok[rs, t, hp * P:(hp + 1) * P], vtok[rs, t, hp * P:(hp + 1) * P], hp == 0)
                for hp in range(HP):
                    mm(ps[:, 4 + t, hp * P + c * CH:hp * P + (c + 1) * CH], state[:, ch % 2, hp, :], ar[:, hp, 1, toks],
                       c == 0 and hp == 0)
                pe.wait_ge(r_sb, ch + 1)
                for h in range(HR):
                    last = mm(ps[rs, 1 + h // 4, (h % 4) * P:(h % 4 + 1) * P], invT[:, t * 8 + (h % 2) * 4 + h // 2, rs],
                              rs_[:, (h // 2) * P:(h // 2 + 1) * P], h % 4 == 0)
                last.then_inc(u_ps, 1)
                pe.wait_ge(u_sb, ch + 1)
                for hp in range(HP):
                    last = mm(ps[:, 3, hp * P:(hp + 1) * P], btok[rs, t, hp * P:(hp + 1) * P], us[rs, t, hp * P:(hp + 1) * P], False)
                last.then_inc(s_ps, 1)
                if c == 1:
                    for h in range(HR):
                        u = t * 8 + (h % 2) * 4 + h // 2
                        o = ps[64 * (h % 2):64 * (h % 2) + 64, 4 + t, (h // 2) * P:(h // 2 + 1) * P]
                        mm(o, vtok[:, t, h * 64:(h + 1) * 64], gram[:, u, 3, :], False)
                        last = mm(o, us[:, t, h * 64:(h + 1) * 64], gram[:, u, 1, :], False)
                    last.then_inc(yh_ps, 1)
            pe.wait_ge(yh_sb, 1)
            for b in range(2):
                last = mm(ps[:, 6 + b, :], heads, yT[:, 2 * b:2 * b + 2, :])
            last.then_inc(mean_ps, 1)
            pe.wait_ge(yc_sb, 2)
            for b in range(2):
                last = mm(ps[:, 6 + b, :], heads, sqr[:, 2 * b:2 * b + 2, :])
            last.then_inc(var_ps, 1)

            pe.wait_ge(y_rwkv_sb, 1)
            for i, y in enumerate((gT, y_swa, y_mem)):
                if i:
                    pe.wait_ge(gate_sb, i)
                for c in range(KC // 2):
                    w = take("gate", (i, c))
                    for cc in range(2):
                        k = 2 * c + cc
                        for f in range(KC):
                            last = mm(half(0, f), w[:, cc * D + f * P:cc * D + (f + 1) * P], xT[:, k, :], k == 0 and f % 2 == 0, k == KC - 1)
                    last.then_inc(slots_used, 1)
                pe.wait_ge(slots_used, index[("gate", (i, KC // 2 - 1))] + 1)
                pe.sem_inc(gate_ps, 1)
                if i:
                    pe.wait_ge(merged_sb, i)
                for c in range(2):
                    w = take("branch", (i, c))
                    for cc in range(2):
                        k = 2 * c + cc
                        for f in range(KC):
                            last = mm(half(4, f), w[:, cc * D + f * P:cc * D + (f + 1) * P], y[:, k, :], k == 0 and f % 2 == 0, k == 3)
                    last.then_inc(slots_used, 1)
                pe.wait_ge(slots_used, index[("branch", (i, 1))] + 1)
                pe.sem_inc(branch_ps, 1)
            pe.wait_ge(merged_sb, 3)
            for c in range(KC // 2):
                w = take("out", c)
                for cc in range(2):
                    k = 2 * c + cc
                    for t in range(TT):
                        for n in range(2):
                            last = mm(ps[:, 2 * t + n, :], mergedT[:, k, t * P:(t + 1) * P],
                                      w[:, cc * D + n * 512:cc * D + (n + 1) * 512], k == 0, k == KC - 1)
                last.then_inc(slots_used, 1)
            pe.wait_ge(slots_used, NMIX)
            pe.sem_inc(out_ps, 1)
            for t in range(TT):
                pe.wait_ge(hn_sb, t + 1)
                for c in range(KC):
                    last = pe.transpose(half(4, c)[:, t * P:(t + 1) * P], hn[:, t, c * P:(c + 1) * P], ident)
            last.then_inc(hnT_ps, 1)
            pe.wait_ge(hnT_sb, 1)
            pe.wait_ge(late_loaded, 16 * 5)
            for t in range(TT):
                for c in range(KC):
                    last = mm(ps[:, 0, t * NE:(t + 1) * NE], hnT[:, c, t * P:(t + 1) * P], wrt[:, c, :], t == 0 and c == 0, c == KC - 1)
            last.then_inc(logit_ps, 1)
            pe.wait_ge(chosen_sb, 1)
            before = const("before")
            mm(ps[:, 1, 0:NE], before, chosen[:, 0, :])
            mm(ps[:, 1, NE:2 * NE], ones, chosen[:, 0, :], False)
            mm(ps[:, 1, NE:2 * NE], before, chosen[:, 1, :], False)
            mm(ps[:, 2, 0:NE], ones, chosen[:, 0, :])
            mm(ps[:, 2, 0:NE], ones, chosen[:, 1, :], False).then_inc(rank_ps, 1)
            pe.wait_ge(gates_sb, 1)
            for t in range(TT):
                last = pe.transpose(ps[0:NE, 3, t * P:(t + 1) * P], gates[:, t, :], ident)
            last.then_inc(gT_ps, 1)
            pe.wait_ge(gT_sb, 1)
            for t in range(TT):
                for n in range(2):
                    last = mm(ps[:, 4 + 2 * t + n, :], gatesT[0:NE, t * P:(t + 1) * P], b2rows[0:NE, n * 512:(n + 1) * 512])
            last.then_inc(b2_ps, 1)
            pe.wait_ge(route_done, 1)

            def gather(N):
                pe.wait_ge(sel_sb, N + 1)
                for c in range(KC):
                    for t in range(TT):
                        last = mm(ps[:, 4 + c // 4, (c % 4) * P:(c % 4 + 1) * P], hn[:, t, c * P:(c + 1) * P],
                                  sel[:, t, :, :], c % 4 == 0 and t == 0, t == 1)
                last.then_inc(xg_ps, 1)

            def up(E, N, parity, between, zero=False):
                pe.wait_ge(b1_full[parity], (N + 1) * 16)
                if parity == 0:
                    pe.wait_ge(xg_sb, N * 2 + 2)
                for z in range(2):
                    for hf in range(2):
                        mm(ps[64 * hf:64 * hf + 64, z, :], ones[0:1, 0:SLOTS],
                           b1row[0:1, parity, hf * D + z:(hf + 1) * D:2], True, False)
                for c in range(KC):
                    s, times, n = w1_place(c, E, zero)
                    pe.wait_ge(slot_full[s], times * 16 + 16 * uses[s])
                    for z in range(2):
                        for hf in range(2):
                            last = mm(ps[64 * hf:64 * hf + 64, z, :], xg[:, c, parity * SLOTS:(parity + 1) * SLOTS],
                                      slot(s)[:, hf * D + z:(hf + 1) * D:2], False, c == KC - 1)
                    last.then_inc(slots_used, 1)
                    if between:
                        between(c)
                pe.wait_ge(slots_used, n + (NMIX + 1))
                pe.sem_inc(up_ps, 1)

            def down(E, final=False):
                pe.wait_ge(actT_sb, E + 1)
                for i in range(4):
                    s, times, n = w2_place(i, E, final)
                    pe.wait_ge(slot_full[s], times * 16 + 16 * uses[s])
                    for cc in range(2):
                        k = 2 * i + cc
                        for dh in range(2):
                            last = mm(ps[64 * dh:64 * dh + 64, 3, :], actT[:, k % 4, k // 4, :],
                                      slot(s)[:, cc * D + dh * 512:cc * D + (dh + 1) * 512], k == 0, k == 7)
                    last.then_inc(slots_used, 1)
                pe.wait_ge(slots_used, n + (NMIX + 1))
                pe.sem_inc(down_ps, 1)

            def turn(E):
                pe.wait_ge(act_sb, E + 1)
                for m in range(4):
                    last = pe.transpose(ps[:, 2, m * P:(m + 1) * P], act_[:, m * P:(m + 1) * P], ident)
                last.then_inc(actT_ps, 1)

            def turn_gates(N, first):
                pe.wait_ge(selg_sb, N + 1)
                if not first:
                    pe.wait_ge(acc_sb, N * 2)
                for t in range(TT):
                    last = pe.transpose(ps[:, 6, t * P:(t + 1) * P], selg[:, t, :, :].rearrange("p e s -> p (e s)"), ident)
                last.then_inc(selgT_ps, 1)

            def scatter(N, t):
                if t == 0:
                    pe.wait_ge(selgT_sb, N + 1)
                    pe.wait_ge(yrow_sb, N * 4 + 4)
                else:
                    pe.wait_ge(acc_sb, N * 2 + 1)
                for n in range(2):
                    last = mm(ps[:, 6 + n, :], selgT[:, t, :], yrow[:, n * 512:(n + 1) * 512])
                last.then_inc(sc_ps, 1)

            def pair(q, k, first, last, very_first=False):
                E, N = q * NE + k * 2, q * NPAIR + k
                if not very_first:
                    pe.wait_ge(up_read, E)
                up(E, N, 0, None, first)
                if not first:
                    down(E - 1)
                turn(E)

                def between(c):
                    if c == 0:
                        turn_gates(N - 1, False)
                    elif c == 2:
                        scatter(N - 1, 0)
                    elif c == 5:
                        scatter(N - 1, 1)

                pe.wait_ge(up_read, E + 1)
                up(E + 1, N, 1, None if first else between)
                if not last:
                    gather(N + 1)
                down(E)
                turn(E + 1)

            def one_pass(q, very_first=False):
                N0 = q * NPAIR
                gather(N0)
                pair(q, 0, True, False, very_first)
                with pe.Fori(1, NPAIR - 1) as k:
                    pair(q, k, False, False)
                pair(q, NPAIR - 1, False, True)
                down(q * NE + NE - 1, True)
                turn_gates(N0 + NPAIR - 1, False)
                scatter(N0 + NPAIR - 1, 0)
                scatter(N0 + NPAIR - 1, 1)

            one_pass(0, True)
            most = pe.value_load(cnti[0:1, 0:1], min_val=0, max_val=T)
            with pe.If(most > SLOTS):
                with pe.Fori(1, PASSES) as q:
                    one_pass(q)

        @block.scalar
        def _(act):
            steps = [0]

            def link(ins):
                steps[0] += 1
                ins.then_inc(act_step, 1)
                act.wait_ge(act_step, steps[0])

            act.dma_start(cst[:], consts).then_inc(cst_loaded, 16)
            for name, src, width in (("attn", attn_norm_w, 8), ("memn", mem_norm_w, 8), ("mu", rwkv_mu, 14),
                                     ("w0", rwkv_w0, 4), ("a0", rwkv_a0, 4), ("kk", rwkv_kk, 4), ("ka", rwkv_ka, 4),
                                     ("rk", rwkv_rk.rearrange("l h n -> l (h n)"), 4), ("lnw", rwkv_lnx_w, 4),
                                     ("lnb", rwkv_lnx_b, 4), ("bswa", b_swa, 6)):
                act.dma_start(prows[PCOLS[name]:PCOLS[name] + width, :],
                              src[0].rearrange("(r c) -> r c", c=P)).then_inc(prm_loaded, 16)
            act.dma_start(lora[0:64, :], rwkv_w2[0]).then_inc(lora_loaded, 16)
            act.dma_start(lora[64:P, :], rwkv_a2[0]).then_inc(lora_loaded, 16)
            act.dma_start(gate2[:], rwkv_g2[0]).then_inc(lora_loaded, 16)
            act.dma_start(sinks[:], swa_sinks.to_broadcast([P, 8])).then_inc(sink_loaded, 16)

            act.wait_ge(x_loaded, 16)
            act.wait_ge(mem_loaded, 16)
            for i, src in enumerate((xrows, memrows)):
                for t in range(TT):
                    link(act.activation(dump[:, t, :], src[:, t, :], ACT.Square, accum_out=ss[:, 2 * i + t:2 * i + t + 1]))
            act.wait_ge(zeroed, 2)
            act.activation(ss[:, 4:8], ss[:, 0:4], ACT.Sqrt, scale=1.0 / D, bias=epsc[:, 0:1]).then_inc(root, 1)
            act.wait_ge(memT_ps, 1)
            for c in range(KC):
                last = act.activation(memT[:, c, :], ps[:, 4 + c // 2, (c % 2) * T:(c % 2 + 1) * T], ACT.Copy, scale=col("memn", c))
            last.then_inc(memT_sb, 1)
            act.wait_ge(rwkv_ps, 1)
            for b in (6, 0, 1, 2, 3, 4, 5):
                act.activation(raw[:, 2 * b:2 * b + 2, 1:T + 1], ps[:, b, :].rearrange("p (c t) -> p c t", c=2), ACT.Copy).then_inc(raw_sb, 1)
            act.wait_ge(lora_in, 1)
            act.activation(proj[0:64, 12, :], proj[0:64, 12, :], ACT.Tanh).then_inc(lora_act, 1)
            act.activation(proj[:, 13, :], proj[:, 13, :], ACT.Sigmoid).then_inc(lora_act, 1)
            act.wait_ge(rest_ps, 1)
            for f in range(4):
                act.activation(sq_[:, f, :], ps[:, f // 2, (f % 2) * T:(f % 2 + 1) * T], ACT.Identity, scale=SWA_SCALE,
                               bias=bq[:, f:f + 1]).then_inc(rest_sb, 1)
            act.activation(skd[0:64, 0, :], ps[0:64, 2, 0:T], ACT.Identity, bias=col("bswa", 4)[0:64]).then_inc(rest_sb, 1)
            act.activation(skd[64:P, 1, :], ps[64:P, 2, 0:T], ACT.Identity, bias=col("bswa", 4)[64:P]).then_inc(rest_sb, 1)
            act.activation(svT, ps[:, 2, T:2 * T], ACT.Identity, bias=col("bswa", 5)).then_inc(rest_sb, 1)
            act.wait_ge(rest_sb, 7)
            act.activation(skd[64:P, 0, :], skd[0:64, 0, :], ACT.Copy).then_inc(rest_sb, 1)
            act.activation(skd[0:64, 1, :], skd[64:P, 1, :], ACT.Copy).then_inc(rest_sb, 1)
            act.activation(mq[:, 0:2, :], ps[:, 3, :].rearrange("p (c t) -> p c t", c=2), ACT.Copy).then_inc(rest_sb, 1)
            act.activation(mq[:, 2:4, :], ps[:, 4, :].rearrange("p (c t) -> p c t", c=2), ACT.Copy).then_inc(rest_sb, 1)
            act.wait_ge(kv_ps, 1)
            for b in range(2):
                act.activation(kmT[:, 2 * b:2 * b + 2, :], ps[:, 5 + b, :].rearrange("p (c t) -> p c t", c=2), ACT.Copy).then_inc(kv_sb, 1)
            for t in range(TT):
                act.activation(vm[:, t, :], ps[:, (7 + t) % 8, :], ACT.Copy).then_inc(kv_sb, 1)
            act.wait_ge(shifted, 1)
            act.wait_ge(zw_ps, 1)
            for f in range(HP):
                last = act.activation(pex[:, f, :], ps[:, 1 + f // 2, (f % 2) * T:(f % 2 + 1) * T], ACT.Sigmoid, bias=col("w0", f))
            last.then_inc(rate_sb, 1)
            act.wait_ge(za_ps, 1)
            for f in range(HP):
                last = act.activation(rate_a[:, f, :], ps[:, 3 + f // 2, (f % 2) * T:(f % 2 + 1) * T], ACT.Sigmoid, bias=col("a0", f))
            last.then_inc(a_sb, 1)
            act.wait_ge(g_ps, 1)
            for b in range(2):
                last = act.activation(gT[:, 2 * b:2 * b + 2, :], ps[:, 5 + b, :].rearrange("p (c t) -> p c t", c=2), ACT.Copy)
            last.then_inc(g_sb, 1)
            act.wait_ge(kk_clamped, 1)
            act.activation(pinc, pinc, ACT.Sqrt).then_inc(kk_root, 1)
            act.wait_ge(svT_ps, 1)
            act.activation(sv, ps[:, 5, 0:T].rearrange("p (t f) -> p t f", t=TT), ACT.Copy).then_inc(sv_sb, 1)
            act.wait_ge(csum_sb, 1)
            act.activation(pinc, csum, ACT.Exp, scale=-EXP_HALF).then_inc(powers_sb, 1)
            act.activation(pinv, csum, ACT.Exp, scale=EXP_HALF).then_inc(powers_sb, 1)
            act.activation(pex, pex, ACT.Exp, scale=-EXP_HALF).then_inc(powers_sb, 1)
            pm = probs.rearrange("p (n h m) -> p n h m", n=2, h=4)
            for n in range(TT):
                act.wait_ge(negmax, n + 1)
                for h in range(4):
                    last = act.activation(pm[:, n, h, :], ps[:, 1 + 2 * n + h // 2, (h % 2) * T:(h % 2 + 1) * T], ACT.Exp,
                                          scale=MEM_SCALE, bias=stat[:, 1, 4 * n + h:4 * n + h + 1],
                                          accum_out=stat[:, 2, 4 * n + h:4 * n + h + 1])
                last.then_inc(expd, 1)
            for n in range(TT):
                act.wait_ge(pT_ps, n + 1)
                for b in range(2):
                    act.activation(probsT[:, n * D + b * 512:n * D + (b + 1) * 512], ps[:, (5 + 2 * n + b) % 8, :], ACT.Copy).then_inc(pT_sb, 1)
            for n in range(TT):
                act.wait_ge(pv_ps, n + 1)
                act.activation(y_mem[:, :, n * P:(n + 1) * P], ps[:, 1 + n, :].rearrange("p (c t) -> p c t", c=4), ACT.Copy).then_inc(pv_sb, 1)
            act.wait_ge(sink_loaded, 16)
            for n in range(TT):
                W = P * (n + 1)
                act.wait_ge(negmax, n + 3)
                for h in range(8):
                    o = (h % 2) * 4 + h // 2
                    act.activation(probs[:, o * W:(o + 1) * W], probs[:, o * W:(o + 1) * W], ACT.Exp,
                                   bias=stat[:, 1, o:o + 1], accum_out=stat[:, 2, o:o + 1])
                act.activation(stat[:, 4, :], stat[:, 3, :], ACT.Exp).then_inc(expd, 1)
                act.wait_ge(pT_ps, n + 3)
                for b in range(2 * (n + 1)):
                    act.activation(probsT[:, b * 512:(b + 1) * 512], ps[:, (5 if n == 0 else 3) + b, :], ACT.Copy).then_inc(pT_sb, 1)
                act.wait_ge(pv_ps, n + 3)
                act.activation(y_swa[:, :, n * P:(n + 1) * P], ps[:, 1 + n, :].rearrange("p (c t) -> p c t", c=4), ACT.Copy).then_inc(pv_sb, 1)
            for i, dst in enumerate((btok, ktok, vtok)):
                for t in range(TT):
                    act.wait_ge(tok_ps, 2 * i + t + 1)
                    act.activation(dst[:, t, :], ps[:, (3 + 2 * i + t) % 8, :], ACT.Copy).then_inc(tok_sb, 1)

            def own_half(a):
                return a.rearrange("p (c q v) -> p c q v", q=4, v=64)[:, :, 0:4:3, :]

            for t in range(TT):
                act.wait_ge(av_ps, t + 1)
                for b in range(2):
                    act.activation(av[:, t, b * T:(b + 1) * T].rearrange("p (c a v) -> p c a v", a=2, v=64),
                                   own_half(ps[:, 4 + 2 * t + b, :]), ACT.Copy).then_inc(av_sb, 1)
            for ch in range(NCH):
                rs = slice(64 * (ch % 2), 64 * (ch % 2) + 64)
                act.wait_ge(u_ps, ch + 1)
                for b in range(2):
                    last = act.activation(us[rs, ch // 2, b * T:(b + 1) * T].rearrange("p (c a v) -> p c a v", a=2, v=64),
                                          own_half(ps[rs, 1 + b, :]), ACT.Copy)
                last.then_inc(u_sb, 1)
            act.wait_ge(var_ps, 1)
            for b in range(2):
                last = act.activation(sqr[:, 2 * b:2 * b + 2, :], ps[:, 6 + b, :].rearrange("p (c t) -> p c t", c=2), ACT.Sqrt,
                                      scale=1.0 / 64, bias=epsc[:, 1:2])
            last.then_inc(var_root, 1)
            for i in range(3):
                act.wait_ge(gate_ps, i + 1)
                if i:
                    act.wait_ge(merged_sb, i)
                for b in range(4):
                    last = act.activation(gsig[:, b, :], ps[:, b, :], ACT.Sigmoid)
                last.then_inc(gate_sb, 1)
            for t in range(TT):
                act.wait_ge(resid, t + 1)
                act.activation(hnT.rearrange("p c t -> p (c t)")[:, t * D:(t + 1) * D], xrows[:, t, :], ACT.Square,
                               accum_out=ss[:, t:t + 1]).then_inc(ffn_ss, 1)
            act.wait_ge(ffn_ss, 2)
            act.activation(ss[:, 4:6], ss[:, 0:2], ACT.Sqrt, scale=1.0 / D, bias=epsc[:, 0:1]).then_inc(ffn_root, 1)
            act.wait_ge(hnT_ps, 1)
            for b in range(4):
                last = act.activation(hnT[:, 2 * b:2 * b + 2, :], ps[:, 4 + b, :].rearrange("p (c t) -> p c t", c=2), ACT.Copy)
            last.then_inc(hnT_sb, 1)
            act.wait_ge(top_sb, 1)
            for t in range(TT):
                last = act.activation(gates[:, t, :], logit[:, t, :], ACT.Exp, bias=rtmp[:, t, 0:1])
            last.then_inc(top_exp, 1)
            act.wait_ge(gT_ps, 1)
            act.activation(gatesT[0:NE, :], ps[0:NE, 3, 0:T], ACT.Copy).then_inc(gT_sb, 1)
            act.wait_ge(route_done, 1)

            def gathered(N):
                act.wait_ge(xg_ps, N + 1)
                for b in range(2):
                    act.activation(xg[:, 4 * b:4 * b + 4, :], ps[:, 4 + b, :].rearrange("p (c s) -> p c s", c=4), ACT.Copy).then_inc(xg_sb, 1)

            def sigmoid(E):
                act.wait_ge(glu_sb, E + 1)
                act.activation(sig, glu, ACT.Sigmoid, scale=ALPHA).then_inc(sig_sb, 1)

            def downed(E, parity):
                act.wait_ge(down_ps, E + 1)
                for dh in range(2):
                    act.activation(yrow[64 * parity:64 * parity + 64, dh * 512:(dh + 1) * 512], ps[64 * dh:64 * dh + 64, 3, :],
                                   ACT.Copy).then_inc(yrow_sb, 1)

            def turned(E):
                act.wait_ge(actT_ps, E + 1)
                act.activation(actT.rearrange("p m h s -> p (m h s)"), ps[:, 2, :], ACT.Copy).then_inc(actT_sb, 1)

            def gates_turned(N):
                act.wait_ge(selgT_ps, N + 1)
                act.activation(selgT.rearrange("p t n -> p (t n)"), ps[:, 6, 0:T], ACT.Copy).then_inc(selgT_sb, 1)

            def pair(q, k, first, last):
                E, N = q * NE + k * 2, q * NPAIR + k
                sigmoid(E)
                if not first:
                    downed(E - 1, 1)
                turned(E)
                if not first:
                    gates_turned(N - 1)
                sigmoid(E + 1)
                if not last:
                    gathered(N + 1)
                downed(E, 0)
                turned(E + 1)

            def one_pass(q):
                gathered(q * NPAIR)
                pair(q, 0, True, False)
                with act.Fori(1, NPAIR - 1) as k:
                    pair(q, k, False, False)
                pair(q, NPAIR - 1, False, True)
                downed(q * NE + NE - 1, 1)
                gates_turned(q * NPAIR + NPAIR - 1)

            one_pass(0)
            most = act.value_load(cnti[0:1, 0:1], min_val=0, max_val=T)
            with act.If(most > SLOTS):
                with act.Fori(1, PASSES) as q:
                    one_pass(q)
            act.wait_ge(moe_done, 1)
            for t in range(TT):
                act.activation(outrow[:, t, :], xrows[:, t, :], ACT.Square, accum_out=ss[:, t:t + 1]).then_inc(fin_ss, 1)
            act.wait_ge(fin_ss, 2)
            act.activation(ss[:, 4:6], ss[:, 0:2], ACT.Sqrt, scale=1.0 / D, bias=epsc[:, 0:1]).then_inc(fin_root, 1)

        @block.vector
        def _(dve):
            steps = [0]

            def step(ins):
                steps[0] += 1
                ins.then_inc(dve_step, 1)

            def settle():
                dve.wait_ge(dve_step, steps[0])

            def link(ins):
                step(ins)
                settle()

            TS, TTn, STT = dve.tensor_scalar, dve.tensor_tensor, dve.scalar_tensor_tensor

            dve.memset(epsc[:, 0:1], EPS).then_inc(zeroed, 1)
            dve.memset(epsc[:, 1:2], LNX_EPS).then_inc(zeroed, 1)
            dve.wait_ge(prm_ps, 1)
            link(dve.tensor_copy(prm[:], ps[:, 7, 0:NPCOL]))
            step(TS(omka[:], prm[:, PCOLS["ka"]:PCOLS["ka"] + 4], -1.0, 1.0, ALU.mult, ALU.add))
            TS(bq[:], prm[:, PCOLS["bswa"]:PCOLS["bswa"] + 4], SWA_SCALE, None, ALU.mult).then_inc(prm_sb, 1)
            dve.wait_ge(root, 1)
            link(dve.reciprocal(ss[:, 4:8], ss[:, 4:8]))
            for t in range(TT):
                TS(xscaled[:, t, :], xrows[:, t, :], ss[:, 4 + t:5 + t], None, ALU.mult).then_inc(scaled, 1)
            for t in range(TT):
                TS(memrows[:, t, :], memrows[:, t, :], ss[:, 6 + t:7 + t], None, ALU.mult).then_inc(scaled_m, 1)
            dve.wait_ge(xT_ps, 1)
            for c in range(KC):
                last = TS(xT[:, c, :], ps[:, c // 2, (c % 2) * T:(c % 2 + 1) * T], col("attn", c), None, ALU.mult)
            last.then_inc(xT_sb, 1)
            dve.wait_ge(mem_loaded, 16)
            link(dve.memset(raw[:, :, 0:1], 0.0))

            def shift(a, b, signal):
                link(TTn(proj[:, a:b, :], raw[:, a:b, 0:T], raw[:, a:b, 1:T + 1], ALU.subtract))
                for f in range(a, b):
                    last = STT(proj[:, f, :], proj[:, f, :], col("mu", f), raw[:, f, 1:T + 1], ALU.mult, ALU.add)
                last.then_inc(signal, 1)

            dve.wait_ge(raw_sb, 1)
            shift(12, 14, lora_in)
            dve.wait_ge(raw_sb, 7)
            shift(0, 12, shifted)
            dve.wait_ge(shifted, 1)
            for f in range(HP):
                step(TS(kkn[:, f, :], proj[:, 4 + f, :], col("kk", f), None, ALU.mult))
            settle()
            TTn(csum, kkn, kkn, ALU.mult).then_inc(kk_sq, 1)
            dve.wait_ge(kk_ps, 1)
            for b in range(2):
                last = TS(pinc[:, 2 * b:2 * b + 2, :], ps[:, (7 + b) % 8, :].rearrange("p (c t) -> p c t", c=2), 1e-24, None, ALU.max)
            last.then_inc(kk_clamped, 1)
            dve.wait_ge(rate_sb, 1)
            for f in range(HP):
                step(dve.tensor_tensor_scan(csum[:, f, :], const("resets"), pex[:, f, :], 0.0, ALU.mult, ALU.add))
            settle()
            dve.wait_ge(kk_root, 1)
            link(dve.reciprocal(pinc, pinc))
            link(TTn(kkn, kkn, pinc, ALU.mult))
            TTn(pex, csum, pex, ALU.subtract).then_inc(csum_sb, 1)
            dve.wait_ge(a_sb, 1)
            link(TTn(ar[:, :, 0, :], kkn, rate_a, ALU.mult))
            for f in range(HP):
                step(TS(rate_a[:, f, :], rate_a[:, f, :], col("ka", f), omka[:, f:f + 1], ALU.mult, ALU.add))
            settle()
            link(TTn(proj[:, 4:8, :], proj[:, 4:8, :], rate_a, ALU.mult))
            dve.wait_ge(powers_sb, 2)
            step(TTn(bT, ar[:, :, 0, :], pinv, ALU.mult))
            step(TTn(kT, proj[:, 4:8, :], pinv, ALU.mult))
            step(TTn(ar[:, :, 1, :], proj[:, 0:4, :], pinc, ALU.mult))
            for c in range(NCH):
                step(dve.tensor_copy(pend[:, :, c], pinc[:, :, c * CH + CH - 1]))
            dve.wait_ge(powers_sb, 3)
            settle()
            STT(ar[:, :, 0, :], kkn, -1.0, pex, ALU.mult, ALU.mult).then_inc(tilde_sb, 1)
            dve.wait_ge(tilde_sb, 1)
            for f in range(HP):
                last = STT(kkn[:, f, :], proj[:, f, :], col("rk", f), proj[:, 4 + f, :], ALU.mult, ALU.mult)
            last.then_inc(rk_sb, 1)
            for n in range(TT):
                dve.wait_ge(score_ps, n + 1)
                link(dve.tensor_reduce(stat[:, 0, 4 * n:4 * n + 4],
                                       ps[:, 1 + 2 * n:3 + 2 * n, :].rearrange("p b (h m) -> p (b h) m", h=2), AX.X, ALU.max))
                TS(stat[:, 1, 4 * n:4 * n + 4], stat[:, 0, 4 * n:4 * n + 4], -MEM_SCALE, None, ALU.mult).then_inc(negmax, 1)
            dve.wait_ge(rk_ps, 1)
            for b in range(2):
                last = TTn(bonus[:, 2 * b:2 * b + 2, :], ps[:, (7 + b) % 8, :].rearrange("p (c t) -> p c t", c=2),
                           proj[:, 8 + 2 * b:10 + 2 * b, :], ALU.mult)
            last.then_inc(bonus_sb, 1)
            pm = probs.rearrange("p (n h m) -> p n h m", n=2, h=4)
            for n in range(TT):
                dve.wait_ge(expd, n + 1)
                link(dve.reciprocal(stat[:, 5, 4 * n:4 * n + 4], stat[:, 2, 4 * n:4 * n + 4]))
                TTn(pm[:, n], pm[:, n], stat[:, 5, 4 * n:4 * n + 4].unsqueeze(2).to_broadcast([P, 4, T]), ALU.mult).then_inc(normed, 1)
            dve.wait_ge(sink_loaded, 16)
            for n in range(TT):
                W = P * (n + 1)
                dve.wait_ge(score_ps, n + 3)
                dve.wait_ge(pT_ps, n + 2)
                for h in range(8):
                    o = (h % 2) * 4 + h // 2
                    if n == 0:
                        src = ps[:, 3 + h % 2, (h // 2) * P:(h // 2 + 1) * P]
                    else:
                        src = ps[:, 3 + h // 4 if h % 2 == 0 else (7 + h // 4) % 8, (h // 2 % 2) * T:(h // 2 % 2 + 1) * T]
                    step(STT(probs[:, o * W:(o + 1) * W], const("dist", 2 * P - W, W), -SLOPES[h], src, ALU.mult, ALU.add))
                settle()
                if n == 0:
                    link(dve.tensor_copy(stat[:, 5, :].rearrange("p (a c) -> p a c", a=2),
                                         sinks[:].rearrange("p (c a) -> p a c", a=2)))
                    link(dve.tensor_copy(sinks[:], stat[:, 5, :]))
                link(dve.tensor_reduce(stat[:, 0, :], probs[:, 0:8 * W].rearrange("p (h m) -> p h m", h=8), AX.X, ALU.max))
                link(TTn(stat[:, 0, :], stat[:, 0, :], sinks[:], ALU.max))
                step(TTn(stat[:, 3, :], sinks[:], stat[:, 0, :], ALU.subtract))
                settle()
                TS(stat[:, 1, :], stat[:, 0, :], -1.0, None, ALU.mult).then_inc(negmax, 1)
                dve.wait_ge(expd, n + 3)
                link(TTn(stat[:, 5, :], stat[:, 2, :], stat[:, 4, :], ALU.add))
                link(dve.reciprocal(stat[:, 5, :], stat[:, 5, :]))
                pw = probs[:, 0:8 * W].rearrange("p (h m) -> p h m", h=8)
                TTn(pw, pw, stat[:, 5, :].unsqueeze(2).to_broadcast([P, 8, W]), ALU.mult).then_inc(normed, 1)

            for g in range(4):
                for i in range(4):
                    n = 4 * g + i
                    dve.wait_ge(gram_ps, n + 1)
                    TTn(gram[:, n].rearrange("p (x y) t -> p x y t", x=2), ps[:, n % 6, :].rearrange("p (x y t) -> p x y t", x=2, y=2),
                        const("causal").rearrange("p (y t) -> p y t", y=2).unsqueeze(1).to_broadcast([P, 2, 2, P]),
                        ALU.mult).then_inc(gram_sb, 1)
                us4 = slice(4 * g, 4 * g + 4)
                dve.wait_ge(gram_sb, 4 * g + 4)
                step(TTn(invT[:, us4, :], gram[:, us4, 0, :], const("level0t").unsqueeze(1).to_broadcast([P, 4, P]), ALU.mult))
                dve.wait_ge(ab_ps, g + 1)
                link(TTn(inv[:, us4, :], ps[:, 6 + g % 2, :].rearrange("p (u t) -> p u t", u=4),
                         const("level", 0, P).unsqueeze(1).to_broadcast([P, 4, P]), ALU.mult))
                step(TTn(invT[:, us4, :], invT[:, us4, :], ident.unsqueeze(1).to_broadcast([P, 4, P]), ALU.add))
                TTn(inv[:, us4, :], inv[:, us4, :], ident.unsqueeze(1).to_broadcast([P, 4, P]), ALU.add).then_inc(inv_sb, 1)
            for j in range(1, LEVELS):
                for g in range(4):
                    dve.wait_ge(t1_ps, 4 * (j - 1) + g + 1)
                    TTn(t1s[:, g], ps[:, g, :].rearrange("p (u t) -> p u t", u=4),
                        const("level", j * P, P).unsqueeze(1).to_broadcast([P, 4, P]), ALU.mult).then_inc(t1_sb, 1)
                for g in range(4):
                    us4 = slice(4 * g, 4 * g + 4)
                    dve.wait_ge(xx_ps, 4 * (j - 1) + g + 1)
                    dve.wait_ge(inv_sb, 4 * (j - 1) + g + 1)
                    if j < LEVELS - 1:
                        TTn(inv[:, us4, :], inv[:, us4, :], ps[:, 4 + 2 * (g % 2), :].rearrange("p (u t) -> p u t", u=4), ALU.add)
                    TTn(invT[:, us4, :], invT[:, us4, :], ps[:, 5 + 2 * (g % 2), :].rearrange("p (u t) -> p u t", u=4),
                        ALU.add).then_inc(inv_sb, 1)
            step(dve.memset(state[:, 0], 0.0))
            dve.memset(rs_, 0.0).then_inc(zeroed, 1)
            for ch in range(NCH):
                t, c = ch // 2, ch % 2
                rs = slice(64 * c, 64 * c + 64)
                step(TTn(decay_end[:, ch % 2], heads.unsqueeze(1).to_broadcast([P, HP, P]),
                         pend[:, :, ch].unsqueeze(2).to_broadcast([P, HP, P]), ALU.mult))
                dve.wait_ge(r_ps, ch + 1)
                dve.wait_ge(av_sb, 4)
                if ch == 0:
                    dve.wait_ge(zeroed, 3)
                else:
                    dve.wait_ge(u_ps, ch)
                TTn(rs_[rs, :], ps[rs, 0, :], av[rs, t, :], ALU.add).then_inc(r_sb, 1)
                if ch < NCH - 1:
                    dve.wait_ge(s_ps, ch + 1)
                    settle()
                    link(TTn(state[:, (ch + 1) % 2], state[:, ch % 2], ps[:, 3, :].rearrange("p (c v) -> p c v", c=HP), ALU.add))
                    TTn(state[:, (ch + 1) % 2], state[:, (ch + 1) % 2], decay_end[:, ch % 2], ALU.mult).then_inc(s_sb, 1)
                    dve.wait_ge(s_sb, ch + 1)
                if c == 1:
                    dve.wait_ge(yh_ps, t + 1)
                    step(dve.tensor_copy(yT[:, :, t * P:(t + 1) * P], ps[:, 4 + t, :].rearrange("p (c v) -> p c v", c=HP)))
            settle()
            dve.sem_inc(yh_sb, 1)
            dve.wait_ge(mean_ps, 1)
            for b in range(2):
                step(STT(yc[:, 2 * b:2 * b + 2, :], ps[:, 6 + b, :].rearrange("p (c t) -> p c t", c=2), -1.0 / 64,
                         yT[:, 2 * b:2 * b + 2, :], ALU.mult, ALU.add))
            settle()
            dve.sem_inc(yc_sb, 1)
            TTn(sqr, yc, yc, ALU.mult).then_inc(yc_sb, 1)
            dve.wait_ge(var_root, 1)
            link(dve.reciprocal(sqr, sqr))
            link(TTn(yc, yc, sqr, ALU.mult))
            for f in range(HP):
                step(TS(yc[:, f, :], yc[:, f, :], col("lnw", f), col("lnb", f), ALU.mult, ALU.add))
            settle()
            link(TTn(yc, yc, bonus, ALU.add))
            TTn(gT, gT, yc, ALU.mult).then_inc(y_rwkv_sb, 1)
            for i in range(3):
                dve.wait_ge(branch_ps, i + 1)
                dve.wait_ge(gate_sb, i + 1)
                if i == 0:
                    TTn(merged, gsig, ps[:, 4:8, :], ALU.mult).then_inc(merged_sb, 1)
                else:
                    link(TTn(gsig, gsig, ps[:, 4:8, :], ALU.mult))
                    dve.wait_ge(merged_sb, i)
                    TTn(merged, merged, gsig, ALU.add).then_inc(merged_sb, 1)
            dve.wait_ge(out_ps, 1)
            for t in range(TT):
                TTn(xrows[:, t, :].rearrange("p (b n) -> p b n", b=2), xrows[:, t, :].rearrange("p (b n) -> p b n", b=2),
                    ps[:, 2 * t:2 * t + 2, :], ALU.add).then_inc(resid, 1)
            dve.wait_ge(ffn_root, 1)
            dve.wait_ge(late_loaded, 16 * 5)
            link(dve.reciprocal(ss[:, 4:6], ss[:, 4:6]))
            for t in range(TT):
                STT(hn[:, t, :], xrows[:, t, :], ss[:, 4 + t:5 + t], ffnw, ALU.mult, ALU.mult).then_inc(hn_sb, 1)
            dve.wait_ge(logit_ps, 1)
            link(TTn(logit[:], ps[:, 0, 0:TT * NE].rearrange("p (t e) -> p t e", t=TT), brt[:].unsqueeze(1).to_broadcast([P, TT, NE]), ALU.add))
            for t in range(TT):
                step(dve.max(top8[:, t, :], logit[:, t, :]))
            settle()
            TS(rtmp[:, :, 0], top8[:, :, 0], -1.0, None, ALU.mult).then_inc(top_sb, 1)
            dve.wait_ge(top_sb, 1)
            link(dve.memset(top8[:, :, 4:8], 3e38))
            for t in range(TT):
                step(dve.match_replace(rest[:, t, :], top8[:, t, :], logit[:, t, :], -3e38))
            settle()
            TTn(chosen[:], rest[:], logit[:], ALU.not_equal).then_inc(chosen_sb, 1)
            dve.wait_ge(chosen_sb, 1)
            dve.wait_ge(top_exp, 1)
            link(TTn(gates[:], gates[:], chosen[:], ALU.mult))
            link(dve.tensor_reduce(rtmp[:, :, 1], gates[:], AX.X, ALU.add))
            link(dve.reciprocal(rtmp[:, :, 2], rtmp[:, :, 1]))
            TTn(gates[:], gates[:], rtmp[:, :, 2].unsqueeze(2).to_broadcast([P, TT, NE]), ALU.mult).then_inc(gates_sb, 1)
            dve.wait_ge(rank_ps, 1)
            step(STT(rank1[:], ps[:, 1, 0:TT * NE].rearrange("p (t e) -> p t e", t=TT), 1.0, chosen[:], ALU.add, ALU.mult))
            link(dve.tensor_reduce(cnt[:], ps[:, 2, 0:NE], AX.X, ALU.max))
            link(dve.tensor_copy(cnti[:], cnt[:]))
            dve.wait_ge(b2_ps, 1)
            for t in range(TT):
                step(TTn(xrows[:, t, :].rearrange("p (b n) -> p b n", b=2), xrows[:, t, :].rearrange("p (b n) -> p b n", b=2),
                         ps[:, 4 + 2 * t:6 + 2 * t, :], ALU.add))
            settle()
            dve.sem_inc(route_done, 1)

            def columns(a, k):
                return a[:, :, bass.ds(k * 2, 2)].unsqueeze(3).to_broadcast([P, TT, 2, SLOTS])

            def places(q):
                a = CONST["iota"][0]
                return cst[:, bass.ds(q * SLOTS + a, SLOTS)].unsqueeze(1).unsqueeze(1).to_broadcast([P, TT, 2, SLOTS])

            def select(q, k, N, very_first=False):
                if not very_first:
                    dve.wait_ge(xg_ps, N)
                TTn(sel, places(q), columns(rank1, k), ALU.is_equal).then_inc(sel_sb, 1)

            def select_gates(q, k, N, very_first=False):
                if not very_first:
                    dve.wait_ge(selgT_ps, N)
                TTn(selg, places(q), columns(rank1, k), ALU.is_equal).then_inc(selg_raw, 1)
                dve.wait_ge(selg_raw, N + 1)
                TTn(selg, selg, columns(gates, k), ALU.mult).then_inc(selg_sb, 1)

            def swiglu(E, very_first=False):
                dve.wait_ge(up_ps, E + 1)
                if not very_first:
                    dve.wait_ge(act_sb, E)
                TS(glu, ps[:, 0, :], LIMIT, None, ALU.min).then_inc(glu_sb, 1)
                TS(lin, ps[:, 1, :], LIMIT, -LIMIT, ALU.min, ALU.max).then_inc(up_read, 1)
                dve.wait_ge(up_read, E + 1)
                dve.wait_ge(glu_sb, E + 1)
                STT(lin, lin, 1.0, glu, ALU.add, ALU.mult).then_inc(prod_sb, 1)
                dve.wait_ge(prod_sb, E + 1)
                dve.wait_ge(sig_sb, E + 1)
                if not very_first:
                    dve.wait_ge(actT_ps, E)
                TTn(act_, lin, sig, ALU.mult).then_inc(act_sb, 1)

            def add_up(N, t, very_first=False):
                dve.wait_ge(sc_ps, N * 2 + t + 1)
                if not very_first:
                    dve.wait_ge(acc_sb, N * 2 + t)
                a = xrows[:, t, :].rearrange("p (b n) -> p b n", b=2)
                TTn(a, a, ps[:, 6:8, :], ALU.add).then_inc(acc_sb, 1)

            def pair(q, k, first, last, very_first=False, second=False):
                E, N = q * NE + k * 2, q * NPAIR + k
                if not last:
                    select(q, k + 1, N + 1)
                if not first:
                    select_gates(q, k - 1, N - 1, second)
                swiglu(E, very_first)
                if not first:
                    add_up(N - 1, 0, second)
                    add_up(N - 1, 1)
                swiglu(E + 1)

            def one_pass(q, very_first=False):
                select(q, 0, q * NPAIR, very_first)
                pair(q, 0, True, False, very_first)
                if very_first:
                    pair(q, 1, False, False, False, True)
                    with dve.Fori(2, NPAIR - 1) as k:
                        pair(q, k, False, False)
                else:
                    with dve.Fori(1, NPAIR - 1) as k:
                        pair(q, k, False, False)
                pair(q, NPAIR - 1, False, True)
                N = q * NPAIR + NPAIR - 1
                select_gates(q, NPAIR - 1, N)
                add_up(N, 0)
                add_up(N, 1)

            one_pass(0, True)
            most = dve.value_load(cnti[0:1, 0:1], min_val=0, max_val=T)
            with dve.If(most > SLOTS):
                with dve.Fori(1, PASSES) as q:
                    one_pass(q)
            dve.wait_ge(acc_sb, 2 * NPAIR)
            dve.sem_inc(moe_done, 1)
            dve.wait_ge(fin_root, 1)
            link(dve.reciprocal(ss[:, 4:6], ss[:, 4:6]))
            for t in range(TT):
                STT(outrow[:, t, :], xrows[:, t, :], ss[:, 4 + t:5 + t], finw, ALU.mult, ALU.mult).then_inc(final_sb, 1)


_INS = ["x", "mem", "attn_norm_w", "mem_norm_w", "w_in", "b_swa", "rwkv_mu", "rwkv_w0", "rwkv_w2", "rwkv_a0", "rwkv_a2",
        "rwkv_g2", "rwkv_kk", "rwkv_ka", "rwkv_rk", "rwkv_lnx_w", "rwkv_lnx_b", "swa_sinks", "w_mem_kv", "w_gate",
        "w_branch", "w_out", "ffn_norm_w", "w_router", "b_router", "w_exp1", "b_exp1", "w_exp2", "b_exp2", "final_norm_w"]


def kernel(**inputs):
    import concourse.bacc as bacc
    from concourse.bass_utils import run_bass_kernel_spmd

    nc = bacc.Bacc("TRN2", target_bir_lowering=False, num_devices=1)
    arrays = {f"in_{name}": np.ascontiguousarray(inputs[name]) for name in _INS}
    arrays["in_consts"] = constants()
    args = [nc.dram_tensor(name, a.shape, F32, kind="ExternalInput").ap() for name, a in arrays.items()]
    args.append(nc.dram_tensor("out_0", (1, T, D), F32, kind="ExternalOutput").ap())
    build(nc, *args)
    r = run_bass_kernel_spmd(nc, [arrays], core_ids=[0])
    return r.results[0]["out_0"]
```

```python
from contextlib import ExitStack

import numpy as np

import concourse.bass as bass
from concourse import mybir

P = 128
D = 1024
T = 256
KC = D // P
TT = T // P
F32 = mybir.dt.float32
I32 = mybir.dt.int32
ALU = mybir.AluOpType
ACT = mybir.ActivationFunctionType
AX = mybir.AxisListType

HR = 8
HP = HR // 2
CH = 64
NCH = T // CH
LEVELS = 6
EXP_HALF = float(np.exp(-0.5))
LNX_EPS = 64e-5
EPS = 1e-5
N_RWKV = 14
C_RWKV = N_RWKV * P
C_REST = 10 * P
MEM_SCALE = float(P) ** -0.5
SWA_SCALE = 64.0 ** -0.5
SLOPES = [2.0 ** (-8.0 * (h + 1) / 8) for h in range(8)]
MASKED = 1e30

NE = 32
NPAIR = NE // 2
SLOTS = 64
PASSES = T // SLOTS
ALPHA = 1.702
LIMIT = 7.0

RING = 12
HALF = RING // 2
SLOT = 2048
CPE = 12

PCOLS = {}
_at = 0
for _n, _w in (("attn", 8), ("memn", 8), ("mu", 14), ("w0", 4), ("a0", 4), ("kk", 4), ("ka", 4), ("rk", 4),
               ("lnw", 4), ("lnb", 4), ("bswa", 6)):
    PCOLS[_n] = _at
    _at += _w
NPCOL = _at

CONST = {}
_at = 0
for _n, _w in (("ident", P), ("heads", P), ("causal", 2 * P), ("level", LEVELS * P), ("level0t", P), ("before", P),
               ("ones", P), ("dist", 2 * P), ("iota", T), ("resets", T)):
    CONST[_n] = (_at, _w)
    _at += _w
NCONST = _at


def constants():
    c = np.zeros((P, NCONST), np.float32)

    def put(name, a):
        at, w = CONST[name]
        c[:, at:at + w] = a

    i = np.arange(P)
    p, f = i[:, None], i[None, :]
    same = (p // CH) == (f // CH)
    put("ident", p == f)
    put("heads", same)
    put("causal", np.concatenate([same & (p < f), same & (p <= f)], 1))
    level = [((p >> (j + 1)) == (f >> (j + 1))) & ((p >> j) % 2 == 1) & ((f >> j) % 2 == 0) for j in range(LEVELS)]
    put("level", np.concatenate(level, 1))
    put("level0t", level[0].T)
    put("before", p < f)
    put("ones", 1.0)
    j = np.arange(2 * P)[None, :]
    dist = p + P - j
    put("dist", np.where((dist >= 0) & (dist < P), dist, MASKED))
    put("iota", np.arange(1, T + 1)[None, :])
    put("resets", (np.arange(T)[None, :] % CH != 0))
    return c


BRANCHES = (2, 1, 0)
UNITS = [(b, f) for b in BRANCHES for f in range(4)]
PIECES = 6
N_FILL = 8


def fill_points():
    points = [(ch, s) for ch in range(NCH) for s in "abc"] + ["mean", "var", "rest"]
    counts = [1] * (3 * NCH) + [2, 3]
    counts.append(PIECES * N_FILL - sum(counts))
    at, out = 0, {}
    for p, n in zip(points, counts):
        out[p] = list(range(at, at + n))
        at += n
    return out


def mixer_chunks():
    order = [("in_rwkv", c) for c in range(KC)] + [("in_rest", c) for c in range(KC)]
    order += [("mem_kv", c) for c in range(KC // 2)]

    def merge(b):
        return [("gate", (b, 0)), ("gate", (b, 1)), ("branch", (b, 0)), ("gate", (b, 2)), ("gate", (b, 3)), ("branch", (b, 1))]

    order += merge(2) + merge(1)
    n_narrow = len(order)
    order += merge(0) + [("out", c) for c in range(KC // 2)]
    wide = len(order) - n_narrow
    slots = [n % HALF for n in range(n_narrow)] + [(n - wide) % RING for n in range(wide)]
    return order, slots


def build(nc, x, mem, w_in, rwkv_w2, rwkv_a2, rwkv_g2, swa_sinks, w_mem_kv, w_gate, w_branch, w_out,
          ffn_norm_w, w_router, b_router, w_exp1, b_exp1, w_exp2, b_exp2, final_norm_w, params, consts, out):
    order, slots = mixer_chunks()
    NMIX = len(order)
    index = {key: n for n, key in enumerate(order)}
    uses = [slots.count(s) for s in range(RING)]
    past = [slots[:n].count(s) for n, s in enumerate(slots)]
    previous = [max([m for m in range(n) if slots[m] == s], default=None) for n, s in enumerate(slots)]
    last_in = [max(m for m in range(NMIX) if slots[m] == s) for s in range(RING)]
    assert last_in == list(range(NMIX - RING, NMIX))

    with ExitStack() as ctx:
        def sb(name, shape, dt=F32):
            return ctx.enter_context(nc.sbuf_tensor(name, shape, dt))

        def sem(name):
            return ctx.enter_context(nc.semaphore(name))

        ring = sb("ring", [P, RING * SLOT])
        upper = sb("upper", [P, 70 * 256])
        cst = sb("cst", [P, NCONST])
        xrows = sb("xrows", [P, TT, D])
        xT = sb("xT", [P, KC, T])
        lora = sb("lora", [P, 512])
        gate2 = sb("gate2", [P, 512])
        merged = sb("merged", [P, 4, 512])
        prm = sb("prm", [P, NPCOL])
        omka = sb("omka", [P, HP])
        bq = sb("bq", [P, HP])
        epsc = sb("epsc", [P, 2])
        ss = sb("ss", [P, 8])
        sinks = sb("sinks", [P, 8])
        stat = sb("stat", [P, 6, 8])
        pend = sb("pend", [P, HP, NCH])
        brt = sb("brt", [P, NE])
        logit = sb("logit", [P, TT, NE])
        top8 = sb("top8", [P, TT, 8])
        rest = sb("rest", [P, TT, NE])
        chosen = sb("chosen", [P, TT, NE])
        gates = sb("gates", [P, TT, NE])
        rank1 = sb("rank1", [P, TT, NE])
        rtmp = sb("rtmp", [P, TT, 4])
        cnt = sb("cnt", [P, 1])
        cnti = sb("cnti", [P, 1], I32)
        ps = ctx.enter_context(nc.psum_tensor("ps", [P, 8, 512], F32))

        def kb(at, size, pattern=None, **dims):
            if at < 48:
                assert at + size <= 48
                a = ring[:, HALF * SLOT + at * 256:HALF * SLOT + (at + size) * 256]
            else:
                a = upper[:, (at - 48) * 256:(at - 48 + size) * 256]
            return a.rearrange(pattern, **dims) if pattern else a

        def const(name, at=0, width=None):
            a, w = CONST[name]
            return cst[:, a + at:a + at + (width or w)]

        def col(name, n=0):
            return prm[:, PCOLS[name] + n:PCOLS[name] + n + 1]

        ident = const("ident")
        heads = const("heads")
        ones = const("ones")
        four = "p (c t) -> p c t"

        proj = kb(0, 14, four, c=14)
        raw = ring[:, HALF * SLOT + 22 * 256:HALF * SLOT + 22 * 256 + N_RWKV * (T + 1)].rearrange(four, c=N_RWKV)
        csum = kb(14, 4, four, c=4)
        pex = kb(18, 4, four, c=4)
        pinv = kb(22, 4, four, c=4)
        pinc = kb(26, 4, four, c=4)
        rate_a = kb(30, 4, four, c=4)
        kkn = kb(34, 4, four, c=4)
        ar = kb(38, 8, "p (c k t) -> p c k t", c=4, k=2)
        bT = kb(48, 4, four, c=4)
        kT = kb(52, 4, four, c=4)
        gT = kb(56, 4, four, c=4)
        btok = kb(60, 4, "p (t f) -> p t f", t=TT)
        ktok = kb(64, 4, "p (t f) -> p t f", t=TT)
        vtok = kb(68, 4, "p (t f) -> p t f", t=TT)
        dump = kb(38, 8, "p (t f) -> p t f", t=TT)
        xscaled = kb(60, 8, "p (t f) -> p t f", t=TT)
        probs = kb(60, 8)
        mprobs = kb(14, 8)
        mprobsT = kb(22, 8)
        dump_m = kb(22, 8, "p (t f) -> p t f", t=TT)
        gram = kb(72, 32, "p (u k t) -> p u k t", u=16, k=4)
        memT = kb(72, 8, "p (c t) -> p c t", c=KC)
        memrows = kb(80, 8, "p (t f) -> p t f", t=TT)
        probsT = kb(80, 8)
        sq_ = kb(88, 4, four, c=4)
        skd = kb(92, 2, four, c=2)
        svT = kb(94, 1)
        sv = kb(95, 1, "p (t f) -> p t f", t=TT)
        mq = kb(96, 4, four, c=4)
        kmT = kb(100, 4, four, c=4)
        vm = kb(104, 4, "p (t f) -> p t f", t=TT)
        y_swa = kb(110, 4, four, c=4)
        y_mem = kb(114, 4, four, c=4)
        inv = kb(14, 8, "p (u t) -> p u t", u=16)
        invT = kb(22, 8, "p (u t) -> p u t", u=16)
        bonus = kb(30, 4, four, c=4)
        sqr = kb(34, 4, four, c=4)
        t1s = kb(0, 8, "p (g u t) -> p g u t", g=4, u=4)
        av = kb(0, 4, "p (t f) -> p t f", t=TT)
        us = kb(4, 4, "p (t f) -> p t f", t=TT)
        rs_ = kb(12, 2)
        state = kb(48, 4, "p (b c v) -> p b c v", b=2, c=HP)
        decay_end = kb(52, 4, "p (b c v) -> p b c v", b=2, c=HP)
        yT = kb(14, 4, four, c=4)
        yc = kb(18, 4, four, c=4)
        gsig = kb(104, 4, "p (b n) -> p b n", b=2)
        mergedT = merged[:].rearrange("p b (c t) -> p (b c) t", c=2)
        ffnw = kb(80, 4)
        finw = kb(84, 4)
        b1row = kb(88, 16, "p (e f) -> p e f", e=2)
        b2rows = kb(68, 4)
        wrt = kb(108, 1, "p (c e) -> p c e", c=KC)
        hn = kb(60, 8, "p (t f) -> p t f", t=TT)
        hnT = kb(110, 8, "p (c t) -> p c t", c=KC)
        xg = kb(48, 4, "p (c s) -> p c s", c=KC)
        glu = kb(52, 2)
        lin = kb(54, 2)
        sig = kb(104, 2)
        act_ = kb(106, 2)
        actT = kb(72, 2, "p (m h s) -> p m h s", m=4, h=2)
        yrow = kb(74, 4)
        sel = kb(78, 1, "p (t e s) -> p t e s", t=TT, e=2)
        selg = kb(79, 1, "p (t e s) -> p t e s", t=TT, e=2)
        selgT = kb(108, 1, "p (t n) -> p t n", t=TT)
        gatesT = kb(109, 1)
        outrow = kb(110, 8, "p (t f) -> p t f", t=TT)

        def slot(s):
            return ring[:, s * SLOT:(s + 1) * SLOT]

        slot_full = [sem(f"slot_full{s}") for s in range(RING)]
        slots_used = sem("slots_used")
        x_loaded = [sem("x_loaded0"), sem("x_loaded1")]
        mem_loaded, prm_loaded, ident_loaded, cst_loaded = sem("mem_loaded"), sem("prm_loaded"), sem("ident_loaded"), sem("cst_loaded")
        lora_loaded, sink_loaded, late_loaded = sem("lora_loaded"), sem("sink_loaded"), sem("late_loaded")
        b1_full = [sem("b1_full0"), sem("b1_full1")]
        root, root_m, scaled, scaled_m, prm_sb = sem("root"), sem("root_m"), sem("scaled"), sem("scaled_m"), sem("prm_sb")
        xT_ps, memT_ps, xT_sb, memT_sb = sem("xT_ps"), sem("memT_ps"), sem("xT_sb"), sem("memT_sb")
        rwkv_ps, raw_sb, lora_in, shifted, lora_act = sem("rwkv_ps"), sem("raw_sb"), sem("lora_in"), sem("shifted"), sem("lora_act")
        rest_ps, rest_sb, kv_ps, kv_sb = sem("rest_ps"), sem("rest_sb"), sem("kv_ps"), sem("kv_sb")
        zw_ps, za_ps, g_ps, rate_sb, a_sb, g_sb = sem("zw_ps"), sem("za_ps"), sem("g_ps"), sem("rate_sb"), sem("a_sb"), sem("g_sb")
        kk_sq, kk_ps, kk_clamped, kk_root = sem("kk_sq"), sem("kk_ps"), sem("kk_clamped"), sem("kk_root")
        csum_sb, powers_sb, tilde_sb, rk_sb, rk_ps, bonus_sb = (sem("csum_sb"), sem("powers_sb"), sem("tilde_sb"),
                                                               sem("rk_sb"), sem("rk_ps"), sem("bonus_sb"))
        score_ps, score_sb, negmax, expd, normed, pT_ps, pT_sb, pv_ps, pv_sb = (
            sem("score_ps"), sem("score_sb"), sem("negmax"), sem("expd"), sem("normed"), sem("pT_ps"), sem("pT_sb"),
            sem("pv_ps"), sem("pv_sb"))
        svT_ps, sv_sb = sem("svT_ps"), sem("sv_sb")
        tok_ps, tok_sb = sem("tok_ps"), sem("tok_sb")
        gram_ps, gram_sb, level0_sb, turned_ps, invT_sb, inv_sb, t1_ps, t1_sb, xx_ps = (
            sem("gram_ps"), sem("gram_sb"), sem("level0_sb"), sem("turned_ps"), sem("invT_sb"),
                                                              sem("inv_sb"), sem("t1_ps"), sem("t1_sb"), sem("xx_ps"))
        av_ps, av_sb, zeroed, r_ps, r_sb, u_ps, u_sb, s_ps, s_sb, yh_ps = (
            sem("av_ps"), sem("av_sb"), sem("zeroed"), sem("r_ps"), sem("r_sb"), sem("u_ps"), sem("u_sb"),
            sem("s_ps"), sem("s_sb"), sem("yh_ps"))
        yh_sb, mean_ps, yc_sb, var_ps, var_root, y_rwkv_sb = (sem("yh_sb"), sem("mean_ps"), sem("yc_sb"), sem("var_ps"),
                                                              sem("var_root"), sem("y_rwkv_sb"))
        gate_ps, gate_sb, branch_ps, merged_sb, out_ps, resid = (sem("gate_ps"), sem("gate_sb"), sem("branch_ps"),
                                                                 sem("merged_sb"), sem("out_ps"), sem("resid"))
        ffn_ss, ffn_root, hn_sb, hnT_ps, hnT_sb, logit_ps = (sem("ffn_ss"), sem("ffn_root"), sem("hn_sb"), sem("hnT_ps"),
                                                             sem("hnT_sb"), sem("logit_ps"))
        top_sb, top_exp, chosen_sb, rank_ps, gates_sb, gT_ps, gT_sb, b2_ps, route_done = (
            sem("top_sb"), sem("top_exp"), sem("chosen_sb"), sem("rank_ps"), sem("gates_sb"), sem("gT_ps"), sem("gT_sb"),
            sem("b2_ps"), sem("route_done"))
        b2_sb = sem("b2_sb")
        sel_sb, xg_ps, xg_sb, up_ps, up_read, glu_sb, sig_sb, prod_sb, act_sb = (
            sem("sel_sb"), sem("xg_ps"), sem("xg_sb"), sem("up_ps"), sem("up_read"), sem("glu_sb"), sem("sig_sb"),
            sem("prod_sb"), sem("act_sb"))
        actT_ps, actT_sb, down_ps, yrow_sb, selg_raw, selg_sb, selgT_ps, selgT_sb, sc_ps, acc_sb = (
            sem("actT_ps"), sem("actT_sb"), sem("down_ps"), sem("yrow_sb"), sem("selg_raw"), sem("selg_sb"),
            sem("selgT_ps"), sem("selgT_sb"), sem("sc_ps"), sem("acc_sb"))
        moe_done, fin_ss, fin_root, final_sb, stored = (sem("moe_done"), sem("fin_ss"), sem("fin_root"), sem("final_sb"),
                                                        sem("stored"))
        dve_step, act_step = sem("dve_step"), sem("act_step")

        block = ctx.enter_context(nc.Block())

        def w1_place(c, E, zero):
            if zero:
                return c, E + 1, E * CPE + c
            return (c - 4) % RING, E + (0 if c < 4 else 1), E * CPE + (c - 4)

        def w2_place(i, E, final):
            if final:
                return i + 8, E + 1, E * CPE + (i + 8)
            return i + 4, E + 2, E * CPE + (i + 16)

        def rows(w):
            return w.rearrange("(c p) f -> p c f", p=P)

        @block.sync
        def _(sp):
            for t in range(TT):
                sp.dma_start(xrows[:, t, :], x[0, t * P:(t + 1) * P, :]).then_inc(x_loaded[t], 16)
            sp.dma_start(prm[:], params).then_inc(prm_loaded, 16)
            sp.dma_start(cst[:, 0:2 * P], consts[:, 0:2 * P]).then_inc(ident_loaded, 16)
            w_in_r = rows(w_in[0])
            kv_r = rows(w_mem_kv[0])
            out_r = rows(w_out[0])
            for n, (name, c) in enumerate(order):
                s = slots[n]
                if previous[n] is not None:
                    sp.wait_ge(slots_used, previous[n] + 1)
                elif s >= HALF:
                    sp.wait_ge(y_rwkv_sb, 1)
                wide = slot(s).rearrange("p (c f) -> p c f", c=2)
                if name == "in_rwkv":
                    dst, src = slot(s)[:, 0:C_RWKV], w_in_r[:, c, 0:C_RWKV]
                elif name == "in_rest":
                    dst, src = slot(s)[:, 0:C_REST], w_in_r[:, c, C_RWKV:C_RWKV + C_REST]
                elif name == "mem_kv":
                    dst, src = wide, kv_r[:, 2 * c:2 * c + 2, :]
                elif name == "gate":
                    dst = slot(s).rearrange("p (c f) -> p c f", c=KC)
                    src = rows(w_gate[0, c[0]])[:, :, c[1] * 256:(c[1] + 1) * 256]
                elif name == "branch":
                    dst = slot(s).rearrange("p (c f) -> p c f", c=4)
                    src = rows(w_branch[0, c[0]])[:, :, c[1] * 512:(c[1] + 1) * 512]
                else:
                    dst, src = wide, out_r[:, 2 * c:2 * c + 2, :]
                sp.dma_start(dst, src).then_inc(slot_full[s], 16)
                if n == 2:
                    sp.dma_start(memrows, mem[0].rearrange("(t p) d -> p t d", p=P)).then_inc(mem_loaded, 16)
                if n == 3:
                    sp.dma_start(cst[:, 2 * P:], consts[:, 2 * P:]).then_inc(cst_loaded, 16)
                    sp.dma_start(lora[0:64, :], rwkv_w2[0]).then_inc(lora_loaded, 16)
                    sp.dma_start(lora[64:P, :], rwkv_a2[0]).then_inc(lora_loaded, 16)
                    sp.dma_start(gate2[:], rwkv_g2[0]).then_inc(lora_loaded, 16)
                    sp.dma_start(sinks[:], swa_sinks.to_broadcast([P, 8])).then_inc(sink_loaded, 16)
            sp.dma_start(ffnw, ffn_norm_w.to_broadcast([P, D])).then_inc(late_loaded, 16)
            sp.dma_start(finw, final_norm_w.unsqueeze(0).to_broadcast([P, D])).then_inc(late_loaded, 16)
            sp.dma_start(b2rows[0:NE, :], b_exp2[0]).then_inc(late_loaded, 16)
            sp.dma_start(wrt, w_router[0].rearrange("(c p) e -> p c e", p=P)).then_inc(late_loaded, 16)
            sp.dma_start(brt[:], b_router.to_broadcast([P, NE])).then_inc(late_loaded, 16)

            def load_w1(e, E, parity, zero=False):
                for c in range(KC):
                    s, _, n = w1_place(c, E, zero)
                    sp.wait_ge(slots_used, n + (NMIX - RING + 1))
                    if c == 0:
                        sp.dma_start(b1row[0:1, parity, :], b_exp1[0, bass.ds(e, 1), :]).then_inc(b1_full[parity], 16)
                    sp.dma_start(slot(s), w_exp1[0, bass.ds(e, 1), c * P:(c + 1) * P, :].rearrange("a p f -> p (a f)"))\
                      .then_inc(slot_full[s], 16)

            def load_w2(e, E, final=False):
                for i in range(4):
                    s, _, n = w2_place(i, E, final)
                    sp.wait_ge(slots_used, n + (NMIX - RING + 1))
                    sp.dma_start(slot(s).rearrange("p (c f) -> p c f", c=2),
                                 w_exp2[0, bass.ds(e, 1), 2 * i * P:(2 * i + 2) * P, :].rearrange("a (c p) f -> p (a c) f", p=P))\
                      .then_inc(slot_full[s], 16)

            def load_pass(q):
                E = q * NE
                load_w1(0, E, 0, True)
                with sp.Fori(0, NPAIR - 1) as k:
                    load_w1(k * 2 + 1, E + k * 2 + 1, 1)
                    load_w2(k * 2, E + k * 2)
                    load_w1(k * 2 + 2, E + k * 2 + 2, 0)
                    load_w2(k * 2 + 1, E + k * 2 + 1)
                load_w1(NE - 1, E + NE - 1, 1)
                load_w2(NE - 2, E + NE - 2)
                load_w2(NE - 1, E + NE - 1, True)

            load_pass(0)
            sp.wait_ge(route_done, 1)
            most = sp.value_load(cnti[0:1, 0:1], min_val=0, max_val=T)
            with sp.If(most > SLOTS):
                with sp.Fori(1, PASSES) as q:
                    load_pass(q)
            sp.wait_ge(final_sb, 1)
            sp.dma_start(out[0].rearrange("(t p) d -> p t d", p=P)[:, 0, :], outrow[:, 0, :]).then_inc(stored, 16)
            sp.wait_ge(final_sb, 2)
            sp.dma_start(out[0].rearrange("(t p) d -> p t d", p=P)[:, 1, :], outrow[:, 1, :]).then_inc(stored, 16)
            sp.wait_ge(stored, 32)

        @block.tensor
        def _(pe):
            def mm(o, l, r, start=True, stop=True):
                return pe.matmul(o, l, r, start=start, stop=stop, skip_group_check=True)

            def half(bank, n):
                return ps[:, bank + n // 2, (n % 2) * T:(n % 2) * T + T]

            def take(name, c):
                n = index[(name, c)]
                pe.wait_ge(slot_full[slots[n]], 16 * (past[n] + 1))
                return slot(slots[n])

            pe.wait_ge(ident_loaded, 16)
            for t in range(TT):
                pe.wait_ge(scaled, t + 1)
                for c in range(KC):
                    last = pe.transpose(half(0, c)[:, t * P:(t + 1) * P], xscaled[:, t, c * P:(c + 1) * P], ident)
                    if t == 1 and c % 2:
                        last.then_inc(xT_ps, 1)

            for c in range(KC):
                w = take("in_rwkv", c)
                for f in range(N_RWKV):
                    if c == 0 and f in (0, 2, 4, 6):
                        pe.wait_ge(xT_sb, f + 2)
                    last = mm(half(0, f), w[:, f * P:(f + 1) * P], xT[:, c, :], c == 0 and f % 2 == 0, c == KC - 1)
                last.then_inc(slots_used if c < KC - 1 else rwkv_ps, 1)

            def low_rank(c):
                if c == 1:
                    pe.wait_ge(raw_sb, 7)
                    pe.wait_ge(lora_loaded, 48)
                    pe.wait_ge(lora_act, 1)
                    for f in range(HP):
                        last = mm(half(5, f), lora[0:64, f * P:(f + 1) * P], proj[0:64, 12, :], f % 2 == 0)
                    last.then_inc(zw_ps, 1)
                elif c == 2:
                    pe.wait_ge(rate_sb, 1)
                    for f in range(HP):
                        last = mm(half(7 - f // 2 * 2, f % 2), lora[64:P, f * P:(f + 1) * P], proj[64:P, 12, :], f % 2 == 0)
                    last.then_inc(za_ps, 1)
                elif c == 3:
                    pe.wait_ge(lora_act, 2)
                    pe.wait_ge(a_sb, 1)
                    for f in range(HP):
                        last = mm(half(6, f), gate2[:, f * P:(f + 1) * P], proj[:, 13, :], f % 2 == 0)
                    last.then_inc(g_ps, 1)
                elif c == 4:
                    pe.wait_ge(g_sb, 1)
                    pe.wait_ge(kk_sq, 1)
                    for b in range(2):
                        last = mm(ps[:, 5 + b, :], heads, csum[:, 2 * b:2 * b + 2, :])
                    last.then_inc(kk_ps, 1)
                elif c in (5, 6):
                    pe.wait_ge(kk_clamped, 1)
                    if c == 5:
                        pe.wait_ge(scaled_m, 2)
                    else:
                        pe.wait_ge(memT_sb, 4)
                    for i in range(4):
                        k = 4 * (c - 5) + i
                        dst = half(7 - i // 2 * 2, i % 2) if c == 5 else half(6, i)
                        for t in range(TT):
                            last = pe.transpose(dst[:, t * P:(t + 1) * P], memrows[:, t, k * P:(k + 1) * P], ident)
                    last.then_inc(memT_ps, 1)

            for c in range(KC):
                w = take("in_rest", c)
                for f in range(10):
                    if c == 0 and f % 2 == 0:
                        pe.wait_ge(raw_sb, f // 2 + 2)
                    last = mm(half(0, f), w[:, f * P:(f + 1) * P], xT[:, c, :], c == 0 and f % 2 == 0, c == KC - 1)
                    if c == 0 and f == 0:
                        last.then_inc(slots_used, 1)
                last.then_inc(slots_used if c < KC - 1 else rest_ps, 1)
                low_rank(c)

            def mem_kv(first, end):
                for k in range(first, end):
                    c, cc = k // 2, k % 2
                    w = take("mem_kv", c)
                    for f in range(4):
                        mm(half(5, f), w[:, cc * D + f * P:cc * D + (f + 1) * P], memT[:, k, :], k == 0 and f % 2 == 0, k == KC - 1)
                    for t in range(TT):
                        last = mm(ps[:, (7 + t) % 8, :], memT[:, k, t * P:(t + 1) * P], w[:, cc * D + 512:cc * D + D],
                                  k == 0, k == KC - 1)
                    if cc:
                        last.then_inc(slots_used if k < KC - 1 else kv_ps, 1)

            pe.wait_ge(memT_sb, 8)
            pe.wait_ge(rest_sb, 7)
            for t in range(TT):
                last = pe.transpose(ps[:, 1, t * P:(t + 1) * P], svT[:, t * P:(t + 1) * P], ident)
                last.then_inc(slots_used if t == 0 else svT_ps, 1)
            pe.wait_ge(rest_sb, 11)
            for h in range(8):
                b = 64 * (h % 2)
                last = mm(ps[:, 3 + h % 2, (h // 2) * P:(h // 2 + 1) * P], sq_[b:b + 64, h // 2, 0:P],
                          skd[b:b + 64, h // 4, 0:P], h < 2)
            last.then_inc(score_ps, 1)
            mem_kv(0, 3)
            pe.wait_ge(normed, 1)
            pe.wait_ge(sv_sb, 1)
            for h in range(8):
                last = pe.transpose(ps[:, 1 + h // 4, (h % 4) * P:(h % 4 + 1) * P],
                                    probs[:, ((h % 2) * 4 + h // 2) * P:((h % 2) * 4 + h // 2 + 1) * P], ident)
            last.then_inc(pT_ps, 1)
            mem_kv(3, 4)
            pe.wait_ge(pT_sb, 2)
            for h in range(8):
                b = 64 * (h % 2)
                last = mm(ps[b:b + 64, 3, (h // 2) * P:(h // 2 + 1) * P], sv[:, 0, (h // 4) * 64:(h // 4) * 64 + 64],
                          probsT[:, h * P:(h + 1) * P], h < 2)
            last.then_inc(pv_ps, 1)
            for h in (0, 2, 4, 6, 1, 3, 5, 7):
                b = 64 * (h % 2)
                bank = 1 + h // 4 if h % 2 == 0 else 4 - h // 4
                if h == 5:
                    pe.wait_ge(pv_sb, 1)
                last = mm(ps[:, bank, (h // 2 % 2) * T:(h // 2 % 2 + 1) * T], sq_[b:b + 64, h // 2, P:T],
                          skd[b:b + 64, h // 4, :], h // 2 % 2 == 0)
            last.then_inc(score_ps, 1)
            mem_kv(4, 7)
            pe.wait_ge(normed, 2)
            for h in range(8):
                for m in range(2):
                    at = ((h % 2) * 4 + h // 2) * T + m * P
                    last = pe.transpose(ps[:, 1 + h // 2, (h % 2) * T + m * P:(h % 2) * T + (m + 1) * P],
                                        probs[:, at:at + P], ident)
            last.then_inc(pT_ps, 1)
            mem_kv(7, 8)
            pe.wait_ge(pT_sb, 6)
            for h in range(8):
                b = 64 * (h % 2)
                for m in range(2):
                    last = mm(ps[b:b + 64, 1, (h // 2) * P:(h // 2 + 1) * P], sv[:, m, (h // 4) * 64:(h // 4) * 64 + 64],
                              probsT[:, (2 * h + m) * P:(2 * h + m + 1) * P], h < 2 and m == 0, m == 1)
                    if h == 0 and m == 0:
                        last.then_inc(slots_used, 1)
            last.then_inc(pv_ps, 1)

            pe.wait_ge(kv_sb, 4)
            for n in range(TT):
                for h in range(4):
                    last = mm(half(2 + 3 * n, h), mq[:, h, n * P:(n + 1) * P], kmT[:, h, :], h % 2 == 0)
                last.then_inc(score_ps, 1)
            pe.wait_ge(tilde_sb, 1)
            for i, (src, banks) in enumerate(((bT, (7, 0)), (kT, (1, 4)), (proj[:, 8:12, :], (7, 0)))):
                if i == 1:
                    pe.wait_ge(pv_sb, 2)
                elif i == 2:
                    pe.wait_ge(tok_sb, 2)
                for t in range(TT):
                    for c in range(HP):
                        last = pe.transpose(ps[:, banks[t], c * P:(c + 1) * P], src[:, c, t * P:(t + 1) * P], ident)
                    last.then_inc(tok_ps, 1)
            pe.wait_ge(tok_sb, 4)
            pe.wait_ge(rk_sb, 1)
            for b in range(2):
                last = mm(ps[:, 1 + 3 * b, :], heads, kkn[:, 2 * b:2 * b + 2, :])
            last.then_inc(rk_ps, 1)
            pm = mprobs.rearrange("p (n h m) -> p n h m", n=2, h=4)
            pmT = mprobsT.rearrange("p (n h m q) -> p n h m q", n=2, h=4, m=2)
            for n in range(TT):
                pe.wait_ge(normed, n + 3)
                for h in range(4):
                    for m in range(2):
                        last = pe.transpose(ps[:, 2 + 3 * n + h // 2, (h % 2) * T + m * P:(h % 2) * T + (m + 1) * P],
                                            pm[:, n, h, m * P:(m + 1) * P], ident)
                last.then_inc(pT_ps, 1)
            pe.wait_ge(tok_sb, 6)
            for n in range(TT):
                pe.wait_ge(pT_sb, 2 * n + 8)
                for h in range(4):
                    for m in range(2):
                        last = mm(ps[:, (7 + n) % 8, h * P:(h + 1) * P], vm[:, m, h * P:(h + 1) * P], pmT[:, n, h, m, :],
                                  h == 0 and m == 0, m == 1)
                last.then_inc(pv_ps, 1)
            pe.wait_ge(bonus_sb, 1)
            pe.wait_ge(cst_loaded, 16)
            def turn_inverse(j, g):
                m = 4 * j + g
                if j == 0:
                    pe.wait_ge(level0_sb, g + 1)
                else:
                    pe.wait_ge(inv_sb, m + 1)
                if m >= 6:
                    pe.wait_ge(invT_sb, m - 5)
                elif m >= 2:
                    pe.wait_ge(inv_sb, m - 1)
                for i in range(4):
                    last = pe.transpose(ps[:, 6 + g % 2, i * P:(i + 1) * P], (inv if j else invT)[:, 4 * g + i, :], ident)
                last.then_inc(turned_ps, 1)

            pe.wait_ge(pv_sb, 4)
            for g in range(4):
                t, par = g // 2, g % 2
                b = 64 * par
                for i in range(4):
                    n = 4 * g + i
                    if n >= 6:
                        pe.wait_ge(gram_sb, n - 5)
                    ts = slice(t * P, (t + 1) * P)
                    mm(ps[:, n % 6, 0:T], bT[b:b + 64, i, ts], ar[b:b + 64, i, :, ts])
                    mm(ps[:, n % 6, T:2 * T], kT[b:b + 64, i, ts], ar[b:b + 64, i, :, ts], False).then_inc(gram_ps, 1)
                if g:
                    turn_inverse(0, g - 1)
            for j in range(1, LEVELS):
                late = {0: 3} if j == 1 else {0: 2, 1: 3}
                for g in range(4):
                    pe.wait_ge(inv_sb, 4 * (j - 1) + g + 1)
                    if j == 1:
                        pe.wait_ge(gram_sb, 16)
                    for i in range(4):
                        u = 4 * g + i
                        last = mm(ps[:, g, i * P:(i + 1) * P], gram[:, u, 0, :], inv[:, u, :], i == 0)
                    last.then_inc(t1_ps, 1)
                    if g in late:
                        turn_inverse(j - 1, late[g])
                for g in range(4):
                    n = 4 * (j - 1) + g
                    pe.wait_ge(t1_sb, n + 1)
                    if n >= 2:
                        pe.wait_ge(inv_sb, 4 + n - 1)
                    if j > 1:
                        pe.wait_ge(invT_sb, n - 3)
                    for i in range(4):
                        u = 4 * g + i
                        if j < LEVELS - 1:
                            last = mm(ps[:, 4 + g % 2, i * P:(i + 1) * P], invT[:, u, :], t1s[:, g, i, :], i == 0)
                        else:
                            last = mm(ps[:, 4 + g % 2, i * P:(i + 1) * P], t1s[:, g, i, :], invT[:, u, :], i == 0)
                    last.then_inc(xx_ps, 1)
                    if g >= 2 and j < LEVELS - 1:
                        turn_inverse(j, g - 2)
            pe.wait_ge(inv_sb, 4 * LEVELS)
            for t in range(TT):
                for h in range(HR):
                    last = mm(ps[:, 4 + 2 * t + h // 4, (h % 4) * P:(h % 4 + 1) * P],
                              gram[:, t * 8 + (h % 2) * 4 + h // 2, 2, :], vtok[:, t, (h // 2) * P:(h // 2 + 1) * P], h % 4 == 0)
                last.then_inc(av_ps, 1)
            pe.wait_ge(zeroed, 3)
            pe.wait_ge(av_sb, 4)

            def piece(p):
                m, r = p // PIECES, p % PIECES
                b, f = UNITS[m]
                if r < 4:
                    if r == 0 and m:
                        pe.wait_ge(gate_sb, m)
                    w = take("gate", (b, f))
                    for k in (2 * r, 2 * r + 1):
                        for ff in range(2):
                            last = mm(half(6, ff), w[:, k * 256 + ff * P:k * 256 + (ff + 1) * P], xT[:, k, :],
                                      k == 0 and ff == 0, k == KC - 1)
                            if k == 0 and ff == 0 and m and m % 2 == 0:
                                last.then_inc(slots_used, 1)
                    if r == 3:
                        last.then_inc(gate_ps, 1)
                else:
                    if r == 4 and m:
                        pe.wait_ge(merged_sb, m)
                    w = take("branch", (b, f // 2))
                    for k in (2 * (r - 4), 2 * (r - 4) + 1):
                        for ff in range(2):
                            at = k * 512 + (f % 2) * 256 + ff * P
                            last = mm(half(7, ff), w[:, at:at + P], (gT, y_swa, y_mem)[b][:, k, :], k == 0 and ff == 0, k == 3)
                            if k == 0 and ff == 0:
                                last.then_inc(slots_used, 1)
                    if r == 5:
                        last.then_inc(branch_ps, 1)

            points = fill_points()

            def fill(point):
                for p in points[point]:
                    piece(p)

            for ch in range(NCH):
                t, c = ch // 2, ch % 2
                rs = slice(64 * c, 64 * c + 64)
                toks = slice(ch * CH, (ch + 1) * CH)
                if ch:
                    pe.wait_ge(s_sb, ch)
                for hp in range(HP):
                    last = mm(ps[rs, 0, hp * P:(hp + 1) * P], ar[:, hp, 0, toks], state[:, ch % 2, hp, :], hp == 0)
                last.then_inc(r_ps, 1)
                for hp in range(HP):
                    mm(ps[:, 3, hp * P:(hp + 1) * P], ktok[rs, t, hp * P:(hp + 1) * P], vtok[rs, t, hp * P:(hp + 1) * P], hp == 0)
                for hp in range(HP):
                    mm(ps[:, 4 + t, hp * P + c * CH:hp * P + (c + 1) * CH], state[:, ch % 2, hp, :], ar[:, hp, 1, toks],
                       c == 0 and hp == 0)
                fill((ch, "a"))
                pe.wait_ge(r_sb, ch + 1)
                for h in range(HR):
                    last = mm(ps[rs, 1 + h // 4, (h % 4) * P:(h % 4 + 1) * P], invT[:, t * 8 + (h % 2) * 4 + h // 2, rs],
                              rs_[:, (h // 2) * P:(h // 2 + 1) * P], h % 4 == 0)
                last.then_inc(u_ps, 1)
                fill((ch, "b"))
                pe.wait_ge(u_sb, ch + 1)
                for hp in range(HP):
                    last = mm(ps[:, 3, hp * P:(hp + 1) * P], btok[rs, t, hp * P:(hp + 1) * P], us[rs, t, hp * P:(hp + 1) * P], False)
                last.then_inc(s_ps, 1)
                fill((ch, "c"))
                if c == 1:
                    for h in range(HR):
                        u = t * 8 + (h % 2) * 4 + h // 2
                        o = ps[64 * (h % 2):64 * (h % 2) + 64, 4 + t, (h // 2) * P:(h // 2 + 1) * P]
                        mm(o, vtok[:, t, h * 64:(h + 1) * 64], gram[:, u, 3, :], False)
                        last = mm(o, us[:, t, h * 64:(h + 1) * 64], gram[:, u, 1, :], False)
                    last.then_inc(yh_ps, 1)
            fill("mean")
            pe.wait_ge(yh_sb, 1)
            for b in range(2):
                last = mm(ps[:, b, :], heads, yT[:, 2 * b:2 * b + 2, :])
            last.then_inc(mean_ps, 1)
            fill("var")
            pe.wait_ge(yc_sb, 2)
            for b in range(2):
                last = mm(ps[:, b, :], heads, sqr[:, 2 * b:2 * b + 2, :])
            last.then_inc(var_ps, 1)
            fill("rest")
            pe.wait_ge(y_rwkv_sb, 1)
            for p in range(PIECES * N_FILL, PIECES * len(UNITS)):
                piece(p)
            for t in range(TT):
                for k in range(KC):
                    w = take("out", k // 2)
                    if t == 0 and k % 2 == 0:
                        pe.wait_ge(merged_sb, N_FILL + k // 2 + 1)
                    for n in range(2):
                        last = mm(ps[:, 2 * t + n, :], mergedT[:, k, t * P:(t + 1) * P],
                                  w[:, (k % 2) * D + n * 512:(k % 2) * D + (n + 1) * 512], k == 0, k == KC - 1)
                        if t == 0 and k == 0 and n == 0:
                            last.then_inc(slots_used, 1)
                    if t == 1 and k % 2 and k < KC - 1:
                        last.then_inc(slots_used, 1)
                last.then_inc(out_ps, 1)
            pe.wait_ge(out_ps, 2)
            pe.sem_inc(slots_used, 1)
            pe.wait_ge(late_loaded, 16 * 5)
            for t in range(TT):
                pe.wait_ge(hn_sb, t + 1)
                for c in range(KC):
                    last = pe.transpose(ps[:, 4 + 2 * t + c // 4, (c % 4) * P:(c % 4 + 1) * P], hn[:, t, c * P:(c + 1) * P], ident)
                    if c % 4 == 3:
                        last.then_inc(hnT_ps, 1)
                for c in range(KC):
                    if c % 4 == 0:
                        pe.wait_ge(hnT_sb, 2 * t + c // 4 + 1)
                    last = mm(ps[:, 0, t * NE:(t + 1) * NE], hnT[:, c, t * P:(t + 1) * P], wrt[:, c, :], t == 0 and c == 0, c == KC - 1)
            last.then_inc(logit_ps, 1)
            pe.wait_ge(chosen_sb, 1)
            before = const("before")
            mm(ps[:, 1, 0:NE], before, chosen[:, 0, :])
            mm(ps[:, 1, NE:2 * NE], ones, chosen[:, 0, :], False)
            mm(ps[:, 1, NE:2 * NE], before, chosen[:, 1, :], False).then_inc(rank_ps, 1)
            mm(ps[:, 2, 0:NE], ones, chosen[:, 0, :])
            mm(ps[:, 2, 0:NE], ones, chosen[:, 1, :], False).then_inc(rank_ps, 1)

            def gather(N):
                pe.wait_ge(sel_sb, N + 1)
                for c in range(KC):
                    for t in range(TT):
                        last = mm(ps[:, 4 + c // 4, (c % 4) * P:(c % 4 + 1) * P], hn[:, t, c * P:(c + 1) * P],
                                  sel[:, t, :, :], c % 4 == 0 and t == 0, t == 1)
                last.then_inc(xg_ps, 1)

            def up(E, N, parity, between, zero=False):
                pe.wait_ge(b1_full[parity], (N + 1) * 16)
                if parity == 0:
                    pe.wait_ge(xg_sb, N * 2 + 2)
                for z in range(2):
                    for hf in range(2):
                        mm(ps[64 * hf:64 * hf + 64, z, :], ones[0:1, 0:SLOTS],
                           b1row[0:1, parity, hf * D + z:(hf + 1) * D:2], True, False)
                for c in range(KC):
                    s, times, n = w1_place(c, E, zero)
                    pe.wait_ge(slot_full[s], times * 16 + 16 * uses[s])
                    for z in range(2):
                        for hf in range(2):
                            last = mm(ps[64 * hf:64 * hf + 64, z, :], xg[:, c, parity * SLOTS:(parity + 1) * SLOTS],
                                      slot(s)[:, hf * D + z:(hf + 1) * D:2], False, c == KC - 1)
                    last.then_inc(slots_used, 1)
                    if between:
                        between(c)
                pe.wait_ge(slots_used, n + (NMIX + 1))
                pe.sem_inc(up_ps, 1)

            def down(E, final=False):
                pe.wait_ge(actT_sb, E + 1)
                for i in range(4):
                    s, times, n = w2_place(i, E, final)
                    pe.wait_ge(slot_full[s], times * 16 + 16 * uses[s])
                    for cc in range(2):
                        k = 2 * i + cc
                        for dh in range(2):
                            last = mm(ps[64 * dh:64 * dh + 64, 3, :], actT[:, k % 4, k // 4, :],
                                      slot(s)[:, cc * D + dh * 512:cc * D + (dh + 1) * 512], k == 0, k == 7)
                    last.then_inc(slots_used, 1)
                pe.wait_ge(slots_used, n + (NMIX + 1))
                pe.sem_inc(down_ps, 1)

            def turn(E):
                pe.wait_ge(act_sb, E + 1)
                for m in range(4):
                    last = pe.transpose(ps[:, 2, m * P:(m + 1) * P], act_[:, m * P:(m + 1) * P], ident)
                last.then_inc(actT_ps, 1)

            def turn_gates(N, first):
                pe.wait_ge(selg_sb, N + 1)
                if first:
                    pe.wait_ge(b2_sb, 2)
                else:
                    pe.wait_ge(acc_sb, N * 2)
                for t in range(TT):
                    last = pe.transpose(ps[:, 6, t * P:(t + 1) * P], selg[:, t, :, :].rearrange("p e s -> p (e s)"), ident)
                last.then_inc(selgT_ps, 1)

            def scatter(N, t, bank=6):
                if t == 0:
                    pe.wait_ge(selgT_sb, N + 1)
                    pe.wait_ge(yrow_sb, N * 4 + 4)
                elif bank == 6:
                    pe.wait_ge(acc_sb, N * 2 + 1)
                for n in range(2):
                    last = mm(ps[:, bank + n, :], selgT[:, t, :], yrow[:, n * 512:(n + 1) * 512])
                last.then_inc(sc_ps, 1)

            def second_bias(t):
                if t == 0:
                    pe.wait_ge(gT_sb, 1)
                else:
                    pe.wait_ge(b2_sb, 1)
                for n in range(2):
                    last = mm(ps[:, 6 + n, :], gatesT[0:NE, t * P:(t + 1) * P], b2rows[0:NE, n * 512:(n + 1) * 512])
                last.then_inc(b2_ps, 1)

            def pair(q, k, first, last, turn_wait=None):
                E, N = q * NE + k * 2, q * NPAIR + k
                very_first, second = turn_wait == "first", turn_wait == "second"
                if not very_first:
                    pe.wait_ge(up_read, E)
                up(E, N, 0, None, first)
                if not first:
                    down(E - 1)
                if very_first:
                    pe.wait_ge(gates_sb, 1)
                    for t in range(TT):
                        tr = pe.transpose(ps[0:NE, 3, t * P:(t + 1) * P], gates[:, t, :], ident)
                    tr.then_inc(gT_ps, 1)
                turn(E)
                if very_first:
                    second_bias(0)

                def between(c):
                    if first:
                        if very_first and c == 2:
                            second_bias(1)
                    elif c == 0:
                        turn_gates(N - 1, second)
                    elif c == 2:
                        scatter(N - 1, 0)
                    elif c == 5:
                        scatter(N - 1, 1)

                pe.wait_ge(up_read, E + 1)
                up(E + 1, N, 1, between)
                if not last:
                    gather(N + 1)
                down(E)
                turn(E + 1)

            def one_pass(q, very_first=False):
                N0 = q * NPAIR
                if not very_first:
                    pe.wait_ge(acc_sb, N0 * 2)
                gather(N0)
                if very_first:
                    pair(q, 0, True, False, "first")
                    pair(q, 1, False, False, "second")
                else:
                    pair(q, 0, True, False)
                with pe.Fori(2 if very_first else 1, NPAIR - 1) as k:
                    pair(q, k, False, False)
                pair(q, NPAIR - 1, False, True)
                turn_gates(N0 + NPAIR - 1, False)
                down(q * NE + NE - 1, True)
                scatter(N0 + NPAIR - 1, 0)
                scatter(N0 + NPAIR - 1, 1, 0)

            one_pass(0, True)
            pe.wait_ge(route_done, 1)
            most = pe.value_load(cnti[0:1, 0:1], min_val=0, max_val=T)
            with pe.If(most > SLOTS):
                with pe.Fori(1, PASSES) as q:
                    one_pass(q)

        @block.scalar
        def _(act):
            for t in range(TT):
                act.wait_ge(x_loaded[t], 16)
                act.activation(dump[:, t, :], xrows[:, t, :], ACT.Square, accum_out=ss[:, t:t + 1]).then_inc(act_step, 1)
            act.wait_ge(act_step, 2)
            act.wait_ge(zeroed, 2)
            act.activation(ss[:, 4:6], ss[:, 0:2], ACT.Sqrt, scale=1.0 / D, bias=epsc[:, 0:1]).then_inc(root, 1)
            act.wait_ge(mem_loaded, 16)
            for t in range(TT):
                act.activation(dump_m[:, t, :], memrows[:, t, :], ACT.Square, accum_out=ss[:, 2 + t:3 + t]).then_inc(act_step, 1)
            act.wait_ge(act_step, 4)
            act.activation(ss[:, 6:8], ss[:, 2:4], ACT.Sqrt, scale=1.0 / D, bias=epsc[:, 0:1]).then_inc(root_m, 1)
            act.wait_ge(rwkv_ps, 1)
            for b in (6, 0, 1, 2, 3, 4, 5):
                act.activation(raw[:, 2 * b:2 * b + 2, 1:T + 1], ps[:, b, :].rearrange("p (c t) -> p c t", c=2), ACT.Copy).then_inc(raw_sb, 1)
            act.wait_ge(lora_in, 1)
            act.activation(proj[0:64, 12, :], proj[0:64, 12, :], ACT.Tanh).then_inc(lora_act, 1)
            act.activation(proj[:, 13, :], proj[:, 13, :], ACT.Sigmoid).then_inc(lora_act, 1)
            act.wait_ge(zw_ps, 1)
            for f in range(HP):
                last = act.activation(pex[:, f, :], ps[:, 5 + f // 2, (f % 2) * T:(f % 2 + 1) * T], ACT.Sigmoid, bias=col("w0", f))
            last.then_inc(rate_sb, 1)
            act.wait_ge(shifted, 1)
            act.wait_ge(za_ps, 1)
            for f in range(HP):
                last = act.activation(rate_a[:, f, :], ps[:, 7 - f // 2 * 2, (f % 2) * T:(f % 2 + 1) * T], ACT.Sigmoid, bias=col("a0", f))
            last.then_inc(a_sb, 1)
            act.wait_ge(g_ps, 1)
            for b in range(2):
                last = act.activation(gT[:, 2 * b:2 * b + 2, :], ps[:, 6 + b, :].rearrange("p (c t) -> p c t", c=2), ACT.Copy)
            last.then_inc(g_sb, 1)
            act.wait_ge(kk_clamped, 1)
            act.activation(pinc, pinc, ACT.Sqrt).then_inc(kk_root, 1)
            for n in range(2):
                act.wait_ge(memT_ps, n + 1)
                for i in range(4):
                    bank = 7 - i // 2 * 2 if n == 0 else 6 + i // 2
                    act.activation(memT[:, 4 * n + i, :], ps[:, bank, (i % 2) * T:(i % 2 + 1) * T], ACT.Copy,
                                   scale=col("memn", 4 * n + i)).then_inc(memT_sb, 1)
            act.wait_ge(csum_sb, 1)
            act.activation(pinc, csum, ACT.Exp, scale=-EXP_HALF).then_inc(powers_sb, 1)
            act.activation(pinv, csum, ACT.Exp, scale=EXP_HALF).then_inc(powers_sb, 1)
            act.activation(pex, pex, ACT.Exp, scale=-EXP_HALF).then_inc(powers_sb, 1)
            act.wait_ge(rest_ps, 1)
            for f in range(4):
                act.activation(sq_[:, f, :], ps[:, f // 2, (f % 2) * T:(f % 2 + 1) * T], ACT.Identity, scale=SWA_SCALE,
                               bias=bq[:, f:f + 1]).then_inc(rest_sb, 1)
            act.activation(skd[0:64, 0, :], ps[0:64, 2, 0:T], ACT.Identity, bias=col("bswa", 4)[0:64]).then_inc(rest_sb, 1)
            act.activation(skd[64:P, 1, :], ps[64:P, 2, 0:T], ACT.Identity, bias=col("bswa", 4)[64:P]).then_inc(rest_sb, 1)
            act.activation(svT, ps[:, 2, T:2 * T], ACT.Identity, bias=col("bswa", 5)).then_inc(rest_sb, 1)
            act.wait_ge(rest_sb, 7)
            act.activation(skd[64:P, 0, :], skd[0:64, 0, :], ACT.Copy).then_inc(rest_sb, 1)
            act.activation(skd[0:64, 1, :], skd[64:P, 1, :], ACT.Copy).then_inc(rest_sb, 1)
            act.activation(mq[:, 0:2, :], ps[:, 3, :].rearrange("p (c t) -> p c t", c=2), ACT.Copy).then_inc(rest_sb, 1)
            act.activation(mq[:, 2:4, :], ps[:, 4, :].rearrange("p (c t) -> p c t", c=2), ACT.Copy).then_inc(rest_sb, 1)
            act.wait_ge(svT_ps, 1)
            act.activation(sv, ps[:, 1, 0:T].rearrange("p (t f) -> p t f", t=TT), ACT.Copy).then_inc(sv_sb, 1)
            act.wait_ge(sink_loaded, 16)
            for n in range(TT):
                W = P * (n + 1)
                act.wait_ge(negmax, n + 1)
                for h in range(8):
                    o = (h % 2) * 4 + h // 2
                    act.activation(probs[:, o * W:(o + 1) * W], probs[:, o * W:(o + 1) * W], ACT.Exp,
                                   bias=stat[:, 1, o:o + 1], accum_out=stat[:, 2, o:o + 1])
                act.activation(stat[:, 4, :], stat[:, 3, :], ACT.Exp).then_inc(expd, 1)
                act.wait_ge(pT_ps, n + 1)
                if n == 1:
                    act.wait_ge(pv_ps, 1)
                for b in range(2 * (n + 1)):
                    act.activation(probsT[:, b * 512:(b + 1) * 512], ps[:, 1 + b, :], ACT.Copy).then_inc(pT_sb, 1)
                if n == 0:
                    act.wait_ge(pv_ps, 1)
                    act.activation(y_swa[:, :, 0:P], ps[:, 3, :].rearrange("p (c t) -> p c t", c=4), ACT.Copy).then_inc(pv_sb, 1)
            act.wait_ge(kv_ps, 1)
            for b in range(2):
                act.activation(kmT[:, 2 * b:2 * b + 2, :], ps[:, 5 + b, :].rearrange("p (c t) -> p c t", c=2), ACT.Copy).then_inc(kv_sb, 1)
            for t in range(TT):
                act.activation(vm[:, t, :], ps[:, (7 + t) % 8, :], ACT.Copy).then_inc(kv_sb, 1)
            act.wait_ge(pv_ps, 2)
            act.activation(y_swa[:, :, P:T], ps[:, 1, :].rearrange("p (c t) -> p c t", c=4), ACT.Copy).then_inc(pv_sb, 1)
            pm = mprobs.rearrange("p (n h m) -> p n h m", n=2, h=4)
            for n in range(TT):
                act.wait_ge(negmax, n + 3)
                for h in range(4):
                    last = act.activation(pm[:, n, h, :], ps[:, 2 + 3 * n + h // 2, (h % 2) * T:(h % 2 + 1) * T], ACT.Exp,
                                          scale=MEM_SCALE, bias=stat[:, 1, 4 * n + h:4 * n + h + 1],
                                          accum_out=stat[:, 2, 4 * n + h:4 * n + h + 1])
                last.then_inc(expd, 1)
            for i, (dst, banks) in enumerate(((btok, (7, 0)), (ktok, (1, 4)), (vtok, (7, 0)))):
                for t in range(TT):
                    act.wait_ge(tok_ps, 2 * i + t + 1)
                    act.activation(dst[:, t, :], ps[:, banks[t], :], ACT.Copy).then_inc(tok_sb, 1)
            for n in range(TT):
                act.wait_ge(pT_ps, n + 3)
                for b in range(2):
                    act.activation(mprobsT[:, n * D + b * 512:n * D + (b + 1) * 512], ps[:, 2 + 3 * n + b, :], ACT.Copy).then_inc(pT_sb, 1)
            for n in range(TT):
                act.wait_ge(pv_ps, n + 3)
                act.activation(y_mem[:, :, n * P:(n + 1) * P], ps[:, (7 + n) % 8, :].rearrange("p (c t) -> p c t", c=4), ACT.Copy).then_inc(pv_sb, 1)

            for m in range(4 * (LEVELS - 1)):
                act.wait_ge(turned_ps, m + 1)
                us4 = slice(4 * (m % 4), 4 * (m % 4) + 4)
                act.activation((invT if m >= 4 else inv)[:, us4, :], ps[:, 6 + m % 2, :].rearrange("p (u t) -> p u t", u=4),
                               ACT.Copy).then_inc(invT_sb if m >= 4 else inv_sb, 1)

            def own_half(a):
                return a.rearrange("p (c q v) -> p c q v", q=4, v=64)[:, :, 0:4:3, :]

            for t in range(TT):
                act.wait_ge(av_ps, t + 1)
                for b in range(2):
                    act.activation(av[:, t, b * T:(b + 1) * T].rearrange("p (c a v) -> p c a v", a=2, v=64),
                                   own_half(ps[:, 4 + 2 * t + b, :]), ACT.Copy).then_inc(av_sb, 1)
            def gate(m):
                act.wait_ge(gate_ps, m + 1)
                if m >= 2:
                    act.wait_ge(merged_sb, m - 1)
                act.activation(gsig[:, m % 2, :], ps[:, 6, :], ACT.Sigmoid).then_inc(gate_sb, 1)

            points = fill_points()

            def gates_of(point):
                for p in points[point]:
                    if p % PIECES == 3:
                        gate(p // PIECES)

            for ch in range(NCH):
                rs = slice(64 * (ch % 2), 64 * (ch % 2) + 64)
                act.wait_ge(u_ps, ch + 1)
                for b in range(2):
                    last = act.activation(us[rs, ch // 2, b * T:(b + 1) * T].rearrange("p (c a v) -> p c a v", a=2, v=64),
                                          own_half(ps[rs, 1 + b, :]), ACT.Copy)
                last.then_inc(u_sb, 1)
                for s in "abc":
                    gates_of((ch, s))
            gates_of("mean")
            gates_of("var")
            act.wait_ge(var_ps, 1)
            for b in range(2):
                last = act.activation(sqr[:, 2 * b:2 * b + 2, :], ps[:, b, :].rearrange("p (c t) -> p c t", c=2), ACT.Sqrt,
                                      scale=1.0 / 64, bias=epsc[:, 1:2])
            last.then_inc(var_root, 1)
            gates_of("rest")
            for m in range(N_FILL, len(UNITS)):
                gate(m)
            for t in range(TT):
                act.wait_ge(resid, t + 1)
                act.activation(hnT.rearrange("p c t -> p (c t)")[:, t * D:(t + 1) * D], xrows[:, t, :], ACT.Square,
                               accum_out=ss[:, t:t + 1]).then_inc(ffn_ss, 1)
                act.wait_ge(ffn_ss, t + 1)
                act.activation(ss[:, 4 + t:5 + t], ss[:, t:t + 1], ACT.Sqrt, scale=1.0 / D, bias=epsc[:, 0:1]).then_inc(ffn_root, 1)
            for t in range(TT):
                for b in range(2):
                    act.wait_ge(hnT_ps, 2 * t + b + 1)
                    act.activation(hnT[:, 4 * b:4 * b + 4, t * P:(t + 1) * P], ps[:, 4 + 2 * t + b, :].rearrange("p (c t) -> p c t", c=4),
                                   ACT.Copy).then_inc(hnT_sb, 1)
            act.wait_ge(top_sb, 1)
            for t in range(TT):
                last = act.activation(gates[:, t, :], logit[:, t, :], ACT.Exp, bias=rtmp[:, t, 0:1])
            last.then_inc(top_exp, 1)

            def gathered(N):
                act.wait_ge(xg_ps, N + 1)
                for b in range(2):
                    act.activation(xg[:, 4 * b:4 * b + 4, :], ps[:, 4 + b, :].rearrange("p (c s) -> p c s", c=4), ACT.Copy).then_inc(xg_sb, 1)

            def sigmoid(E):
                act.wait_ge(glu_sb, E + 1)
                act.activation(sig, glu, ACT.Sigmoid, scale=ALPHA).then_inc(sig_sb, 1)

            def downed(E, parity):
                act.wait_ge(down_ps, E + 1)
                for dh in range(2):
                    act.activation(yrow[64 * parity:64 * parity + 64, dh * 512:(dh + 1) * 512], ps[64 * dh:64 * dh + 64, 3, :],
                                   ACT.Copy).then_inc(yrow_sb, 1)

            def turned(E):
                act.wait_ge(actT_ps, E + 1)
                act.activation(actT.rearrange("p m h s -> p (m h s)"), ps[:, 2, :], ACT.Copy).then_inc(actT_sb, 1)

            def gates_turned(N):
                act.wait_ge(selgT_ps, N + 1)
                act.activation(selgT.rearrange("p t n -> p (t n)"), ps[:, 6, 0:T], ACT.Copy).then_inc(selgT_sb, 1)

            def pair(q, k, first, last, very_first=False):
                E, N = q * NE + k * 2, q * NPAIR + k
                if very_first:
                    act.wait_ge(gT_ps, 1)
                    act.activation(gatesT[0:NE, :], ps[0:NE, 3, 0:T], ACT.Copy).then_inc(gT_sb, 1)
                sigmoid(E)
                if not first:
                    downed(E - 1, 1)
                turned(E)
                if not first:
                    gates_turned(N - 1)
                sigmoid(E + 1)
                if not last:
                    gathered(N + 1)
                downed(E, 0)
                turned(E + 1)

            def one_pass(q, very_first=False):
                gathered(q * NPAIR)
                pair(q, 0, True, False, very_first)
                with act.Fori(1, NPAIR - 1) as k:
                    pair(q, k, False, False)
                pair(q, NPAIR - 1, False, True)
                gates_turned(q * NPAIR + NPAIR - 1)
                downed(q * NE + NE - 1, 1)

            one_pass(0, True)
            act.wait_ge(route_done, 1)
            most = act.value_load(cnti[0:1, 0:1], min_val=0, max_val=T)
            with act.If(most > SLOTS):
                with act.Fori(1, PASSES) as q:
                    one_pass(q)
            act.activation(ss[:, 7:8], epsc[:, 0:1], ACT.Sqrt)
            for t in range(TT):
                act.wait_ge(moe_done, t + 1)
                act.activation(outrow[:, t, :], xrows[:, t, :], ACT.Square, accum_out=ss[:, t:t + 1]).then_inc(fin_ss, 1)
                act.wait_ge(fin_ss, t + 1)
                act.activation(ss[:, 4 + t:5 + t], ss[:, t:t + 1], ACT.Sqrt, scale=1.0 / D, bias=epsc[:, 0:1]).then_inc(fin_root, 1)

        @block.vector
        def _(dve):
            steps = [0]

            def step(ins):
                steps[0] += 1
                ins.then_inc(dve_step, 1)

            def settle():
                dve.wait_ge(dve_step, steps[0])

            def link(ins):
                step(ins)
                settle()

            TS, TTn, STT = dve.tensor_scalar, dve.tensor_tensor, dve.scalar_tensor_tensor

            dve.memset(epsc[:, 0:1], EPS).then_inc(zeroed, 1)
            dve.memset(epsc[:, 1:2], LNX_EPS).then_inc(zeroed, 1)
            dve.wait_ge(root, 1)
            link(dve.reciprocal(ss[:, 4:6], ss[:, 4:6]))
            for t in range(TT):
                TS(xscaled[:, t, :], xrows[:, t, :], ss[:, 4 + t:5 + t], None, ALU.mult).then_inc(scaled, 1)
            dve.wait_ge(prm_loaded, 16)
            step(TS(omka[:], prm[:, PCOLS["ka"]:PCOLS["ka"] + 4], -1.0, 1.0, ALU.mult, ALU.add))
            TS(bq[:], prm[:, PCOLS["bswa"]:PCOLS["bswa"] + 4], SWA_SCALE, None, ALU.mult).then_inc(prm_sb, 1)
            for c in range(KC):
                if c % 2 == 0:
                    dve.wait_ge(xT_ps, c // 2 + 1)
                TS(xT[:, c, :], ps[:, c // 2, (c % 2) * T:(c % 2 + 1) * T], col("attn", c), None, ALU.mult).then_inc(xT_sb, 1)
            dve.wait_ge(root_m, 1)
            link(dve.reciprocal(ss[:, 6:8], ss[:, 6:8]))
            for t in range(TT):
                TS(memrows[:, t, :], memrows[:, t, :], ss[:, 6 + t:7 + t], None, ALU.mult).then_inc(scaled_m, 1)
            link(dve.memset(raw[:, :, 0:1], 0.0))

            def shift(a, b, signal):
                link(TTn(proj[:, a:b, :], raw[:, a:b, 0:T], raw[:, a:b, 1:T + 1], ALU.subtract))
                for f in range(a, b):
                    last = STT(proj[:, f, :], proj[:, f, :], col("mu", f), raw[:, f, 1:T + 1], ALU.mult, ALU.add)
                last.then_inc(signal, 1)

            dve.wait_ge(raw_sb, 1)
            shift(12, 14, lora_in)
            dve.wait_ge(raw_sb, 7)
            shift(0, 12, shifted)
            dve.wait_ge(shifted, 1)
            for f in range(HP):
                step(TS(kkn[:, f, :], proj[:, 4 + f, :], col("kk", f), None, ALU.mult))
            settle()
            TTn(csum, kkn, kkn, ALU.mult).then_inc(kk_sq, 1)
            dve.wait_ge(kk_ps, 1)
            for b in range(2):
                last = TS(pinc[:, 2 * b:2 * b + 2, :], ps[:, 5 + b, :].rearrange("p (c t) -> p c t", c=2), 1e-24, None, ALU.max)
            last.then_inc(kk_clamped, 1)
            dve.wait_ge(rate_sb, 1)
            dve.wait_ge(cst_loaded, 16)
            for f in range(HP):
                step(dve.tensor_tensor_scan(csum[:, f, :], const("resets"), pex[:, f, :], 0.0, ALU.mult, ALU.add))
            settle()
            dve.wait_ge(kk_root, 1)
            link(dve.reciprocal(pinc, pinc))
            link(TTn(kkn, kkn, pinc, ALU.mult))
            TTn(pex, csum, pex, ALU.subtract).then_inc(csum_sb, 1)
            dve.wait_ge(a_sb, 1)
            link(TTn(ar[:, :, 0, :], kkn, rate_a, ALU.mult))
            for f in range(HP):
                step(TS(rate_a[:, f, :], rate_a[:, f, :], col("ka", f), omka[:, f:f + 1], ALU.mult, ALU.add))
            settle()
            link(TTn(proj[:, 4:8, :], proj[:, 4:8, :], rate_a, ALU.mult))
            dve.wait_ge(powers_sb, 2)
            step(TTn(bT, ar[:, :, 0, :], pinv, ALU.mult))
            step(TTn(kT, proj[:, 4:8, :], pinv, ALU.mult))
            step(TTn(ar[:, :, 1, :], proj[:, 0:4, :], pinc, ALU.mult))
            for c in range(NCH):
                step(dve.tensor_copy(pend[:, :, c], pinc[:, :, c * CH + CH - 1]))
            dve.wait_ge(powers_sb, 3)
            settle()
            STT(ar[:, :, 0, :], kkn, -1.0, pex, ALU.mult, ALU.mult).then_inc(tilde_sb, 1)
            dve.wait_ge(tilde_sb, 1)
            for f in range(HP):
                last = STT(kkn[:, f, :], proj[:, f, :], col("rk", f), proj[:, 4 + f, :], ALU.mult, ALU.mult)
            last.then_inc(rk_sb, 1)
            dve.wait_ge(sink_loaded, 16)
            for n in range(TT):
                W = P * (n + 1)
                dve.wait_ge(score_ps, n + 1)
                if n == 1:
                    dve.wait_ge(pT_ps, 1)
                for h in range(8):
                    o = (h % 2) * 4 + h // 2
                    if n == 0:
                        src = ps[:, 3 + h % 2, (h // 2) * P:(h // 2 + 1) * P]
                    else:
                        src = ps[:, 1 + h // 4 if h % 2 == 0 else 4 - h // 4, (h // 2 % 2) * T:(h // 2 % 2 + 1) * T]
                    step(STT(probs[:, o * W:(o + 1) * W], const("dist", 2 * P - W, W), -SLOPES[h], src, ALU.mult, ALU.add))
                settle()
                if n == 0:
                    link(dve.tensor_copy(stat[:, 5, :].rearrange("p (a c) -> p a c", a=2),
                                         sinks[:].rearrange("p (c a) -> p a c", a=2)))
                    link(dve.tensor_copy(sinks[:], stat[:, 5, :]))
                link(dve.tensor_reduce(stat[:, 0, :], probs[:, 0:8 * W].rearrange("p (h m) -> p h m", h=8), AX.X, ALU.max))
                link(TTn(stat[:, 0, :], stat[:, 0, :], sinks[:], ALU.max))
                step(TTn(stat[:, 3, :], sinks[:], stat[:, 0, :], ALU.subtract))
                settle()
                TS(stat[:, 1, :], stat[:, 0, :], -1.0, None, ALU.mult).then_inc(negmax, 1)
                dve.wait_ge(expd, n + 1)
                link(TTn(stat[:, 5, :], stat[:, 2, :], stat[:, 4, :], ALU.add))
                link(dve.reciprocal(stat[:, 5, :], stat[:, 5, :]))
                pw = probs[:, 0:8 * W].rearrange("p (h m) -> p h m", h=8)
                TTn(pw, pw, stat[:, 5, :].unsqueeze(2).to_broadcast([P, 8, W]), ALU.mult).then_inc(normed, 1)

            for n in range(TT):
                dve.wait_ge(score_ps, n + 3)
                link(dve.tensor_reduce(stat[:, 0, 4 * n:4 * n + 4],
                                       ps[:, 2 + 3 * n:4 + 3 * n, :].rearrange("p b (h m) -> p (b h) m", h=2), AX.X, ALU.max))
                TS(stat[:, 1, 4 * n:4 * n + 4], stat[:, 0, 4 * n:4 * n + 4], -MEM_SCALE, None, ALU.mult).then_inc(negmax, 1)
            pm = mprobs.rearrange("p (n h m) -> p n h m", n=2, h=4)
            for n in range(TT):
                dve.wait_ge(expd, n + 3)
                link(dve.reciprocal(stat[:, 5, 4 * n:4 * n + 4], stat[:, 2, 4 * n:4 * n + 4]))
                TTn(pm[:, n], pm[:, n], stat[:, 5, 4 * n:4 * n + 4].unsqueeze(2).to_broadcast([P, 4, T]), ALU.mult).then_inc(normed, 1)
            dve.wait_ge(rk_ps, 1)
            for b in range(2):
                last = TTn(bonus[:, 2 * b:2 * b + 2, :], ps[:, 1 + 3 * b, :].rearrange("p (c t) -> p c t", c=2),
                           proj[:, 8 + 2 * b:10 + 2 * b, :], ALU.mult)
            last.then_inc(bonus_sb, 1)

            for g in range(4):
                for i in range(4):
                    n = 4 * g + i
                    dve.wait_ge(gram_ps, n + 1)
                    TTn(gram[:, n].rearrange("p (x y) t -> p x y t", x=2), ps[:, n % 6, :].rearrange("p (x y t) -> p x y t", x=2, y=2),
                        const("causal").rearrange("p (y t) -> p y t", y=2).unsqueeze(1).to_broadcast([P, 2, 2, P]),
                        ALU.mult).then_inc(gram_sb, 1)
                us4 = slice(4 * g, 4 * g + 4)
                dve.wait_ge(gram_sb, 4 * g + 4)
                link(TTn(invT[:, us4, :], gram[:, us4, 0, :], const("level0t").unsqueeze(1).to_broadcast([P, 4, P]), ALU.mult))
                TTn(invT[:, us4, :], invT[:, us4, :], ident.unsqueeze(1).to_broadcast([P, 4, P]), ALU.add).then_inc(level0_sb, 1)
            for j in range(1, LEVELS):
                for g in range(4):
                    dve.wait_ge(t1_ps, 4 * (j - 1) + g + 1)
                    TTn(t1s[:, g], ps[:, g, :].rearrange("p (u t) -> p u t", u=4),
                        const("level", j * P, P).unsqueeze(1).to_broadcast([P, 4, P]), ALU.mult).then_inc(t1_sb, 1)
                for g in range(4):
                    us4 = slice(4 * g, 4 * g + 4)
                    dve.wait_ge(xx_ps, 4 * (j - 1) + g + 1)
                    x_ = inv if j < LEVELS - 1 else invT
                    TTn(x_[:, us4, :], x_[:, us4, :], ps[:, 4 + g % 2, :].rearrange("p (u t) -> p u t", u=4),
                        ALU.add).then_inc(inv_sb, 1)
            step(dve.memset(state[:, 0], 0.0))
            dve.memset(rs_, 0.0).then_inc(zeroed, 1)
            points = fill_points()

            def merge(m):
                f = UNITS[m][1]
                dve.wait_ge(branch_ps, m + 1)
                dve.wait_ge(gate_sb, m + 1)
                if m < 4:
                    TTn(merged[:, f, :], gsig[:, m % 2, :], ps[:, 7, :], ALU.mult).then_inc(merged_sb, 1)
                else:
                    link(TTn(gsig[:, m % 2, :], gsig[:, m % 2, :], ps[:, 7, :], ALU.mult))
                    dve.wait_ge(merged_sb, m - 3)
                    TTn(merged[:, f, :], merged[:, f, :], gsig[:, m % 2, :], ALU.add).then_inc(merged_sb, 1)

            def merges_of(point):
                for p in points[point]:
                    if p % PIECES == 5:
                        merge(p // PIECES)

            for ch in range(NCH):
                t, c = ch // 2, ch % 2
                rs = slice(64 * c, 64 * c + 64)
                step(TTn(decay_end[:, ch % 2], heads.unsqueeze(1).to_broadcast([P, HP, P]),
                         pend[:, :, ch].unsqueeze(2).to_broadcast([P, HP, P]), ALU.mult))
                dve.wait_ge(r_ps, ch + 1)
                dve.wait_ge(av_sb, 4)
                if ch == 0:
                    dve.wait_ge(zeroed, 3)
                else:
                    dve.wait_ge(u_ps, ch)
                TTn(rs_[rs, :], ps[rs, 0, :], av[rs, t, :], ALU.add).then_inc(r_sb, 1)
                merges_of((ch, "a"))
                if ch < NCH - 1:
                    dve.wait_ge(s_ps, ch + 1)
                    settle()
                    link(TTn(state[:, (ch + 1) % 2], state[:, ch % 2], ps[:, 3, :].rearrange("p (c v) -> p c v", c=HP), ALU.add))
                    TTn(state[:, (ch + 1) % 2], state[:, (ch + 1) % 2], decay_end[:, ch % 2], ALU.mult).then_inc(s_sb, 1)
                    dve.wait_ge(s_sb, ch + 1)
                merges_of((ch, "b"))
                merges_of((ch, "c"))
                if c == 1:
                    dve.wait_ge(yh_ps, t + 1)
                    step(dve.tensor_copy(yT[:, :, t * P:(t + 1) * P], ps[:, 4 + t, :].rearrange("p (c v) -> p c v", c=HP)))
            settle()
            dve.sem_inc(yh_sb, 1)
            merges_of("mean")
            dve.wait_ge(mean_ps, 1)
            for b in range(2):
                step(STT(yc[:, 2 * b:2 * b + 2, :], ps[:, b, :].rearrange("p (c t) -> p c t", c=2), -1.0 / 64,
                         yT[:, 2 * b:2 * b + 2, :], ALU.mult, ALU.add))
            settle()
            dve.sem_inc(yc_sb, 1)
            TTn(sqr, yc, yc, ALU.mult).then_inc(yc_sb, 1)
            merges_of("var")
            dve.wait_ge(var_root, 1)
            link(dve.reciprocal(sqr, sqr))
            link(TTn(yc, yc, sqr, ALU.mult))
            for f in range(HP):
                step(TS(yc[:, f, :], yc[:, f, :], col("lnw", f), col("lnb", f), ALU.mult, ALU.add))
            settle()
            link(TTn(yc, yc, bonus, ALU.add))
            TTn(gT, gT, yc, ALU.mult).then_inc(y_rwkv_sb, 1)
            merges_of("rest")
            for m in range(N_FILL, len(UNITS)):
                merge(m)
            for t in range(TT):
                dve.wait_ge(out_ps, t + 1)
                TTn(xrows[:, t, :].rearrange("p (b n) -> p b n", b=2), xrows[:, t, :].rearrange("p (b n) -> p b n", b=2),
                    ps[:, 2 * t:2 * t + 2, :], ALU.add).then_inc(resid, 1)
                dve.wait_ge(ffn_root, t + 1)
                if t == 0:
                    dve.wait_ge(late_loaded, 16 * 5)
                link(dve.reciprocal(ss[:, 4 + t:5 + t], ss[:, 4 + t:5 + t]))
                STT(hn[:, t, :], xrows[:, t, :], ss[:, 4 + t:5 + t], ffnw, ALU.mult, ALU.mult).then_inc(hn_sb, 1)
            dve.wait_ge(logit_ps, 1)
            link(TTn(logit[:], ps[:, 0, 0:TT * NE].rearrange("p (t e) -> p t e", t=TT), brt[:].unsqueeze(1).to_broadcast([P, TT, NE]), ALU.add))
            for t in range(TT):
                step(dve.max(top8[:, t, :], logit[:, t, :]))
            settle()
            TS(rtmp[:, :, 0], top8[:, :, 0], -1.0, None, ALU.mult).then_inc(top_sb, 1)
            dve.wait_ge(top_sb, 1)
            link(dve.memset(top8[:, :, 4:8], 3e38))
            for t in range(TT):
                step(dve.match_replace(rest[:, t, :], top8[:, t, :], logit[:, t, :], -3e38))
            settle()
            TTn(chosen[:], rest[:], logit[:], ALU.not_equal).then_inc(chosen_sb, 1)
            dve.wait_ge(chosen_sb, 1)
            dve.wait_ge(top_exp, 1)
            link(TTn(gates[:], gates[:], chosen[:], ALU.mult))
            link(dve.tensor_reduce(rtmp[:, :, 1], gates[:], AX.X, ALU.add))
            link(dve.reciprocal(rtmp[:, :, 2], rtmp[:, :, 1]))
            TTn(gates[:], gates[:], rtmp[:, :, 2].unsqueeze(2).to_broadcast([P, TT, NE]), ALU.mult).then_inc(gates_sb, 1)
            dve.wait_ge(rank_ps, 1)
            step(STT(rank1[:], ps[:, 1, 0:TT * NE].rearrange("p (t e) -> p t e", t=TT), 1.0, chosen[:], ALU.add, ALU.mult))
            settle()

            def columns(a, k):
                return a[:, :, bass.ds(k * 2, 2)].unsqueeze(3).to_broadcast([P, TT, 2, SLOTS])

            def places(q):
                a = CONST["iota"][0]
                return cst[:, bass.ds(q * SLOTS + a, SLOTS)].unsqueeze(1).unsqueeze(1).to_broadcast([P, TT, 2, SLOTS])

            def select(q, k, N, very_first=False):
                if not very_first:
                    dve.wait_ge(xg_ps, N)
                TTn(sel, places(q), columns(rank1, k), ALU.is_equal).then_inc(sel_sb, 1)

            def select_gates(q, k, N, very_first=False):
                if not very_first:
                    dve.wait_ge(selgT_ps, N)
                TTn(selg, places(q), columns(rank1, k), ALU.is_equal).then_inc(selg_raw, 1)
                dve.wait_ge(selg_raw, N + 1)
                TTn(selg, selg, columns(gates, k), ALU.mult).then_inc(selg_sb, 1)

            def swiglu(E, very_first=False):
                dve.wait_ge(up_ps, E + 1)
                if not very_first:
                    dve.wait_ge(act_sb, E)
                TS(glu, ps[:, 0, :], LIMIT, None, ALU.min).then_inc(glu_sb, 1)
                TS(lin, ps[:, 1, :], LIMIT, -LIMIT, ALU.min, ALU.max).then_inc(up_read, 1)
                dve.wait_ge(up_read, E + 1)
                dve.wait_ge(glu_sb, E + 1)
                STT(lin, lin, 1.0, glu, ALU.add, ALU.mult).then_inc(prod_sb, 1)
                dve.wait_ge(prod_sb, E + 1)
                dve.wait_ge(sig_sb, E + 1)
                if not very_first:
                    dve.wait_ge(actT_ps, E)
                TTn(act_, lin, sig, ALU.mult).then_inc(act_sb, 1)

            def add_up(N, t, very_first=False, bank=6):
                dve.wait_ge(sc_ps, N * 2 + t + 1)
                if not very_first:
                    dve.wait_ge(acc_sb, N * 2 + t)
                a = xrows[:, t, :].rearrange("p (b n) -> p b n", b=2)
                TTn(a, a, ps[:, bank:bank + 2, :], ALU.add).then_inc(acc_sb, 1)

            def second_bias(t):
                dve.wait_ge(b2_ps, t + 1)
                a = xrows[:, t, :].rearrange("p (b n) -> p b n", b=2)
                TTn(a, a, ps[:, 6:8, :], ALU.add).then_inc(b2_sb, 1)

            def largest_count():
                dve.wait_ge(rank_ps, 2)
                link(dve.tensor_reduce(cnt[:], ps[:, 2, 0:NE], AX.X, ALU.max))
                link(dve.tensor_copy(cnti[:], cnt[:]))
                dve.sem_inc(route_done, 1)

            def pair(q, k, first, last, very_first=False, second=False):
                E, N = q * NE + k * 2, q * NPAIR + k
                if very_first:
                    largest_count()
                if not last:
                    select(q, k + 1, N + 1)
                if not first:
                    select_gates(q, k - 1, N - 1, second)
                swiglu(E, very_first)
                if very_first:
                    second_bias(0)
                    second_bias(1)
                    dve.wait_ge(b2_sb, 2)
                if not first:
                    add_up(N - 1, 0, second)
                    add_up(N - 1, 1)
                swiglu(E + 1)

            def one_pass(q, very_first=False):
                select(q, 0, q * NPAIR, very_first)
                pair(q, 0, True, False, very_first)
                if very_first:
                    pair(q, 1, False, False, False, True)
                    with dve.Fori(2, NPAIR - 1) as k:
                        pair(q, k, False, False)
                else:
                    with dve.Fori(1, NPAIR - 1) as k:
                        pair(q, k, False, False)
                pair(q, NPAIR - 1, False, True)
                N = q * NPAIR + NPAIR - 1
                select_gates(q, NPAIR - 1, N)
                add_up(N, 0)
                add_up(N, 1, False, 0)
                dve.wait_ge(acc_sb, N * 2 + 2)

            one_pass(0, True)
            most = dve.value_load(cnti[0:1, 0:1], min_val=0, max_val=T)
            with dve.If(most > SLOTS):
                with dve.Fori(1, PASSES) as q:
                    one_pass(q)
            for t in range(TT):
                dve.sem_inc(moe_done, 1)
            for t in range(TT):
                dve.wait_ge(fin_root, t + 1)
                link(dve.reciprocal(ss[:, 4 + t:5 + t], ss[:, 4 + t:5 + t]))
                STT(outrow[:, t, :], xrows[:, t, :], ss[:, 4 + t:5 + t], finw, ALU.mult, ALU.mult).then_inc(final_sb, 1)


_INS = ["x", "mem", "w_in", "rwkv_w2", "rwkv_a2", "rwkv_g2", "swa_sinks", "w_mem_kv", "w_gate", "w_branch", "w_out",
        "ffn_norm_w", "w_router", "b_router", "w_exp1", "b_exp1", "w_exp2", "b_exp2", "final_norm_w"]
_COLUMNS = ["attn_norm_w", "mem_norm_w", "rwkv_mu", "rwkv_w0", "rwkv_a0", "rwkv_kk", "rwkv_ka", "rwkv_rk", "rwkv_lnx_w",
            "rwkv_lnx_b", "b_swa"]


def kernel(**inputs):
    import concourse.bacc as bacc
    from concourse.bass_utils import run_bass_kernel_spmd

    nc = bacc.Bacc("TRN2", target_bir_lowering=False, num_devices=1)
    arrays = {f"in_{name}": np.ascontiguousarray(inputs[name]) for name in _INS}
    arrays["in_params"] = np.ascontiguousarray(np.concatenate([np.asarray(inputs[n]).reshape(-1, P) for n in _COLUMNS]).T)
    arrays["in_consts"] = constants()
    args = [nc.dram_tensor(name, a.shape, F32, kind="ExternalInput").ap() for name, a in arrays.items()]
    args.append(nc.dram_tensor("out_0", (1, T, D), F32, kind="ExternalOutput").ap())
    build(nc, *args)
    r = run_bass_kernel_spmd(nc, [arrays], core_ids=[0])
    return r.results[0]["out_0"]
```

```python
from contextlib import ExitStack

import numpy as np

import concourse.bass as bass
from concourse import mybir

P = 128
D = 1024
T = 256
KC = D // P
TT = T // P
F32 = mybir.dt.float32
I32 = mybir.dt.int32
ALU = mybir.AluOpType
ACT = mybir.ActivationFunctionType
AX = mybir.AxisListType

HR = 8
HP = HR // 2
CH = 64
NCH = T // CH
LEVELS = 6
EXP_HALF = float(np.exp(-0.5))
LNX_EPS = 64e-5
EPS = 1e-5
N_RWKV = 14
C_RWKV = N_RWKV * P
C_REST = 10 * P
MEM_SCALE = float(P) ** -0.5
SWA_SCALE = 64.0 ** -0.5
SLOPES = [2.0 ** (-8.0 * (h + 1) / 8) for h in range(8)]
MASKED = 1e30

NE = 32
NPAIR = NE // 2
SLOTS = 64
PASSES = T // SLOTS
ALPHA = 1.702
LIMIT = 7.0

RING = 16
NARROW = 6
SLOT = 2048
CPE = 12
GROUP = 4
TURNS = GROUP * CPE // RING
WIDE_AT = (8, 72, 80, 88, 96, 0, 16, 24, 32, 40)

PCOLS = {}
_at = 0
for _n, _w in (("attn", 8), ("memn", 8), ("mu", 14), ("w0", 4), ("a0", 4), ("kk", 4), ("ka", 4), ("rk", 4),
               ("lnw", 4), ("lnb", 4), ("bswa", 6)):
    PCOLS[_n] = _at
    _at += _w
NPCOL = _at

CONST = {}
_at = 0
for _n, _w in (("ident", P), ("heads", P), ("causal", 2 * P), ("level", LEVELS * P), ("level0t", P), ("before", P),
               ("ones", P), ("dist", 2 * P), ("iota", T), ("resets", T)):
    CONST[_n] = (_at, _w)
    _at += _w
NCONST = _at


def constants():
    c = np.zeros((P, NCONST), np.float32)

    def put(name, a):
        at, w = CONST[name]
        c[:, at:at + w] = a

    i = np.arange(P)
    p, f = i[:, None], i[None, :]
    same = (p // CH) == (f // CH)
    put("ident", p == f)
    put("heads", same)
    put("causal", np.concatenate([same & (p < f), same & (p <= f)], 1))
    level = [((p >> (j + 1)) == (f >> (j + 1))) & ((p >> j) % 2 == 1) & ((f >> j) % 2 == 0) for j in range(LEVELS)]
    put("level", np.concatenate(level, 1))
    put("level0t", level[0].T)
    put("before", p < f)
    put("ones", 1.0)
    j = np.arange(2 * P)[None, :]
    dist = p + P - j
    put("dist", np.where((dist >= 0) & (dist < P), dist, MASKED))
    put("iota", np.arange(1, T + 1)[None, :])
    put("resets", (np.arange(T)[None, :] % CH != 0))
    return c


BRANCHES = (2, 1, 0)
UNITS = [(b, f) for b in BRANCHES for f in range(4)]
PIECES = 6
N_FILL = 8


def fill_points():
    points = [(ch, s) for ch in range(NCH) for s in "abc"] + ["mean", "var", "rest"]
    counts = [1] * (3 * NCH) + [2, 3]
    counts.append(PIECES * N_FILL - sum(counts))
    at, out = 0, {}
    for p, n in zip(points, counts):
        out[p] = list(range(at, at + n))
        at += n
    return out


def mixer_chunks():
    order = [("in_rwkv", c) for c in range(KC)] + [("in_rest", c) for c in range(KC)]
    order += [("mem_kv", c) for c in range(KC // 2)]

    def merge(b):
        return [("gate", (b, 0)), ("gate", (b, 1)), ("branch", (b, 0)), ("gate", (b, 2)), ("gate", (b, 3)), ("branch", (b, 1))]

    order += merge(2) + merge(1)
    n_narrow = len(order)
    order += merge(0) + [("out", c) for c in range(KC // 2)]
    wide = len(order) - n_narrow
    slots = [(n - n_narrow) % NARROW for n in range(n_narrow)] + [NARROW + n for n in range(wide)]
    return order, slots


def build(nc, x, mem, w_in, rwkv_w2, rwkv_a2, rwkv_g2, swa_sinks, w_mem_kv, w_gate, w_branch, w_out,
          ffn_norm_w, w_router, b_router, w_exp1, b_exp1, w_exp2, b_exp2, final_norm_w, params, consts, out):
    order, slots = mixer_chunks()
    NMIX = len(order)
    index = {key: n for n, key in enumerate(order)}
    uses = [slots.count(s) for s in range(RING)]
    past = [slots[:n].count(s) for n, s in enumerate(slots)]
    previous = [max([m for m in range(n) if slots[m] == s], default=None) for n, s in enumerate(slots)]
    last_in = [max(m for m in range(NMIX) if slots[m] == s) for s in range(RING)]
    assert last_in == list(range(NMIX - RING, NMIX))

    with ExitStack() as ctx:
        def sb(name, shape, dt=F32):
            return ctx.enter_context(nc.sbuf_tensor(name, shape, dt))

        def sem(name):
            return ctx.enter_context(nc.semaphore(name))

        ring = sb("ring", [P, NARROW * SLOT + 48 * 256])
        upper = sb("upper", [P, 70 * 256])
        cst = sb("cst", [P, NCONST])
        xrows = sb("xrows", [P, TT, D])
        xT = sb("xT", [P, KC, T])
        factors = sb("factors", [P, 1024])
        lora = factors[:, 0:512]
        gate2 = factors[:, 512:1024]
        merged = sb("merged", [P, 4, 512])
        prm = sb("prm", [P, NPCOL])
        omka = sb("omka", [P, HP])
        bq = sb("bq", [P, HP])
        epsc = sb("epsc", [P, 2])
        ss = sb("ss", [P, 8])
        sinks = sb("sinks", [P, 8])
        stat = sb("stat", [P, 6, 8])
        pend = sb("pend", [P, HP, NCH])
        brt = sb("brt", [P, NE])
        logit = sb("logit", [P, TT, NE])
        top8 = sb("top8", [P, TT, 8])
        rest = sb("rest", [P, TT, NE])
        chosen = sb("chosen", [P, TT, NE])
        gates = sb("gates", [P, TT, NE])
        rank1 = sb("rank1", [P, TT, NE])
        rtmp = sb("rtmp", [P, TT, 4])
        cnt = sb("cnt", [P, 1])
        cnti = sb("cnti", [P, 1], I32)
        ps = ctx.enter_context(nc.psum_tensor("ps", [P, 8, 512], F32))

        def kb(at, size, pattern=None, **dims):
            if at < 48:
                assert at + size <= 48
                a = ring[:, NARROW * SLOT + at * 256:NARROW * SLOT + (at + size) * 256]
            else:
                a = upper[:, (at - 48) * 256:(at - 48 + size) * 256]
            return a.rearrange(pattern, **dims) if pattern else a

        def const(name, at=0, width=None):
            a, w = CONST[name]
            return cst[:, a + at:a + at + (width or w)]

        def col(name, n=0):
            return prm[:, PCOLS[name] + n:PCOLS[name] + n + 1]

        ident = const("ident")
        heads = const("heads")
        ones = const("ones")
        four = "p (c t) -> p c t"

        proj = kb(0, 14, four, c=14)
        raw = ring[:, NARROW * SLOT + 22 * 256:NARROW * SLOT + 22 * 256 + N_RWKV * (T + 1)].rearrange(four, c=N_RWKV)
        csum = kb(14, 4, four, c=4)
        pex = kb(18, 4, four, c=4)
        pinv = kb(22, 4, four, c=4)
        pinc = kb(26, 4, four, c=4)
        rate_a = kb(30, 4, four, c=4)
        kkn = kb(34, 4, four, c=4)
        ar = kb(38, 8, "p (c k t) -> p c k t", c=4, k=2)
        bT = kb(48, 4, four, c=4)
        kT = kb(52, 4, four, c=4)
        gT = kb(56, 4, four, c=4)
        btok = kb(60, 4, "p (t f) -> p t f", t=TT)
        ktok = kb(64, 4, "p (t f) -> p t f", t=TT)
        vtok = kb(68, 4, "p (t f) -> p t f", t=TT)
        dump = kb(38, 8, "p (t f) -> p t f", t=TT)
        xscaled = kb(60, 8, "p (t f) -> p t f", t=TT)
        probs = kb(60, 8)
        mprobs = kb(14, 8)
        mprobsT = kb(22, 8)
        dump_m = kb(22, 8, "p (t f) -> p t f", t=TT)
        gram = kb(72, 32, "p (u k t) -> p u k t", u=16, k=4)
        memT = kb(72, 8, "p (c t) -> p c t", c=KC)
        memrows = kb(80, 8, "p (t f) -> p t f", t=TT)
        probsT = kb(80, 8)
        sq_ = kb(88, 4, four, c=4)
        skd = kb(92, 2, four, c=2)
        svT = kb(94, 1)
        sv = kb(95, 1, "p (t f) -> p t f", t=TT)
        mq = kb(96, 4, four, c=4)
        kmT = kb(100, 4, four, c=4)
        vm = kb(104, 4, "p (t f) -> p t f", t=TT)
        y_swa = kb(110, 4, four, c=4)
        y_mem = kb(114, 4, four, c=4)
        inv = kb(8, 8, "p (u t) -> p u t", u=16)
        invT = kb(16, 8, "p (u t) -> p u t", u=16)
        bonus = kb(30, 4, four, c=4)
        sqr = kb(38, 4, four, c=4)
        t1s = kb(0, 8, "p (g u t) -> p g u t", g=4, u=4)
        av = kb(0, 4, "p (t f) -> p t f", t=TT)
        us = kb(4, 4, "p (t f) -> p t f", t=TT)
        rs_ = kb(46, 2)
        state = kb(48, 4, "p (b c v) -> p b c v", b=2, c=HP)
        decay_end = kb(52, 4, "p (b c v) -> p b c v", b=2, c=HP)
        yT = kb(24, 4, four, c=4)
        yc = kb(34, 4, four, c=4)
        gsig = kb(104, 4, "p (b n) -> p b n", b=2)
        mergedT = merged[:].rearrange("p b (c t) -> p (b c) t", c=2)
        xT_flat = xT[:].rearrange("p c t -> p (c t)")
        ffnw = xT_flat[:, 0:D]
        finw = xT_flat[:, D:2 * D]
        b1rows = merged[:].rearrange("p b n -> p (b n)")
        b2rows = kb(68, 4)
        wrt = kb(108, 1, "p (c e) -> p c e", c=KC)
        hn = kb(60, 8, "p (t f) -> p t f", t=TT)
        hnT = kb(110, 8, "p (c t) -> p c t", c=KC)
        sq_dump = kb(48, 4)
        xg = kb(48, 4, "p (c s) -> p c s", c=KC)
        glu = kb(52, 2)
        lin = kb(54, 2)
        sig = kb(104, 2)
        act_ = kb(106, 2)
        actT = kb(56, 2, "p (m h s) -> p m h s", m=4, h=2)
        yrow = factors[:]
        sel = kb(58, 1, "p (t e s) -> p t e s", t=TT, e=2)
        selg = kb(59, 1, "p (t e s) -> p t e s", t=TT, e=2)
        selgT = kb(108, 1, "p (t n) -> p t n", t=TT)
        gatesT = kb(109, 1)
        outrow = kb(110, 8, "p (t f) -> p t f", t=TT)

        def slot(s):
            return ring[:, s * SLOT:(s + 1) * SLOT] if s < NARROW else kb(WIDE_AT[s - NARROW], 8)

        slot_full = [sem(f"slot_full{s}") for s in range(RING)]
        slots_used = sem("slots_used")
        x_loaded = [sem("x_loaded0"), sem("x_loaded1")]
        mem_loaded, prm_loaded, ident_loaded, cst_loaded = sem("mem_loaded"), sem("prm_loaded"), sem("ident_loaded"), sem("cst_loaded")
        lora_loaded, sink_loaded, late_loaded = sem("lora_loaded"), sem("sink_loaded"), sem("late_loaded")
        b1_full = [sem("b1_full0"), sem("b1_full1")]
        root, root_m, scaled, scaled_m, prm_sb = sem("root"), sem("root_m"), sem("scaled"), sem("scaled_m"), sem("prm_sb")
        xT_ps, memT_ps, xT_sb, memT_sb = sem("xT_ps"), sem("memT_ps"), sem("xT_sb"), sem("memT_sb")
        rwkv_ps, raw_sb, lora_in, shifted, lora_act = sem("rwkv_ps"), sem("raw_sb"), sem("lora_in"), sem("shifted"), sem("lora_act")
        rest_ps, rest_sb, kv_ps, kv_sb = sem("rest_ps"), sem("rest_sb"), sem("kv_ps"), sem("kv_sb")
        zw_ps, za_ps, g_ps, rate_sb, a_sb, g_sb = sem("zw_ps"), sem("za_ps"), sem("g_ps"), sem("rate_sb"), sem("a_sb"), sem("g_sb")
        kk_sq, kk_ps, kk_clamped, kk_root = sem("kk_sq"), sem("kk_ps"), sem("kk_clamped"), sem("kk_root")
        csum_sb, powers_sb, tilde_sb, rk_sb, rk_ps, bonus_sb = (sem("csum_sb"), sem("powers_sb"), sem("tilde_sb"),
                                                               sem("rk_sb"), sem("rk_ps"), sem("bonus_sb"))
        score_ps, score_sb, negmax, expd, normed, pT_ps, pT_sb, pv_ps, pv_sb = (
            sem("score_ps"), sem("score_sb"), sem("negmax"), sem("expd"), sem("normed"), sem("pT_ps"), sem("pT_sb"),
            sem("pv_ps"), sem("pv_sb"))
        svT_ps, sv_sb = sem("svT_ps"), sem("sv_sb")
        tok_ps, tok_sb, ktok_ps, ktok_sb = sem("tok_ps"), sem("tok_sb"), sem("ktok_ps"), sem("ktok_sb")
        gram_ps, gram_sb, level0_sb, turned_ps, invT_sb, inv_sb, t1_ps, t1_sb, xx_ps = (
            sem("gram_ps"), sem("gram_sb"), sem("level0_sb"), sem("turned_ps"), sem("invT_sb"),
                                                              sem("inv_sb"), sem("t1_ps"), sem("t1_sb"), sem("xx_ps"))
        av_ps, av_sb, zeroed, r_ps, r_sb, u_ps, u_sb, s_ps, s_sb, yh_ps = (
            sem("av_ps"), sem("av_sb"), sem("zeroed"), sem("r_ps"), sem("r_sb"), sem("u_ps"), sem("u_sb"),
            sem("s_ps"), sem("s_sb"), sem("yh_ps"))
        yh_sb, mean_ps, yc_sb, var_ps, var_root, y_rwkv_sb = (sem("yh_sb"), sem("mean_ps"), sem("yc_sb"), sem("var_ps"),
                                                              sem("var_root"), sem("y_rwkv_sb"))
        gate_ps, gate_sb, branch_ps, merged_sb, out_ps, resid = (sem("gate_ps"), sem("gate_sb"), sem("branch_ps"),
                                                                 sem("merged_sb"), sem("out_ps"), sem("resid"))
        ffn_ss, ffn_root, hn_sb, hnT_ps, hnT_sb, logit_ps = (sem("ffn_ss"), sem("ffn_root"), sem("hn_sb"), sem("hnT_ps"),
                                                             sem("hnT_sb"), sem("logit_ps"))
        top_sb, top_exp, chosen_sb, rank_ps, gates_sb, gT_ps, gT_sb, b2_ps, route_done = (
            sem("top_sb"), sem("top_exp"), sem("chosen_sb"), sem("rank_ps"), sem("gates_sb"), sem("gT_ps"), sem("gT_sb"),
            sem("b2_ps"), sem("route_done"))
        b2_sb = sem("b2_sb")
        sel_sb, xg_ps, xg_sb, up_ps, up_read, glu_sb, sig_sb, prod_sb, act_sb = (
            sem("sel_sb"), sem("xg_ps"), sem("xg_sb"), sem("up_ps"), sem("up_read"), sem("glu_sb"), sem("sig_sb"),
            sem("prod_sb"), sem("act_sb"))
        actT_ps, actT_sb, down_ps, yrow_sb, selg_raw, selg_sb, selgT_ps, selgT_sb, sc_ps, acc_sb = (
            sem("actT_ps"), sem("actT_sb"), sem("down_ps"), sem("yrow_sb"), sem("selg_raw"), sem("selg_sb"),
            sem("selgT_ps"), sem("selgT_sb"), sem("sc_ps"), sem("acc_sb"))
        fin_ss, fin_root, fin_scale, final_sb, stored = (sem("fin_ss"), sem("fin_root"), sem("fin_scale"), sem("final_sb"),
                                                         sem("stored"))
        dve_step, act_step = sem("dve_step"), sem("act_step")

        block = ctx.enter_context(nc.Block())

        def place(g, m):
            return m % RING, g * TURNS + (m // RING + 1), g * (GROUP * CPE) + m

        def w1_place(c, g, r, zero):
            return place(g, r * CPE + c if zero else r * CPE + c - 4)

        def w2_place(i, g, r, final):
            return place(g, r * CPE + i + (8 if final else 16))

        def rows(w):
            return w.rearrange("(c p) f -> p c f", p=P)

        @block.sync
        def _(sp):
            for t in range(TT):
                sp.dma_start(xrows[:, t, :], x[0, t * P:(t + 1) * P, :]).then_inc(x_loaded[t], 16)
            sp.dma_start(prm[:], params).then_inc(prm_loaded, 16)
            sp.dma_start(cst[:, 0:2 * P], consts[:, 0:2 * P]).then_inc(ident_loaded, 16)
            w_in_r = rows(w_in[0])
            kv_r = rows(w_mem_kv[0])
            out_r = rows(w_out[0])
            for n, (name, c) in enumerate(order):
                s = slots[n]
                if previous[n] is not None:
                    sp.wait_ge(slots_used, previous[n] + 1)
                elif s == NARROW:
                    sp.wait_ge(t1_ps, 4 * (LEVELS - 1))
                elif s == NARROW + 1:
                    sp.wait_ge(yh_ps, 2)
                elif s == NARROW + 5:
                    sp.wait_ge(y_rwkv_sb, 1)
                wide = slot(s).rearrange("p (c f) -> p c f", c=2)
                if name == "in_rwkv":
                    dst, src = slot(s)[:, 0:C_RWKV], w_in_r[:, c, 0:C_RWKV]
                elif name == "in_rest":
                    dst, src = slot(s)[:, 0:C_REST], w_in_r[:, c, C_RWKV:C_RWKV + C_REST]
                elif name == "mem_kv":
                    dst, src = wide, kv_r[:, 2 * c:2 * c + 2, :]
                elif name == "gate":
                    dst = slot(s).rearrange("p (c f) -> p c f", c=KC)
                    src = rows(w_gate[0, c[0]])[:, :, c[1] * 256:(c[1] + 1) * 256]
                elif name == "branch":
                    dst = slot(s).rearrange("p (c f) -> p c f", c=4)
                    src = rows(w_branch[0, c[0]])[:, :, c[1] * 512:(c[1] + 1) * 512]
                else:
                    dst, src = wide, out_r[:, 2 * c:2 * c + 2, :]
                sp.dma_start(dst, src).then_inc(slot_full[s], 16)
                if n == 2:
                    sp.dma_start(memrows, mem[0].rearrange("(t p) d -> p t d", p=P)).then_inc(mem_loaded, 16)
                if n == 3:
                    sp.dma_start(cst[:, 2 * P:], consts[:, 2 * P:]).then_inc(cst_loaded, 16)
                    sp.dma_start(lora[0:64, :], rwkv_w2[0]).then_inc(lora_loaded, 16)
                    sp.dma_start(lora[64:P, :], rwkv_a2[0]).then_inc(lora_loaded, 16)
                    sp.dma_start(gate2, rwkv_g2[0]).then_inc(lora_loaded, 16)
                    sp.dma_start(sinks[:], swa_sinks.to_broadcast([P, 8])).then_inc(sink_loaded, 16)
            sp.dma_start(b2rows[0:NE, :], b_exp2[0]).then_inc(late_loaded, 16)
            sp.dma_start(wrt, w_router[0].rearrange("(c p) e -> p c e", p=P)).then_inc(late_loaded, 16)
            sp.dma_start(brt[:], b_router.to_broadcast([P, NE])).then_inc(late_loaded, 16)

            def load_w1(q, a, r, zero=False, bias=True):
                g = q * (NE // GROUP) + a
                for c in range(KC):
                    s, _, n = w1_place(c, g, r, zero)
                    sp.wait_ge(slots_used, n + (NMIX - RING + 1))
                    if c == 0 and bias:
                        at = 64 * (r % 2)
                        sp.dma_start(b1rows[at:at + 1, :], b_exp1[0, bass.ds(a * GROUP + r, 1), :]).then_inc(b1_full[r % 2], 16)
                    sp.dma_start(slot(s), w_exp1[0, bass.ds(a * GROUP + r, 1), c * P:(c + 1) * P, :].rearrange("a p f -> p (a f)"))\
                      .then_inc(slot_full[s], 16)

            def load_w2(q, a, r, final=False):
                g = q * (NE // GROUP) + a
                for i in range(4):
                    s, _, n = w2_place(i, g, r, final)
                    sp.wait_ge(slots_used, n + (NMIX - RING + 1))
                    sp.dma_start(slot(s).rearrange("p (c f) -> p c f", c=2),
                                 w_exp2[0, bass.ds(a * GROUP + r, 1), 2 * i * P:(2 * i + 2) * P, :].rearrange("a (c p) f -> p (a c) f", p=P))\
                      .then_inc(slot_full[s], 16)

            def load_group(q, a, count=GROUP, bias_from=0):
                for r in range(count):
                    load_w1(q, a, r + 1, False, r >= bias_from)
                    load_w2(q, a, r)

            def load_pass(q, very_first=False):
                load_w1(q, 0, 0, True, not very_first)
                if very_first:
                    load_group(q, 0, GROUP, 1)
                with sp.Fori(1 if very_first else 0, NE // GROUP - 1) as a:
                    load_group(q, a)
                load_group(q, NE // GROUP - 1, GROUP - 1)
                load_w2(q, NE // GROUP - 1, GROUP - 1, True)
                for t in range(TT):
                    sp.wait_ge(final_sb, q * TT + t + 1)
                    sp.dma_start(out[0, t * P:(t + 1) * P, :], outrow[:, t, :]).then_inc(stored, 16)

            load_pass(0, True)
            sp.wait_ge(stored, TT * 16)
            sp.wait_ge(route_done, 1)
            most = sp.value_load(cnti[0:1, 0:1], min_val=0, max_val=T)
            with sp.If(most > SLOTS):
                with sp.Fori(1, PASSES) as q:
                    load_pass(q)
                sp.wait_ge(stored, PASSES * TT * 16)

        @block.tensor
        def _(pe):
            def mm(o, l, r, start=True, stop=True):
                return pe.matmul(o, l, r, start=start, stop=stop, skip_group_check=True)

            def half(bank, n):
                return ps[:, bank + n // 2, (n % 2) * T:(n % 2) * T + T]

            def take(name, c):
                n = index[(name, c)]
                pe.wait_ge(slot_full[slots[n]], 16 * (past[n] + 1))
                return slot(slots[n])

            pe.wait_ge(ident_loaded, 16)
            for t in range(TT):
                pe.wait_ge(scaled, t + 1)
                for c in range(KC):
                    last = pe.transpose(half(0, c)[:, t * P:(t + 1) * P], xscaled[:, t, c * P:(c + 1) * P], ident)
                    if t == 1 and c % 2:
                        last.then_inc(xT_ps, 1)

            for c in range(KC):
                w = take("in_rwkv", c)
                for f in range(N_RWKV):
                    if c == 0 and f in (0, 2, 4, 6):
                        pe.wait_ge(xT_sb, f + 2)
                    last = mm(half(0, f), w[:, f * P:(f + 1) * P], xT[:, c, :], c == 0 and f % 2 == 0, c == KC - 1)
                    if c == KC - 1 and f % 2:
                        last.then_inc(rwkv_ps, 1)
                if c < KC - 1:
                    last.then_inc(slots_used, 1)

            def low_rank(c):
                if c == 1:
                    pe.wait_ge(raw_sb, 7)
                    pe.wait_ge(lora_loaded, 48)
                    pe.wait_ge(lora_act, 1)
                    for f in range(HP):
                        last = mm(half(5, f), lora[0:64, f * P:(f + 1) * P], proj[0:64, 12, :], f % 2 == 0)
                    last.then_inc(zw_ps, 1)
                elif c == 2:
                    pe.wait_ge(rate_sb, 1)
                    for f in range(HP):
                        last = mm(half(7 - f // 2 * 2, f % 2), lora[64:P, f * P:(f + 1) * P], proj[64:P, 12, :], f % 2 == 0)
                    last.then_inc(za_ps, 1)
                elif c == 3:
                    pe.wait_ge(lora_act, 2)
                    pe.wait_ge(a_sb, 1)
                    for f in range(HP):
                        last = mm(half(6, f), gate2[:, f * P:(f + 1) * P], proj[:, 13, :], f % 2 == 0)
                    last.then_inc(g_ps, 1)
                elif c == 4:
                    pe.wait_ge(g_sb, 1)
                    pe.wait_ge(kk_sq, 1)
                    for b in range(2):
                        last = mm(ps[:, 5 + b, :], heads, csum[:, 2 * b:2 * b + 2, :])
                    last.then_inc(kk_ps, 1)
                elif c in (5, 6):
                    pe.wait_ge(kk_clamped, 1)
                    if c == 5:
                        pe.wait_ge(scaled_m, 2)
                    else:
                        pe.wait_ge(memT_sb, 4)
                    for i in range(4):
                        k = 4 * (c - 5) + i
                        dst = half(7 - i // 2 * 2, i % 2) if c == 5 else half(6, i)
                        for t in range(TT):
                            last = pe.transpose(dst[:, t * P:(t + 1) * P], memrows[:, t, k * P:(k + 1) * P], ident)
                    last.then_inc(memT_ps, 1)

            for c in range(KC):
                w = take("in_rest", c)
                for f in range(10):
                    if c == 0 and f % 2 == 0:
                        pe.wait_ge(raw_sb, f // 2 + 1)
                    last = mm(half(0, f), w[:, f * P:(f + 1) * P], xT[:, c, :], c == 0 and f % 2 == 0, c == KC - 1)
                    if c == 0 and f == 0:
                        last.then_inc(slots_used, 1)
                last.then_inc(slots_used if c < KC - 1 else rest_ps, 1)
                low_rank(c)

            def mem_kv(first, end):
                for k in range(first, end):
                    c, cc = k // 2, k % 2
                    w = take("mem_kv", c)
                    for f in range(4):
                        key = mm(half(5, f), w[:, cc * D + f * P:cc * D + (f + 1) * P], memT[:, k, :], k == 0 and f % 2 == 0, k == KC - 1)
                    if k == 0:
                        key.then_inc(slots_used, 1)
                    for t in range(TT):
                        if k == 0 and t == 1:
                            pe.wait_ge(rest_sb, 2)
                        last = mm(ps[:, (7 + t) % 8, :], memT[:, k, t * P:(t + 1) * P], w[:, cc * D + 512:cc * D + D],
                                  k == 0, k == KC - 1)
                    if cc:
                        last.then_inc(slots_used if k < KC - 1 else kv_ps, 1)

            pe.wait_ge(memT_sb, 8)
            mem_kv(0, 1)
            pe.wait_ge(rest_sb, 7)
            for t in range(TT):
                last = pe.transpose(ps[:, 1, t * P:(t + 1) * P], svT[:, t * P:(t + 1) * P], ident)
            last.then_inc(svT_ps, 1)
            pe.wait_ge(rest_sb, 11)
            for h in range(8):
                b = 64 * (h % 2)
                last = mm(ps[:, 3 + h % 2, (h // 2) * P:(h // 2 + 1) * P], sq_[b:b + 64, h // 2, 0:P],
                          skd[b:b + 64, h // 4, 0:P], h < 2)
            last.then_inc(score_ps, 1)
            mem_kv(1, 3)
            pe.wait_ge(normed, 2)
            pe.wait_ge(sv_sb, 1)
            for h in range(8):
                last = pe.transpose(ps[:, 1 + h // 4, (h % 4) * P:(h % 4 + 1) * P],
                                    probs[:, ((h % 2) * 4 + h // 2) * P:((h % 2) * 4 + h // 2 + 1) * P], ident)
            last.then_inc(pT_ps, 1)
            mem_kv(3, 4)
            pe.wait_ge(pT_sb, 2)
            for h in range(8):
                b = 64 * (h % 2)
                last = mm(ps[b:b + 64, 3, (h // 2) * P:(h // 2 + 1) * P], sv[:, 0, (h // 4) * 64:(h // 4) * 64 + 64],
                          probsT[:, h * P:(h + 1) * P], h < 2)
            last.then_inc(pv_ps, 1)
            for h in (0, 2, 4, 6, 1, 3, 5, 7):
                b = 64 * (h % 2)
                bank = 1 + h // 4 if h % 2 == 0 else 4 - h // 4
                if h == 5:
                    pe.wait_ge(pv_sb, 1)
                last = mm(ps[:, bank, (h // 2 % 2) * T:(h // 2 % 2 + 1) * T], sq_[b:b + 64, h // 2, P:T],
                          skd[b:b + 64, h // 4, :], h // 2 % 2 == 0)
            last.then_inc(score_ps, 1)
            mem_kv(4, 7)
            pe.wait_ge(normed, 4)
            for h in range(8):
                for m in range(2):
                    at = ((h % 2) * 4 + h // 2) * T + m * P
                    last = pe.transpose(ps[:, 1 + h // 2, (h % 2) * T + m * P:(h % 2) * T + (m + 1) * P],
                                        probs[:, at:at + P], ident)
            last.then_inc(pT_ps, 1)
            mem_kv(7, 8)
            pe.wait_ge(pT_sb, 6)
            for h in range(8):
                b = 64 * (h % 2)
                for m in range(2):
                    last = mm(ps[b:b + 64, 1, (h // 2) * P:(h // 2 + 1) * P], sv[:, m, (h // 4) * 64:(h // 4) * 64 + 64],
                              probsT[:, (2 * h + m) * P:(2 * h + m + 1) * P], h < 2 and m == 0, m == 1)
                    if h == 0 and m == 0:
                        last.then_inc(slots_used, 1)
            last.then_inc(pv_ps, 1)

            pe.wait_ge(tilde_sb, 1)
            for t in range(TT):
                for c in range(HP):
                    last = pe.transpose(ps[:, 4 - t, c * P:(c + 1) * P], kT[:, c, t * P:(t + 1) * P], ident)
                last.then_inc(ktok_ps, 1)
            pe.wait_ge(kv_sb, 2)
            for n in range(TT):
                for h in range(4):
                    if n == 0 and h == 2:
                        pe.wait_ge(ktok_sb, 2)
                    last = mm(half(2 + 3 * n, h), mq[:, h, n * P:(n + 1) * P], kmT[:, h, :], h % 2 == 0)
                last.then_inc(score_ps, 1)
            pe.wait_ge(kv_sb, 4)
            for src, banks in ((bT, (7, 0)), (proj[:, 8:12, :], (1, 4))):
                if banks[0] == 1:
                    pe.wait_ge(pv_sb, 2)
                for t in range(TT):
                    for c in range(HP):
                        last = pe.transpose(ps[:, banks[t], c * P:(c + 1) * P], src[:, c, t * P:(t + 1) * P], ident)
                    last.then_inc(tok_ps, 1)
            pe.wait_ge(tok_sb, 2)
            pe.wait_ge(rk_sb, 1)
            for b in range(2):
                last = mm(ps[:, (7 + b) % 8, :], heads, kkn[:, 2 * b:2 * b + 2, :])
            last.then_inc(rk_ps, 1)
            pm = mprobs.rearrange("p (n h m) -> p n h m", n=2, h=4)
            pmT = mprobsT.rearrange("p (n h m q) -> p n h m q", n=2, h=4, m=2)
            for n in range(TT):
                pe.wait_ge(normed, n + 5)
                for h in range(4):
                    for m in range(2):
                        last = pe.transpose(ps[:, 2 + 3 * n + h // 2, (h % 2) * T + m * P:(h % 2) * T + (m + 1) * P],
                                            pm[:, n, h, m * P:(m + 1) * P], ident)
                last.then_inc(pT_ps, 1)
            pe.wait_ge(tok_sb, 4)
            for n in range(TT):
                pe.wait_ge(pT_sb, 2 * n + 8)
                for h in range(4):
                    for m in range(2):
                        last = mm(ps[:, 1 + 3 * n, h * P:(h + 1) * P], vm[:, m, h * P:(h + 1) * P], pmT[:, n, h, m, :],
                                  h == 0 and m == 0, m == 1)
                last.then_inc(pv_ps, 1)
            pe.wait_ge(bonus_sb, 1)
            pe.wait_ge(cst_loaded, 16)
            def turn_inverse(j, g):
                m = 4 * j + g
                if j == 0:
                    pe.wait_ge(level0_sb, g + 1)
                else:
                    pe.wait_ge(inv_sb, m + 1)
                if m >= 6:
                    pe.wait_ge(invT_sb, m - 5)
                elif m >= 2:
                    pe.wait_ge(inv_sb, m - 1)
                for i in range(4):
                    last = pe.transpose(ps[:, 6 + g % 2, i * P:(i + 1) * P], (inv if j else invT)[:, 4 * g + i, :], ident)
                last.then_inc(turned_ps, 1)

            pe.wait_ge(pv_sb, 4)
            for g in range(4):
                t, par = g // 2, g % 2
                b = 64 * par
                for i in range(4):
                    n = 4 * g + i
                    if n >= 6:
                        pe.wait_ge(gram_sb, n - 5)
                    ts = slice(t * P, (t + 1) * P)
                    mm(ps[:, n % 6, 0:T], bT[b:b + 64, i, ts], ar[b:b + 64, i, :, ts])
                    mm(ps[:, n % 6, T:2 * T], kT[b:b + 64, i, ts], ar[b:b + 64, i, :, ts], False).then_inc(gram_ps, 1)
                if g:
                    turn_inverse(0, g - 1)
            for j in range(1, LEVELS):
                late = {0: 3} if j == 1 else {0: 2, 1: 3}
                for g in range(4):
                    pe.wait_ge(inv_sb, 4 * (j - 1) + g + 1)
                    if j == 1:
                        pe.wait_ge(gram_sb, 16)
                    for i in range(4):
                        u = 4 * g + i
                        last = mm(ps[:, g, i * P:(i + 1) * P], gram[:, u, 0, :], inv[:, u, :], i == 0)
                    last.then_inc(t1_ps, 1)
                    if g in late:
                        turn_inverse(j - 1, late[g])
                for g in range(4):
                    n = 4 * (j - 1) + g
                    pe.wait_ge(t1_sb, n + 1)
                    if n >= 2:
                        pe.wait_ge(inv_sb, 4 + n - 1)
                    if j > 1:
                        pe.wait_ge(invT_sb, n - 3)
                    for i in range(4):
                        u = 4 * g + i
                        if j < LEVELS - 1:
                            last = mm(ps[:, 4 + g % 2, i * P:(i + 1) * P], invT[:, u, :], t1s[:, g, i, :], i == 0)
                        else:
                            last = mm(ps[:, 4 + g % 2, i * P:(i + 1) * P], t1s[:, g, i, :], invT[:, u, :], i == 0)
                    last.then_inc(xx_ps, 1)
                    if g >= 2 and j < LEVELS - 1:
                        turn_inverse(j, g - 2)
            for t in range(TT):
                for h in range(HR):
                    last = mm(ps[:, (6, 1)[t] + h // 4, (h % 4) * P:(h % 4 + 1) * P],
                              gram[:, t * 8 + (h % 2) * 4 + h // 2, 2, :], vtok[:, t, (h // 2) * P:(h // 2 + 1) * P], h % 4 == 0)
                last.then_inc(av_ps, 1)
            pe.wait_ge(inv_sb, 4 * LEVELS)
            pe.wait_ge(zeroed, 3)
            pe.wait_ge(av_sb, 2)

            def piece(p):
                m, r = p // PIECES, p % PIECES
                b, f = UNITS[m]
                if r < 4:
                    if r == 0 and m:
                        pe.wait_ge(gate_sb, m)
                    w = take("gate", (b, f))
                    for k in (2 * r, 2 * r + 1):
                        for ff in range(2):
                            last = mm(half(6, ff), w[:, k * 256 + ff * P:k * 256 + (ff + 1) * P], xT[:, k, :],
                                      k == 0 and ff == 0, k == KC - 1)
                            if k == 0 and ff == 0 and m and m % 2 == 0:
                                last.then_inc(slots_used, 1)
                    if r == 3:
                        last.then_inc(gate_ps, 1)
                else:
                    if r == 4 and m:
                        pe.wait_ge(merged_sb, m)
                    w = take("branch", (b, f // 2))
                    for k in (2 * (r - 4), 2 * (r - 4) + 1):
                        for ff in range(2):
                            at = k * 512 + (f % 2) * 256 + ff * P
                            last = mm(half(7, ff), w[:, at:at + P], (gT, y_swa, y_mem)[b][:, k, :], k == 0 and ff == 0, k == 3)
                            if k == 0 and ff == 0:
                                last.then_inc(slots_used, 1)
                    if r == 5:
                        last.then_inc(branch_ps, 1)

            points = fill_points()

            def fill(point):
                for p in points[point]:
                    piece(p)

            for ch in range(NCH):
                t, c = ch // 2, ch % 2
                rs = slice(64 * c, 64 * c + 64)
                toks = slice(ch * CH, (ch + 1) * CH)
                if ch:
                    pe.wait_ge(s_sb, ch)
                for hp in range(HP):
                    last = mm(ps[rs, 0, hp * P:(hp + 1) * P], ar[:, hp, 0, toks], state[:, ch % 2, hp, :], hp == 0)
                last.then_inc(r_ps, 1)
                for hp in range(HP):
                    mm(ps[:, 3, hp * P:(hp + 1) * P], ktok[rs, t, hp * P:(hp + 1) * P], vtok[rs, t, hp * P:(hp + 1) * P], hp == 0)
                for hp in range(HP):
                    mm(ps[:, 4 + t, hp * P + c * CH:hp * P + (c + 1) * CH], state[:, ch % 2, hp, :], ar[:, hp, 1, toks],
                       c == 0 and hp == 0)
                fill((ch, "a"))
                pe.wait_ge(r_sb, ch + 1)
                for h in range(HR):
                    last = mm(ps[rs, 1 + h // 4, (h % 4) * P:(h % 4 + 1) * P], invT[:, t * 8 + (h % 2) * 4 + h // 2, rs],
                              rs_[:, (h // 2) * P:(h // 2 + 1) * P], h % 4 == 0)
                last.then_inc(u_ps, 1)
                fill((ch, "b"))
                pe.wait_ge(u_sb, ch + 1)
                for hp in range(HP):
                    last = mm(ps[:, 3, hp * P:(hp + 1) * P], btok[rs, t, hp * P:(hp + 1) * P], us[rs, t, hp * P:(hp + 1) * P], False)
                last.then_inc(s_ps, 1)
                fill((ch, "c"))
                if c == 1:
                    for h in range(HR):
                        u = t * 8 + (h % 2) * 4 + h // 2
                        o = ps[64 * (h % 2):64 * (h % 2) + 64, 4 + t, (h // 2) * P:(h // 2 + 1) * P]
                        mm(o, vtok[:, t, h * 64:(h + 1) * 64], gram[:, u, 3, :], False)
                        last = mm(o, us[:, t, h * 64:(h + 1) * 64], gram[:, u, 1, :], False)
                    last.then_inc(yh_ps, 1)
            fill("mean")
            pe.wait_ge(yh_sb, 1)
            for b in range(2):
                last = mm(ps[:, b, :], heads, yT[:, 2 * b:2 * b + 2, :])
            last.then_inc(mean_ps, 1)
            fill("var")
            pe.wait_ge(yc_sb, 2)
            for b in range(2):
                last = mm(ps[:, b, :], heads, sqr[:, 2 * b:2 * b + 2, :])
            last.then_inc(var_ps, 1)
            fill("rest")
            pe.wait_ge(y_rwkv_sb, 1)
            for p in range(PIECES * N_FILL, PIECES * len(UNITS)):
                piece(p)
            def turn_input(t):
                for c in range(KC):
                    if c % 4 == 0:
                        pe.wait_ge(hn_sb, 2 * t + c // 4 + 1)
                        if t == 1 and c == 0:
                            pe.wait_ge(merged_sb, len(UNITS))
                    last = pe.transpose(ps[:, 4 + 2 * t + c // 4, (c % 4) * P:(c % 4 + 1) * P], hn[:, t, c * P:(c + 1) * P], ident)
                    if c % 4 == 3:
                        last.then_inc(hnT_ps, 1)

            for t in range(TT):
                for k in range(KC):
                    w = take("out", k // 2)
                    if t == 0 and k % 2 == 0:
                        pe.wait_ge(merged_sb, N_FILL + k // 2 + 1)
                    for n in range(2):
                        last = mm(ps[:, 2 * t + n, :], mergedT[:, k, t * P:(t + 1) * P],
                                  w[:, (k % 2) * D + n * 512:(k % 2) * D + (n + 1) * 512], k == 0, k == KC - 1)
                        if t == 0 and k == 0 and n == 0:
                            last.then_inc(slots_used, 1)
                    if t == 1 and k % 2 and k < KC - 1:
                        last.then_inc(slots_used, 1)
                    if t == 1 and k == 5:
                        turn_input(0)
                last.then_inc(out_ps, 1)
            for t in range(TT):
                if t == 1:
                    turn_input(1)
                for c in range(KC):
                    if c % 4 == 0:
                        pe.wait_ge(hnT_sb, 2 * t + c // 4 + 1)
                    if t == 0 and c == 0:
                        pe.wait_ge(late_loaded, 16 * 5)
                        pe.wait_ge(resid, 1)
                    last = mm(ps[:, 0, t * NE:(t + 1) * NE], hnT[:, c, t * P:(t + 1) * P], wrt[:, c, :], t == 0 and c == 0, c == KC - 1)
                    if t == 0 and c == 0:
                        last.then_inc(slots_used, 1)
            last.then_inc(logit_ps, 1)
            pe.wait_ge(chosen_sb, 1)
            before = const("before")
            mm(ps[:, 1, 0:NE], before, chosen[:, 0, :])
            mm(ps[:, 1, NE:2 * NE], ones, chosen[:, 0, :], False)
            mm(ps[:, 1, NE:2 * NE], before, chosen[:, 1, :], False).then_inc(rank_ps, 1)
            mm(ps[:, 2, 0:NE], ones, chosen[:, 0, :])
            mm(ps[:, 2, 0:NE], ones, chosen[:, 1, :], False).then_inc(rank_ps, 1)

            def gather(N):
                pe.wait_ge(sel_sb, N + 1)
                for c in range(KC):
                    for t in range(TT):
                        last = mm(ps[:, 4 + c // 4, (c % 4) * P:(c % 4 + 1) * P], hn[:, t, c * P:(c + 1) * P],
                                  sel[:, t, :, :], c % 4 == 0 and t == 0, t == 1)
                last.then_inc(xg_ps, 1)

            def up(g, r, E, N, parity, between, zero=False):
                pe.wait_ge(b1_full[parity], (N + 1) * 16)
                for z in range(2):
                    for hf in range(2):
                        mm(ps[64 * hf:64 * hf + 64, z, :], ones[64 * parity:64 * parity + 1, 0:SLOTS],
                           b1rows[64 * parity:64 * parity + 1, hf * D + z:(hf + 1) * D:2], True, False)
                for c in range(KC):
                    s, times, n = w1_place(c, g, r, zero)
                    if parity == 0 and c % 4 == 0:
                        pe.wait_ge(xg_sb, N * 2 + c // 4 + 1)
                    pe.wait_ge(slot_full[s], times * 16 + 16 * uses[s])
                    for z in range(2):
                        for hf in range(2):
                            last = mm(ps[64 * hf:64 * hf + 64, z, :], xg[:, c, parity * SLOTS:(parity + 1) * SLOTS],
                                      slot(s)[:, hf * D + z:(hf + 1) * D:2], False, c == KC - 1)
                    last.then_inc(slots_used, 1)
                    if between:
                        between(c)
                pe.wait_ge(slots_used, n + (NMIX + 1))
                pe.sem_inc(up_ps, 1)

            def down(g, r, E, final=False):
                pe.wait_ge(actT_sb, E + 1)
                for i in range(4):
                    s, times, n = w2_place(i, g, r, final)
                    pe.wait_ge(slot_full[s], times * 16 + 16 * uses[s])
                    for cc in range(2):
                        k = 2 * i + cc
                        for dh in range(2):
                            last = mm(ps[64 * dh:64 * dh + 64, 3, :], actT[:, k % 4, k // 4, :],
                                      slot(s)[:, cc * D + dh * 512:cc * D + (dh + 1) * 512], k == 0, k == 7)
                    last.then_inc(slots_used, 1)
                pe.wait_ge(slots_used, n + (NMIX + 1))
                pe.sem_inc(down_ps, 1)

            def turn(E):
                pe.wait_ge(act_sb, E + 1)
                for m in range(4):
                    last = pe.transpose(ps[:, 2, m * P:(m + 1) * P], act_[:, m * P:(m + 1) * P], ident)
                last.then_inc(actT_ps, 1)

            def turn_gates(N, first):
                pe.wait_ge(selg_sb, N + 1)
                if first:
                    pe.wait_ge(b2_sb, 2)
                else:
                    pe.wait_ge(acc_sb, N * 2)
                for t in range(TT):
                    last = pe.transpose(ps[:, 6, t * P:(t + 1) * P], selg[:, t, :, :].rearrange("p e s -> p (e s)"), ident)
                last.then_inc(selgT_ps, 1)

            def scatter(N, t, bank=6):
                if t == 0:
                    pe.wait_ge(selgT_sb, N + 1)
                    pe.wait_ge(yrow_sb, N * 4 + 4)
                elif bank == 6:
                    pe.wait_ge(acc_sb, N * 2 + 1)
                for n in range(2):
                    last = mm(ps[:, bank + n, :], selgT[:, t, :], yrow[:, n * 512:(n + 1) * 512])
                last.then_inc(sc_ps, 1)

            def second_bias(t):
                if t == 0:
                    pe.wait_ge(gT_sb, 1)
                else:
                    pe.wait_ge(b2_sb, 1)
                for n in range(2):
                    last = mm(ps[:, 6 + n, :], gatesT[0:NE, t * P:(t + 1) * P], b2rows[0:NE, n * 512:(n + 1) * 512])
                last.then_inc(b2_ps, 1)

            def pair(q, a, p, first, last, turn_wait=None):
                g = q * (NE // GROUP) + a
                E, N, r = g * GROUP + 2 * p, g * 2 + p, 2 * p
                very_first, second = turn_wait == "first", turn_wait == "second"
                if not very_first:
                    pe.wait_ge(up_read, E)
                up(g, r, E, N, 0, None, first)
                if not first:
                    down(g, r - 1, E - 1)
                if very_first:
                    pe.wait_ge(gates_sb, 1)
                    for t in range(TT):
                        tr = pe.transpose(ps[0:NE, 3, t * P:(t + 1) * P], gates[:, t, :], ident)
                    tr.then_inc(gT_ps, 1)
                    second_bias(0)
                turn(E)

                def between(c):
                    if first:
                        if very_first and c == 2:
                            second_bias(1)
                    elif c == 0:
                        turn_gates(N - 1, second)
                    elif c == 2:
                        scatter(N - 1, 0)
                    elif c == 5:
                        scatter(N - 1, 1)

                pe.wait_ge(up_read, E + 1)
                up(g, r + 1, E + 1, N, 1, between)
                if not last:
                    gather(N + 1)
                down(g, r, E)
                turn(E + 1)

            def one_pass(q, very_first=False):
                N0 = q * NPAIR
                if not very_first:
                    pe.wait_ge(acc_sb, N0 * 2)
                gather(N0)
                pair(q, 0, 0, True, False, "first" if very_first else None)
                pair(q, 0, 1, False, False, "second" if very_first else None)
                with pe.Fori(1, NE // GROUP - 1) as a:
                    pair(q, a, 0, False, False)
                    pair(q, a, 1, False, False)
                a = NE // GROUP - 1
                pair(q, a, 0, False, False)
                pair(q, a, 1, False, True)
                turn_gates(N0 + NPAIR - 1, False)
                down(q * (NE // GROUP) + a, GROUP - 1, q * NE + NE - 1, True)
                scatter(N0 + NPAIR - 1, 0)
                scatter(N0 + NPAIR - 1, 1, 0)

            one_pass(0, True)
            pe.wait_ge(route_done, 1)
            most = pe.value_load(cnti[0:1, 0:1], min_val=0, max_val=T)
            with pe.If(most > SLOTS):
                with pe.Fori(1, PASSES) as q:
                    one_pass(q)

        @block.scalar
        def _(act):
            act.wait_ge(zeroed, 1)
            act.activation(ss[:, 7:8], epsc[:, 0:1], ACT.Sqrt)
            for t in range(TT):
                act.wait_ge(x_loaded[t], 16)
                act.activation(dump[:, t, :], xrows[:, t, :], ACT.Square, accum_out=ss[:, t:t + 1]).then_inc(act_step, 1)
            act.wait_ge(act_step, 2)
            act.wait_ge(zeroed, 2)
            act.activation(ss[:, 4:6], ss[:, 0:2], ACT.Sqrt, scale=1.0 / D, bias=epsc[:, 0:1]).then_inc(root, 1)
            act.wait_ge(mem_loaded, 16)
            for t in range(TT):
                act.activation(dump_m[:, t, :], memrows[:, t, :], ACT.Square, accum_out=ss[:, 2 + t:3 + t]).then_inc(act_step, 1)
            act.wait_ge(act_step, 4)
            act.activation(ss[:, 6:8], ss[:, 2:4], ACT.Sqrt, scale=1.0 / D, bias=epsc[:, 0:1]).then_inc(root_m, 1)
            for b in range(7):
                act.wait_ge(rwkv_ps, b + 1)
                act.activation(raw[:, 2 * b:2 * b + 2, 1:T + 1], ps[:, b, :].rearrange("p (c t) -> p c t", c=2), ACT.Copy).then_inc(raw_sb, 1)
            act.wait_ge(lora_in, 1)
            act.activation(proj[0:64, 12, :], proj[0:64, 12, :], ACT.Tanh).then_inc(lora_act, 1)
            act.activation(proj[:, 13, :], proj[:, 13, :], ACT.Sigmoid).then_inc(lora_act, 1)
            act.wait_ge(zw_ps, 1)
            for f in range(HP):
                last = act.activation(pex[:, f, :], ps[:, 5 + f // 2, (f % 2) * T:(f % 2 + 1) * T], ACT.Sigmoid, bias=col("w0", f))
            last.then_inc(rate_sb, 1)
            act.wait_ge(shifted, 1)
            act.wait_ge(za_ps, 1)
            for f in range(HP):
                last = act.activation(rate_a[:, f, :], ps[:, 7 - f // 2 * 2, (f % 2) * T:(f % 2 + 1) * T], ACT.Sigmoid, bias=col("a0", f))
            last.then_inc(a_sb, 1)
            act.wait_ge(g_ps, 1)
            for b in range(2):
                last = act.activation(gT[:, 2 * b:2 * b + 2, :], ps[:, 6 + b, :].rearrange("p (c t) -> p c t", c=2), ACT.Copy)
            last.then_inc(g_sb, 1)
            act.wait_ge(kk_clamped, 1)
            act.activation(pinc, pinc, ACT.Sqrt).then_inc(kk_root, 1)
            for n in range(2):
                act.wait_ge(memT_ps, n + 1)
                for i in range(4):
                    bank = 7 - i // 2 * 2 if n == 0 else 6 + i // 2
                    act.activation(memT[:, 4 * n + i, :], ps[:, bank, (i % 2) * T:(i % 2 + 1) * T], ACT.Copy,
                                   scale=col("memn", 4 * n + i)).then_inc(memT_sb, 1)
            act.wait_ge(csum_sb, 1)
            act.activation(pinc, csum, ACT.Exp, scale=-EXP_HALF).then_inc(powers_sb, 1)
            act.activation(pinv, csum, ACT.Exp, scale=EXP_HALF).then_inc(powers_sb, 1)
            act.activation(pex, pex, ACT.Exp, scale=-EXP_HALF).then_inc(powers_sb, 1)
            act.wait_ge(rest_ps, 1)
            for f in range(4):
                act.activation(sq_[:, f, :], ps[:, f // 2, (f % 2) * T:(f % 2 + 1) * T], ACT.Identity, scale=SWA_SCALE,
                               bias=bq[:, f:f + 1]).then_inc(rest_sb, 1)
            act.activation(skd[0:64, 0, :], ps[0:64, 2, 0:T], ACT.Identity, bias=col("bswa", 4)[0:64]).then_inc(rest_sb, 1)
            act.activation(skd[64:P, 1, :], ps[64:P, 2, 0:T], ACT.Identity, bias=col("bswa", 4)[64:P]).then_inc(rest_sb, 1)
            act.activation(svT, ps[:, 2, T:2 * T], ACT.Identity, bias=col("bswa", 5)).then_inc(rest_sb, 1)
            act.wait_ge(rest_sb, 7)
            act.activation(skd[64:P, 0, :], skd[0:64, 0, :], ACT.Copy).then_inc(rest_sb, 1)
            act.activation(skd[0:64, 1, :], skd[64:P, 1, :], ACT.Copy).then_inc(rest_sb, 1)
            act.activation(mq[:, 0:2, :], ps[:, 3, :].rearrange("p (c t) -> p c t", c=2), ACT.Copy).then_inc(rest_sb, 1)
            act.activation(mq[:, 2:4, :], ps[:, 4, :].rearrange("p (c t) -> p c t", c=2), ACT.Copy).then_inc(rest_sb, 1)
            act.wait_ge(svT_ps, 1)
            act.activation(sv, ps[:, 1, 0:T].rearrange("p (t f) -> p t f", t=TT), ACT.Copy).then_inc(sv_sb, 1)
            act.wait_ge(sink_loaded, 16)
            for n in range(TT):
                W = P * (n + 1)
                for odd in range(2):
                    act.wait_ge(negmax, 2 * n + odd + 1)
                    for o in range(4 * odd, 4 * odd + 4):
                        act.activation(probs[:, o * W:(o + 1) * W], probs[:, o * W:(o + 1) * W], ACT.Exp,
                                       bias=stat[:, 1, o:o + 1], accum_out=stat[:, 2, o:o + 1])
                    act.activation(stat[:, 4, 4 * odd:4 * odd + 4], stat[:, 3, 4 * odd:4 * odd + 4], ACT.Exp).then_inc(expd, 1)
                act.wait_ge(pT_ps, n + 1)
                if n == 1:
                    act.wait_ge(pv_ps, 1)
                for b in range(2 * (n + 1)):
                    act.activation(probsT[:, b * 512:(b + 1) * 512], ps[:, 1 + b, :], ACT.Copy).then_inc(pT_sb, 1)
                if n == 0:
                    act.wait_ge(pv_ps, 1)
                    act.activation(y_swa[:, :, 0:P], ps[:, 3, :].rearrange("p (c t) -> p c t", c=4), ACT.Copy).then_inc(pv_sb, 1)
            act.wait_ge(kv_ps, 1)
            for b in range(2):
                act.activation(kmT[:, 2 * b:2 * b + 2, :], ps[:, 5 + b, :].rearrange("p (c t) -> p c t", c=2), ACT.Copy).then_inc(kv_sb, 1)
            for t in range(TT):
                act.activation(vm[:, t, :], ps[:, (7 + t) % 8, :], ACT.Copy).then_inc(kv_sb, 1)
            act.wait_ge(pv_ps, 2)
            act.activation(y_swa[:, :, P:T], ps[:, 1, :].rearrange("p (c t) -> p c t", c=4), ACT.Copy).then_inc(pv_sb, 1)

            def to_tokens(i):
                dst, banks = ((btok, (7, 0)), (vtok, (1, 4)))[i]
                for t in range(TT):
                    act.wait_ge(tok_ps, 2 * i + t + 1)
                    act.activation(dst[:, t, :], ps[:, banks[t], :], ACT.Copy).then_inc(tok_sb, 1)

            pm = mprobs.rearrange("p (n h m) -> p n h m", n=2, h=4)
            for n in range(TT):
                act.wait_ge(negmax, n + 5)
                for h in range(4):
                    last = act.activation(pm[:, n, h, :], ps[:, 2 + 3 * n + h // 2, (h % 2) * T:(h % 2 + 1) * T], ACT.Exp,
                                          scale=MEM_SCALE, bias=stat[:, 1, 4 * n + h:4 * n + h + 1],
                                          accum_out=stat[:, 2, 4 * n + h:4 * n + h + 1])
                last.then_inc(expd, 1)
                if n == 0:
                    to_tokens(0)
            to_tokens(1)
            for n in range(TT):
                act.wait_ge(pT_ps, n + 3)
                for b in range(2):
                    act.activation(mprobsT[:, n * D + b * 512:n * D + (b + 1) * 512], ps[:, 2 + 3 * n + b, :], ACT.Copy).then_inc(pT_sb, 1)
            for n in range(TT):
                act.wait_ge(pv_ps, n + 3)
                act.activation(y_mem[:, :, n * P:(n + 1) * P], ps[:, 1 + 3 * n, :].rearrange("p (c t) -> p c t", c=4), ACT.Copy).then_inc(pv_sb, 1)

            for m in range(4 * (LEVELS - 1)):
                act.wait_ge(turned_ps, m + 1)
                us4 = slice(4 * (m % 4), 4 * (m % 4) + 4)
                act.activation((invT if m >= 4 else inv)[:, us4, :], ps[:, 6 + m % 2, :].rearrange("p (u t) -> p u t", u=4),
                               ACT.Copy).then_inc(invT_sb if m >= 4 else inv_sb, 1)

            def own_half(a):
                return a.rearrange("p (c q v) -> p c q v", q=4, v=64)[:, :, 0:4:3, :]

            for t in range(TT):
                act.wait_ge(av_ps, t + 1)
                for b in range(2):
                    act.activation(av[:, t, b * T:(b + 1) * T].rearrange("p (c a v) -> p c a v", a=2, v=64),
                                   own_half(ps[:, (6, 1)[t] + b, :]), ACT.Copy).then_inc(av_sb, 1)
            def gate(m):
                act.wait_ge(gate_ps, m + 1)
                if m >= 2:
                    act.wait_ge(merged_sb, m - 1)
                act.activation(gsig[:, m % 2, :], ps[:, 6, :], ACT.Sigmoid).then_inc(gate_sb, 1)

            points = fill_points()

            def gates_of(point):
                for p in points[point]:
                    if p % PIECES == 3:
                        gate(p // PIECES)

            for ch in range(NCH):
                rs = slice(64 * (ch % 2), 64 * (ch % 2) + 64)
                act.wait_ge(u_ps, ch + 1)
                for b in range(2):
                    last = act.activation(us[rs, ch // 2, b * T:(b + 1) * T].rearrange("p (c a v) -> p c a v", a=2, v=64),
                                          own_half(ps[rs, 1 + b, :]), ACT.Copy)
                last.then_inc(u_sb, 1)
                for s in "abc":
                    gates_of((ch, s))
            gates_of("mean")
            gates_of("var")
            act.wait_ge(var_ps, 1)
            for b in range(2):
                last = act.activation(sqr[:, 2 * b:2 * b + 2, :], ps[:, b, :].rearrange("p (c t) -> p c t", c=2), ACT.Sqrt,
                                      scale=1.0 / 64, bias=epsc[:, 1:2])
            last.then_inc(var_root, 1)
            gates_of("rest")
            for m in range(N_FILL, len(UNITS)):
                gate(m)
            act.dma_start(ffnw, ffn_norm_w.to_broadcast([P, D])).then_inc(late_loaded, 16)
            act.dma_start(finw, final_norm_w.unsqueeze(0).to_broadcast([P, D])).then_inc(late_loaded, 16)

            def input_norm(t):
                act.wait_ge(resid, t + 1)
                act.activation(sq_dump, xrows[:, t, :], ACT.Square, accum_out=ss[:, t:t + 1]).then_inc(ffn_ss, 1)
                act.wait_ge(ffn_ss, t + 1)
                act.activation(ss[:, 4 + t:5 + t], ss[:, t:t + 1], ACT.Sqrt, scale=1.0 / D, bias=epsc[:, 0:1]).then_inc(ffn_root, 1)

            for t in range(TT):
                input_norm(t)
                if t == 1:
                    for e in range(2):
                        act.dma_start(b1rows[64 * e:64 * e + 1, :], b_exp1[0, e:e + 1, :]).then_inc(b1_full[e], 16)
                for b in range(2):
                    act.wait_ge(hnT_ps, 2 * t + b + 1)
                    act.activation(hnT[:, 4 * b:4 * b + 4, t * P:(t + 1) * P], ps[:, 4 + 2 * t + b, :].rearrange("p (c t) -> p c t", c=4),
                                   ACT.Copy).then_inc(hnT_sb, 1)
            act.wait_ge(top_sb, 1)
            for t in range(TT):
                last = act.activation(gates[:, t, :], logit[:, t, :], ACT.Exp, bias=rtmp[:, t, 0:1])
            last.then_inc(top_exp, 1)

            def gathered(N):
                act.wait_ge(xg_ps, N + 1)
                for b in range(2):
                    act.activation(xg[:, 4 * b:4 * b + 4, :], ps[:, 4 + b, :].rearrange("p (c s) -> p c s", c=4), ACT.Copy).then_inc(xg_sb, 1)

            def sigmoid(E):
                act.wait_ge(glu_sb, E + 1)
                act.activation(sig, glu, ACT.Sigmoid, scale=ALPHA).then_inc(sig_sb, 1)

            def downed(E, parity):
                act.wait_ge(down_ps, E + 1)
                for dh in range(2):
                    act.activation(yrow[64 * parity:64 * parity + 64, dh * 512:(dh + 1) * 512], ps[64 * dh:64 * dh + 64, 3, :],
                                   ACT.Copy).then_inc(yrow_sb, 1)

            def turned(E):
                act.wait_ge(actT_ps, E + 1)
                act.activation(actT.rearrange("p m h s -> p (m h s)"), ps[:, 2, :], ACT.Copy).then_inc(actT_sb, 1)

            def gates_turned(N):
                act.wait_ge(selgT_ps, N + 1)
                act.activation(selgT.rearrange("p t n -> p (t n)"), ps[:, 6, 0:T], ACT.Copy).then_inc(selgT_sb, 1)

            def pair(q, k, first, last, very_first=False):
                E, N = q * NE + k * 2, q * NPAIR + k
                if very_first:
                    act.wait_ge(gT_ps, 1)
                    act.activation(gatesT[0:NE, :], ps[0:NE, 3, 0:T], ACT.Copy).then_inc(gT_sb, 1)
                sigmoid(E)
                if not first:
                    downed(E - 1, 1)
                turned(E)
                if not first:
                    gates_turned(N - 1)
                sigmoid(E + 1)
                if not last:
                    gathered(N + 1)
                downed(E, 0)
                turned(E + 1)

            def one_pass(q, very_first=False):
                gathered(q * NPAIR)
                pair(q, 0, True, False, very_first)
                with act.Fori(1, NPAIR - 1) as k:
                    pair(q, k, False, False)
                pair(q, NPAIR - 1, False, True)
                gates_turned(q * NPAIR + NPAIR - 1)
                if not very_first:
                    act.wait_ge(stored, q * (TT * 16))
                act.activation(ss[:, 7:8], epsc[:, 0:1], ACT.Sqrt)
                downed(q * NE + NE - 1, 1)
                for t in range(TT):
                    act.wait_ge(acc_sb, (q * NPAIR + NPAIR - 1) * 2 + t + 1)
                    act.activation(outrow[:, t, :], xrows[:, t, :], ACT.Square, accum_out=ss[:, t:t + 1]).then_inc(fin_ss, 1)
                    act.wait_ge(fin_ss, q * TT + t + 1)
                    act.activation(ss[:, 4 + t:5 + t], ss[:, t:t + 1], ACT.Sqrt, scale=1.0 / D, bias=epsc[:, 0:1]).then_inc(fin_root, 1)

            one_pass(0, True)
            act.wait_ge(route_done, 1)
            most = act.value_load(cnti[0:1, 0:1], min_val=0, max_val=T)
            with act.If(most > SLOTS):
                with act.Fori(1, PASSES) as q:
                    one_pass(q)

        @block.vector
        def _(dve):
            steps = [0]

            def step(ins):
                steps[0] += 1
                ins.then_inc(dve_step, 1)

            def settle():
                dve.wait_ge(dve_step, steps[0])

            def link(ins):
                step(ins)
                settle()

            TS, TTn, STT = dve.tensor_scalar, dve.tensor_tensor, dve.scalar_tensor_tensor

            dve.memset(epsc[:, 0:1], EPS).then_inc(zeroed, 1)
            dve.memset(epsc[:, 1:2], LNX_EPS).then_inc(zeroed, 1)
            dve.wait_ge(root, 1)
            link(dve.reciprocal(ss[:, 4:6], ss[:, 4:6]))
            for t in range(TT):
                TS(xscaled[:, t, :], xrows[:, t, :], ss[:, 4 + t:5 + t], None, ALU.mult).then_inc(scaled, 1)
            dve.wait_ge(prm_loaded, 16)
            step(TS(omka[:], prm[:, PCOLS["ka"]:PCOLS["ka"] + 4], -1.0, 1.0, ALU.mult, ALU.add))
            TS(bq[:], prm[:, PCOLS["bswa"]:PCOLS["bswa"] + 4], SWA_SCALE, None, ALU.mult).then_inc(prm_sb, 1)
            for c in range(KC):
                if c % 2 == 0:
                    dve.wait_ge(xT_ps, c // 2 + 1)
                TS(xT[:, c, :], ps[:, c // 2, (c % 2) * T:(c % 2 + 1) * T], col("attn", c), None, ALU.mult).then_inc(xT_sb, 1)
            dve.wait_ge(root_m, 1)
            link(dve.reciprocal(ss[:, 6:8], ss[:, 6:8]))
            for t in range(TT):
                TS(memrows[:, t, :], memrows[:, t, :], ss[:, 6 + t:7 + t], None, ALU.mult).then_inc(scaled_m, 1)
            link(dve.memset(raw[:, :, 0:1], 0.0))

            def shift(a, b, signal):
                link(TTn(proj[:, a:b, :], raw[:, a:b, 0:T], raw[:, a:b, 1:T + 1], ALU.subtract))
                for f in range(a, b):
                    last = STT(proj[:, f, :], proj[:, f, :], col("mu", f), raw[:, f, 1:T + 1], ALU.mult, ALU.add)
                last.then_inc(signal, 1)

            dve.wait_ge(raw_sb, 7)
            shift(12, 14, lora_in)
            shift(0, 12, shifted)
            dve.wait_ge(shifted, 1)
            for f in range(HP):
                step(TS(kkn[:, f, :], proj[:, 4 + f, :], col("kk", f), None, ALU.mult))
            settle()
            TTn(csum, kkn, kkn, ALU.mult).then_inc(kk_sq, 1)
            dve.wait_ge(kk_ps, 1)
            for b in range(2):
                last = TS(pinc[:, 2 * b:2 * b + 2, :], ps[:, 5 + b, :].rearrange("p (c t) -> p c t", c=2), 1e-24, None, ALU.max)
            last.then_inc(kk_clamped, 1)
            dve.wait_ge(rate_sb, 1)
            dve.wait_ge(cst_loaded, 16)
            for f in range(HP):
                step(dve.tensor_tensor_scan(csum[:, f, :], const("resets"), pex[:, f, :], 0.0, ALU.mult, ALU.add))
            settle()
            dve.wait_ge(kk_root, 1)
            link(dve.reciprocal(pinc, pinc))
            link(TTn(kkn, kkn, pinc, ALU.mult))
            TTn(pex, csum, pex, ALU.subtract).then_inc(csum_sb, 1)
            dve.wait_ge(a_sb, 1)
            link(TTn(ar[:, :, 0, :], kkn, rate_a, ALU.mult))
            for f in range(HP):
                step(TS(rate_a[:, f, :], rate_a[:, f, :], col("ka", f), omka[:, f:f + 1], ALU.mult, ALU.add))
            settle()
            link(TTn(proj[:, 4:8, :], proj[:, 4:8, :], rate_a, ALU.mult))
            dve.wait_ge(powers_sb, 2)
            step(TTn(bT, ar[:, :, 0, :], pinv, ALU.mult))
            step(TTn(kT, proj[:, 4:8, :], pinv, ALU.mult))
            step(TTn(ar[:, :, 1, :], proj[:, 0:4, :], pinc, ALU.mult))
            for c in range(NCH):
                step(dve.tensor_copy(pend[:, :, c], pinc[:, :, c * CH + CH - 1]))
            dve.wait_ge(powers_sb, 3)
            settle()
            STT(ar[:, :, 0, :], kkn, -1.0, pex, ALU.mult, ALU.mult).then_inc(tilde_sb, 1)
            dve.wait_ge(tilde_sb, 1)
            for f in range(HP):
                last = STT(kkn[:, f, :], proj[:, f, :], col("rk", f), proj[:, 4 + f, :], ALU.mult, ALU.mult)
            last.then_inc(rk_sb, 1)
            dve.wait_ge(sink_loaded, 16)
            for n in range(TT):
                W = P * (n + 1)
                dve.wait_ge(score_ps, n + 1)
                if n == 1:
                    dve.wait_ge(pT_ps, 1)
                if n == 0:
                    link(dve.tensor_copy(stat[:, 5, :].rearrange("p (a c) -> p a c", a=2),
                                         sinks[:].rearrange("p (c a) -> p a c", a=2)))
                    link(dve.tensor_copy(sinks[:], stat[:, 5, :]))
                for odd in range(2):
                    hs = slice(4 * odd, 4 * odd + 4)
                    pw = probs[:, 4 * odd * W:(4 * odd + 4) * W].rearrange("p (h m) -> p h m", h=4)
                    for h in range(odd, 8, 2):
                        o = odd * 4 + h // 2
                        if n == 0:
                            src = ps[:, 3 + odd, (h // 2) * P:(h // 2 + 1) * P]
                        else:
                            src = ps[:, 4 - h // 4 if odd else 1 + h // 4, (h // 2 % 2) * T:(h // 2 % 2 + 1) * T]
                        step(STT(probs[:, o * W:(o + 1) * W], const("dist", 2 * P - W, W), -SLOPES[h], src, ALU.mult, ALU.add))
                    settle()
                    link(dve.tensor_reduce(stat[:, 0, hs], pw, AX.X, ALU.max))
                    link(TTn(stat[:, 0, hs], stat[:, 0, hs], sinks[:, hs], ALU.max))
                    step(TTn(stat[:, 3, hs], sinks[:, hs], stat[:, 0, hs], ALU.subtract))
                    settle()
                    TS(stat[:, 1, hs], stat[:, 0, hs], -1.0, None, ALU.mult).then_inc(negmax, 1)
                for odd in range(2):
                    hs = slice(4 * odd, 4 * odd + 4)
                    pw = probs[:, 4 * odd * W:(4 * odd + 4) * W].rearrange("p (h m) -> p h m", h=4)
                    dve.wait_ge(expd, 2 * n + odd + 1)
                    link(TTn(stat[:, 5, hs], stat[:, 2, hs], stat[:, 4, hs], ALU.add))
                    link(dve.reciprocal(stat[:, 5, hs], stat[:, 5, hs]))
                    TTn(pw, pw, stat[:, 5, hs].unsqueeze(2).to_broadcast([P, 4, W]), ALU.mult).then_inc(normed, 1)

            for t in range(TT):
                dve.wait_ge(ktok_ps, t + 1)
                dve.tensor_copy(ktok[:, t, :], ps[:, 4 - t, :]).then_inc(ktok_sb, 1)
            for n in range(TT):
                dve.wait_ge(score_ps, n + 3)
                link(dve.tensor_reduce(stat[:, 0, 4 * n:4 * n + 4],
                                       ps[:, 2 + 3 * n:4 + 3 * n, :].rearrange("p b (h m) -> p (b h) m", h=2), AX.X, ALU.max))
                TS(stat[:, 1, 4 * n:4 * n + 4], stat[:, 0, 4 * n:4 * n + 4], -MEM_SCALE, None, ALU.mult).then_inc(negmax, 1)
            pm = mprobs.rearrange("p (n h m) -> p n h m", n=2, h=4)
            for n in range(TT):
                dve.wait_ge(expd, n + 5)
                link(dve.reciprocal(stat[:, 5, 4 * n:4 * n + 4], stat[:, 2, 4 * n:4 * n + 4]))
                TTn(pm[:, n], pm[:, n], stat[:, 5, 4 * n:4 * n + 4].unsqueeze(2).to_broadcast([P, 4, T]), ALU.mult).then_inc(normed, 1)
            dve.wait_ge(rk_ps, 1)
            for b in range(2):
                last = TTn(bonus[:, 2 * b:2 * b + 2, :], ps[:, (7 + b) % 8, :].rearrange("p (c t) -> p c t", c=2),
                           proj[:, 8 + 2 * b:10 + 2 * b, :], ALU.mult)
            last.then_inc(bonus_sb, 1)

            for g in range(4):
                for i in range(4):
                    n = 4 * g + i
                    dve.wait_ge(gram_ps, n + 1)
                    TTn(gram[:, n].rearrange("p (x y) t -> p x y t", x=2), ps[:, n % 6, :].rearrange("p (x y t) -> p x y t", x=2, y=2),
                        const("causal").rearrange("p (y t) -> p y t", y=2).unsqueeze(1).to_broadcast([P, 2, 2, P]),
                        ALU.mult).then_inc(gram_sb, 1)
                us4 = slice(4 * g, 4 * g + 4)
                dve.wait_ge(gram_sb, 4 * g + 4)
                link(TTn(invT[:, us4, :], gram[:, us4, 0, :], const("level0t").unsqueeze(1).to_broadcast([P, 4, P]), ALU.mult))
                TTn(invT[:, us4, :], invT[:, us4, :], ident.unsqueeze(1).to_broadcast([P, 4, P]), ALU.add).then_inc(level0_sb, 1)
            for j in range(1, LEVELS):
                for g in range(4):
                    dve.wait_ge(t1_ps, 4 * (j - 1) + g + 1)
                    TTn(t1s[:, g], ps[:, g, :].rearrange("p (u t) -> p u t", u=4),
                        const("level", j * P, P).unsqueeze(1).to_broadcast([P, 4, P]), ALU.mult).then_inc(t1_sb, 1)
                for g in range(4):
                    us4 = slice(4 * g, 4 * g + 4)
                    dve.wait_ge(xx_ps, 4 * (j - 1) + g + 1)
                    x_ = inv if j < LEVELS - 1 else invT
                    TTn(x_[:, us4, :], x_[:, us4, :], ps[:, 4 + g % 2, :].rearrange("p (u t) -> p u t", u=4),
                        ALU.add).then_inc(inv_sb, 1)
            step(dve.memset(state[:, 0], 0.0))
            dve.memset(rs_, 0.0).then_inc(zeroed, 1)
            points = fill_points()

            def merge(m):
                f = UNITS[m][1]
                dve.wait_ge(branch_ps, m + 1)
                dve.wait_ge(gate_sb, m + 1)
                if m < 4:
                    TTn(merged[:, f, :], gsig[:, m % 2, :], ps[:, 7, :], ALU.mult).then_inc(merged_sb, 1)
                else:
                    link(TTn(gsig[:, m % 2, :], gsig[:, m % 2, :], ps[:, 7, :], ALU.mult))
                    dve.wait_ge(merged_sb, m - 3)
                    TTn(merged[:, f, :], merged[:, f, :], gsig[:, m % 2, :], ALU.add).then_inc(merged_sb, 1)

            def merges_of(point):
                for p in points[point]:
                    if p % PIECES == 5:
                        merge(p // PIECES)

            for ch in range(NCH):
                t, c = ch // 2, ch % 2
                rs = slice(64 * c, 64 * c + 64)
                step(TTn(decay_end[:, ch % 2], heads.unsqueeze(1).to_broadcast([P, HP, P]),
                         pend[:, :, ch].unsqueeze(2).to_broadcast([P, HP, P]), ALU.mult))
                dve.wait_ge(r_ps, ch + 1)
                dve.wait_ge(av_sb, 4)
                if ch == 0:
                    dve.wait_ge(zeroed, 3)
                else:
                    dve.wait_ge(u_ps, ch)
                TTn(rs_[rs, :], ps[rs, 0, :], av[rs, t, :], ALU.add).then_inc(r_sb, 1)
                merges_of((ch, "a"))
                if ch < NCH - 1:
                    dve.wait_ge(s_ps, ch + 1)
                    settle()
                    link(TTn(state[:, (ch + 1) % 2], state[:, ch % 2], ps[:, 3, :].rearrange("p (c v) -> p c v", c=HP), ALU.add))
                    TTn(state[:, (ch + 1) % 2], state[:, (ch + 1) % 2], decay_end[:, ch % 2], ALU.mult).then_inc(s_sb, 1)
                    dve.wait_ge(s_sb, ch + 1)
                merges_of((ch, "b"))
                merges_of((ch, "c"))
                if c == 1:
                    dve.wait_ge(yh_ps, t + 1)
                    step(dve.tensor_copy(yT[:, :, t * P:(t + 1) * P], ps[:, 4 + t, :].rearrange("p (c v) -> p c v", c=HP)))
            settle()
            dve.sem_inc(yh_sb, 1)
            merges_of("mean")
            dve.wait_ge(mean_ps, 1)
            for b in range(2):
                step(STT(yc[:, 2 * b:2 * b + 2, :], ps[:, b, :].rearrange("p (c t) -> p c t", c=2), -1.0 / 64,
                         yT[:, 2 * b:2 * b + 2, :], ALU.mult, ALU.add))
            settle()
            dve.sem_inc(yc_sb, 1)
            TTn(sqr, yc, yc, ALU.mult).then_inc(yc_sb, 1)
            merges_of("var")
            after = [p // PIECES for p in points["rest"] if p % PIECES == 5]
            merge(after[0])
            dve.wait_ge(var_root, 1)
            link(dve.reciprocal(sqr, sqr))
            link(TTn(yc, yc, sqr, ALU.mult))
            for f in range(HP):
                step(TS(yc[:, f, :], yc[:, f, :], col("lnw", f), col("lnb", f), ALU.mult, ALU.add))
            settle()
            link(TTn(yc, yc, bonus, ALU.add))
            TTn(gT, gT, yc, ALU.mult).then_inc(y_rwkv_sb, 1)
            for m in after[1:] + list(range(N_FILL, len(UNITS))):
                merge(m)
            for t in range(TT):
                dve.wait_ge(out_ps, t + 1)
                TTn(xrows[:, t, :].rearrange("p (b n) -> p b n", b=2), xrows[:, t, :].rearrange("p (b n) -> p b n", b=2),
                    ps[:, 2 * t:2 * t + 2, :], ALU.add).then_inc(resid, 1)
                dve.wait_ge(ffn_root, t + 1)
                if t == 0:
                    dve.wait_ge(late_loaded, 16 * 5)
                link(dve.reciprocal(ss[:, 4 + t:5 + t], ss[:, 4 + t:5 + t]))
                for b in range(2):
                    half = slice(b * 512, (b + 1) * 512)
                    STT(hn[:, t, half], xrows[:, t, half], ss[:, 4 + t:5 + t], ffnw[:, half], ALU.mult, ALU.mult).then_inc(hn_sb, 1)
            dve.wait_ge(logit_ps, 1)
            link(TTn(logit[:], ps[:, 0, 0:TT * NE].rearrange("p (t e) -> p t e", t=TT), brt[:].unsqueeze(1).to_broadcast([P, TT, NE]), ALU.add))
            for t in range(TT):
                step(dve.max(top8[:, t, :], logit[:, t, :]))
            settle()
            TS(rtmp[:, :, 0], top8[:, :, 0], -1.0, None, ALU.mult).then_inc(top_sb, 1)
            dve.wait_ge(top_sb, 1)
            link(dve.memset(top8[:, :, 4:8], 3e38))
            for t in range(TT):
                step(dve.match_replace(rest[:, t, :], top8[:, t, :], logit[:, t, :], -3e38))
            settle()
            TTn(chosen[:], rest[:], logit[:], ALU.not_equal).then_inc(chosen_sb, 1)
            dve.wait_ge(chosen_sb, 1)
            dve.wait_ge(top_exp, 1)
            link(TTn(gates[:], gates[:], chosen[:], ALU.mult))
            link(dve.tensor_reduce(rtmp[:, :, 1], gates[:], AX.X, ALU.add))
            link(dve.reciprocal(rtmp[:, :, 2], rtmp[:, :, 1]))
            TTn(gates[:], gates[:], rtmp[:, :, 2].unsqueeze(2).to_broadcast([P, TT, NE]), ALU.mult).then_inc(gates_sb, 1)
            dve.wait_ge(rank_ps, 1)
            step(STT(rank1[:], ps[:, 1, 0:TT * NE].rearrange("p (t e) -> p t e", t=TT), 1.0, chosen[:], ALU.add, ALU.mult))
            settle()

            def columns(a, k):
                return a[:, :, bass.ds(k * 2, 2)].unsqueeze(3).to_broadcast([P, TT, 2, SLOTS])

            def places(q):
                a = CONST["iota"][0]
                return cst[:, bass.ds(q * SLOTS + a, SLOTS)].unsqueeze(1).unsqueeze(1).to_broadcast([P, TT, 2, SLOTS])

            def select(q, k, N, very_first=False):
                if not very_first:
                    dve.wait_ge(xg_ps, N)
                TTn(sel, places(q), columns(rank1, k), ALU.is_equal).then_inc(sel_sb, 1)

            def select_gates(q, k, N, very_first=False):
                if not very_first:
                    dve.wait_ge(selgT_ps, N)
                TTn(selg, places(q), columns(rank1, k), ALU.is_equal).then_inc(selg_raw, 1)
                dve.wait_ge(selg_raw, N + 1)
                TTn(selg, selg, columns(gates, k), ALU.mult).then_inc(selg_sb, 1)

            def swiglu(E, very_first=False):
                dve.wait_ge(up_ps, E + 1)
                if not very_first:
                    dve.wait_ge(act_sb, E)
                TS(glu, ps[:, 0, :], LIMIT, None, ALU.min).then_inc(glu_sb, 1)
                TS(lin, ps[:, 1, :], LIMIT, -LIMIT, ALU.min, ALU.max).then_inc(up_read, 1)
                dve.wait_ge(up_read, E + 1)
                dve.wait_ge(glu_sb, E + 1)
                STT(lin, lin, 1.0, glu, ALU.add, ALU.mult).then_inc(prod_sb, 1)
                dve.wait_ge(prod_sb, E + 1)
                dve.wait_ge(sig_sb, E + 1)
                if not very_first:
                    dve.wait_ge(actT_ps, E)
                TTn(act_, lin, sig, ALU.mult).then_inc(act_sb, 1)

            def add_up(N, t, very_first=False, bank=6):
                dve.wait_ge(sc_ps, N * 2 + t + 1)
                if not very_first:
                    dve.wait_ge(acc_sb, N * 2 + t)
                a = xrows[:, t, :].rearrange("p (b n) -> p b n", b=2)
                TTn(a, a, ps[:, bank:bank + 2, :], ALU.add).then_inc(acc_sb, 1)

            def second_bias(t):
                dve.wait_ge(b2_ps, t + 1)
                a = xrows[:, t, :].rearrange("p (b n) -> p b n", b=2)
                TTn(a, a, ps[:, 6:8, :], ALU.add).then_inc(b2_sb, 1)

            def largest_count():
                dve.wait_ge(rank_ps, 2)
                link(dve.tensor_reduce(cnt[:], ps[:, 2, 0:NE], AX.X, ALU.max))
                link(dve.tensor_copy(cnti[:], cnt[:]))
                dve.sem_inc(route_done, 1)

            def pair(q, k, first, last, very_first=False, second=False):
                E, N = q * NE + k * 2, q * NPAIR + k
                if very_first:
                    largest_count()
                if not last:
                    select(q, k + 1, N + 1)
                if not first:
                    select_gates(q, k - 1, N - 1, second)
                swiglu(E, very_first)
                if very_first:
                    second_bias(0)
                    second_bias(1)
                    dve.wait_ge(b2_sb, 2)
                if not first:
                    add_up(N - 1, 0, second)
                    add_up(N - 1, 1)
                swiglu(E + 1)

            def one_pass(q, very_first=False):
                select(q, 0, q * NPAIR, very_first)
                pair(q, 0, True, False, very_first)
                if very_first:
                    pair(q, 1, False, False, False, True)
                    with dve.Fori(2, NPAIR - 1) as k:
                        pair(q, k, False, False)
                else:
                    with dve.Fori(1, NPAIR - 1) as k:
                        pair(q, k, False, False)
                pair(q, NPAIR - 1, False, True)
                N = q * NPAIR + NPAIR - 1
                select_gates(q, NPAIR - 1, N)
                add_up(N, 0)
                add_up(N, 1, False, 0)
                for t in range(TT):
                    dve.wait_ge(fin_root, q * TT + t + 1)
                    dve.reciprocal(ss[:, 4 + t:5 + t], ss[:, 4 + t:5 + t]).then_inc(fin_scale, 1)
                    dve.wait_ge(fin_scale, q * TT + t + 1)
                    STT(outrow[:, t, :], xrows[:, t, :], ss[:, 4 + t:5 + t], finw, ALU.mult, ALU.mult).then_inc(final_sb, 1)

            one_pass(0, True)
            most = dve.value_load(cnti[0:1, 0:1], min_val=0, max_val=T)
            with dve.If(most > SLOTS):
                with dve.Fori(1, PASSES) as q:
                    one_pass(q)


_INS = ["x", "mem", "w_in", "rwkv_w2", "rwkv_a2", "rwkv_g2", "swa_sinks", "w_mem_kv", "w_gate", "w_branch", "w_out",
        "ffn_norm_w", "w_router", "b_router", "w_exp1", "b_exp1", "w_exp2", "b_exp2", "final_norm_w"]
_COLUMNS = ["attn_norm_w", "mem_norm_w", "rwkv_mu", "rwkv_w0", "rwkv_a0", "rwkv_kk", "rwkv_ka", "rwkv_rk", "rwkv_lnx_w",
            "rwkv_lnx_b", "b_swa"]


def kernel(**inputs):
    import concourse.bacc as bacc
    from concourse.bass_utils import run_bass_kernel_spmd

    nc = bacc.Bacc("TRN2", target_bir_lowering=False, num_devices=1)
    arrays = {f"in_{name}": np.ascontiguousarray(inputs[name]) for name in _INS}
    arrays["in_params"] = np.ascontiguousarray(np.concatenate([np.asarray(inputs[n]).reshape(-1, P) for n in _COLUMNS]).T)
    arrays["in_consts"] = constants()
    args = [nc.dram_tensor(name, a.shape, F32, kind="ExternalInput").ap() for name, a in arrays.items()]
    args.append(nc.dram_tensor("out_0", (1, T, D), F32, kind="ExternalOutput").ap())
    build(nc, *args)
    r = run_bass_kernel_spmd(nc, [arrays], core_ids=[0])
    return r.results[0]["out_0"]
```
